# Optimizing a Trainium2 kernel written in Bass

```python
import math
import jax, jax.numpy as jnp
from jax import lax
import numpy as np

D_MODEL = 1024
BATCH = 1
SEQ = 2048
DEPTH = 2

N_A_LAYERS = DEPTH // 2
N_B_LAYERS = DEPTH - N_A_LAYERS
ALPHA = (2.0 * DEPTH) ** 0.25
BETA = (8.0 * DEPTH) ** -0.25
LN_EPS = 1e-5
A_HEADS = 4
A_DQK = D_MODEL // 8
A_DV = D_MODEL // 4
A_CHUNK = 64
A_PROJ = 2 * A_HEADS * A_DQK + 2 * A_HEADS * A_DV + 2 * A_HEADS
A_NORM_EPS = 1e-6
B_WINDOWS = (128, 512, 2048)
B_DILATIONS = (1, 4, 16)
B_GROUPS = 3
B_HEADS = 8
B_HEAD_DIM = 64
B_WIDTH = B_HEADS * B_HEAD_DIM
ROPE_THETA = 10000.0
MOE_GROUPS = 4
MOE_EXPERTS_PER_GROUP = 8
MOE_EXPERTS = MOE_GROUPS * MOE_EXPERTS_PER_GROUP
MOE_TOPK = 2
MOE_HIDDEN = D_MODEL // 4
MOE_BLOCK = 128

kernel_name = "yoco_mlstm_dilated_hmoe_deepnorm_adaln"

def layer_norm(x, g, b):
    xf = x.astype(jnp.float32)
    mu = jnp.mean(xf, axis=-1, keepdims=True)
    var = jnp.mean(jnp.square(xf - mu), axis=-1, keepdims=True)
    return ((xf - mu) * lax.rsqrt(var + LN_EPS) * g.astype(jnp.float32) + b.astype(jnp.float32)).astype(x.dtype)

def rope(x, pos):
    dh = x.shape[-1]
    half = dh // 2
    inv = jnp.power(jnp.float32(ROPE_THETA), -jnp.arange(half, dtype=jnp.float32) * 2.0 / dh)
    ang = pos.astype(jnp.float32)[..., None] * inv
    ang = ang.reshape(ang.shape[:2] + (1,) * (x.ndim - 3) + (half,))
    cos, sin = jnp.cos(ang), jnp.sin(ang)
    xf = x.astype(jnp.float32)
    x1, x2 = xf[..., :half], xf[..., half:]
    return jnp.concatenate([x1 * cos - x2 * sin, x2 * cos + x1 * sin], axis=-1).astype(x.dtype)

def mlstm_chunkwise(q, k, v, i_pre, f_pre):
    bsz, nh, s, dqk = q.shape
    dv = v.shape[-1]
    nc = s // A_CHUNK

    def chunks(t):
        t = t.astype(jnp.float32).reshape((bsz, nh, nc, A_CHUNK) + t.shape[3:])
        return jnp.moveaxis(t, 2, 0)

    qc, kc, vc = chunks(q), chunks(k), chunks(v)
    ic = chunks(i_pre)
    lfc = chunks(jax.nn.log_sigmoid(f_pre.astype(jnp.float32)))
    causal = jnp.tril(jnp.ones((A_CHUNK, A_CHUNK), dtype=bool))

    def step(carry, inp):
        c_st, n_st, m_st = carry
        qq, kk, vv, ii, lf = inp
        b = jnp.cumsum(lf, axis=-1)
        dmat = jnp.where(causal, b[..., :, None] - b[..., None, :] + ii[..., None, :], -jnp.inf)
        inter = b + m_st[..., None]
        m_t = jnp.maximum(inter, jnp.max(dmat, axis=-1))
        dw = jnp.exp(dmat - m_t[..., None])
        iw = jnp.exp(inter - m_t)
        sc = jnp.einsum('bhtd,bhsd->bhts', qq, kk) * dw
        num = jnp.einsum('bhts,bhsv->bhtv', sc, vv) + iw[..., None] * jnp.einsum('bhtd,bhdv->bhtv', qq, c_st)
        den = jnp.sum(sc, axis=-1) + iw * jnp.einsum('bhtd,bhd->bht', qq, n_st)
        h = num / jnp.maximum(jnp.abs(den), jnp.exp(-m_t))[..., None]
        b_last = b[..., -1]
        ws_log = b_last[..., None] - b + ii
        m_new = jnp.maximum(b_last + m_st, jnp.max(ws_log, axis=-1))
        ws = jnp.exp(ws_log - m_new[..., None])
        decay = jnp.exp(b_last + m_st - m_new)
        c_new = decay[..., None, None] * c_st + jnp.einsum('bhs,bhsd,bhsv->bhdv', ws, kk, vv)
        n_new = decay[..., None] * n_st + jnp.einsum('bhs,bhsd->bhd', ws, kk)
        return (c_new, n_new, m_new), h

    init = (jnp.zeros((bsz, nh, dqk, dv), jnp.float32),
            jnp.zeros((bsz, nh, dqk), jnp.float32),
            jnp.zeros((bsz, nh), jnp.float32))
    _, h = lax.scan(step, init, (qc, kc, vc, ic, lfc))
    return jnp.moveaxis(h, 0, 2).reshape(bsz, nh, s, dv)

def mlstm_mixer(h, w_in, b_gate, norm_g, w_out):
    bsz, s, _ = h.shape
    proj = h @ w_in
    o1 = A_HEADS * A_DQK
    o2 = 2 * o1
    o3 = o2 + A_HEADS * A_DV
    o4 = o3 + A_HEADS * A_DV
    q = proj[..., :o1].reshape(bsz, s, A_HEADS, A_DQK)
    k = proj[..., o1:o2].reshape(bsz, s, A_HEADS, A_DQK) * (A_DQK ** -0.5)
    v = proj[..., o2:o3].reshape(bsz, s, A_HEADS, A_DV)
    o_gate = proj[..., o3:o4]
    gates = proj[..., o4:].astype(jnp.float32) + b_gate.astype(jnp.float32)
    i_pre = jnp.transpose(gates[..., :A_HEADS], (0, 2, 1))
    f_pre = jnp.transpose(gates[..., A_HEADS:], (0, 2, 1))
    ht = mlstm_chunkwise(jnp.transpose(q, (0, 2, 1, 3)), jnp.transpose(k, (0, 2, 1, 3)),
                         jnp.transpose(v, (0, 2, 1, 3)), i_pre, f_pre)
    mu = jnp.mean(ht, axis=-1, keepdims=True)
    var = jnp.mean(jnp.square(ht - mu), axis=-1, keepdims=True)
    hn = (ht - mu) * lax.rsqrt(var + A_NORM_EPS)
    hn = jnp.transpose(hn, (0, 2, 1, 3)).reshape(bsz, s, A_HEADS * A_DV) * norm_g.astype(jnp.float32)
    y = (hn * jax.nn.sigmoid(o_gate.astype(jnp.float32))).astype(h.dtype)
    return y @ w_out

def dilated_branch(q, k, v, window, dilation):
    bsz, s, nh, dh = q.shape
    wb = window // dilation
    span = wb * dilation
    p = -(-s // span) * span
    nb = p // span

    def to_blocks(t):
        t = jnp.pad(t, ((0, 0), (0, p - s), (0, 0), (0, 0)))
        t = t.reshape(bsz, p // dilation, dilation, nh, dh).transpose(0, 2, 1, 3, 4)
        return t.reshape(bsz, dilation, nb, wb, nh, dh)

    def with_prev(t):
        prev = jnp.concatenate([jnp.zeros_like(t[:, :, :1]), t[:, :, :-1]], axis=2)
        return jnp.concatenate([prev, t], axis=3)

    qb = to_blocks(q)
    kw = with_prev(to_blocks(k))
    vw = with_prev(to_blocks(v)).astype(jnp.float32)
    sc = jnp.einsum('brnqhe,brnkhe->brnhqk', qb, kw).astype(jnp.float32) * (dh ** -0.5)
    qi = jnp.arange(wb)[:, None]
    kj = jnp.arange(2 * wb)[None, :]
    band = (kj >= qi) & (kj <= qi + wb)
    valid = band[None] & ((jnp.arange(nb)[:, None, None] > 0) | (kj >= wb)[None])
    sc = jnp.where(valid[None, None, :, None], sc, -jnp.inf)
    m = jnp.max(sc, axis=-1, keepdims=True)
    pr = jnp.exp(sc - m)
    l = jnp.sum(pr, axis=-1)
    o = jnp.einsum('brnhqk,brnkhe->brnqhe', pr, vw) / jnp.swapaxes(l, -1, -2)[..., None]
    lse = jnp.swapaxes(m[..., 0] + jnp.log(l), -1, -2)

    def from_blocks(t):
        t = t.reshape((bsz, dilation, p // dilation) + t.shape[4:]).swapaxes(1, 2)
        return t.reshape((bsz, p) + t.shape[3:])[:, :s]

    return from_blocks(o), from_blocks(lse)

def dilated_mixer(h, positions, k_sh, v_sh, w_q, w_o):
    bsz, s, _ = h.shape
    q = rope((h @ w_q).reshape(bsz, s, B_GROUPS, B_HEADS, B_HEAD_DIM), positions)
    outs, lses = [], []
    for g in range(B_GROUPS):
        o_g, l_g = dilated_branch(q[:, :, g], k_sh[:, :, g], v_sh[:, :, g], B_WINDOWS[g], B_DILATIONS[g])
        outs.append(o_g)
        lses.append(l_g)
    wts = jax.nn.softmax(jnp.stack(lses, axis=0), axis=0)
    o = jnp.sum(wts[..., None] * jnp.stack(outs, axis=0), axis=0)
    return o.reshape(bsz, s, B_WIDTH).astype(h.dtype) @ w_o

def hier_moe(h, w_r1, b_r1, w_r2, b_r2, w_gate, w_up, w_down):
    bsz, s, d = h.shape
    t = h.reshape(-1, d)
    n_tok = t.shape[0]
    p1 = jax.nn.softmax((t @ w_r1).astype(jnp.float32) + b_r1.astype(jnp.float32), axis=-1)
    pg, g_idx = lax.top_k(p1, 1)
    lg2 = ((t @ w_r2).astype(jnp.float32) + b_r2.astype(jnp.float32)).reshape(n_tok, MOE_GROUPS, MOE_EXPERTS_PER_GROUP)
    sel = jnp.take_along_axis(lg2, g_idx[:, :, None], axis=1)[:, 0]
    v2, j2 = lax.top_k(sel, MOE_TOPK)
    weight = pg * jax.nn.softmax(v2, axis=-1)
    expert = g_idx * MOE_EXPERTS_PER_GROUP + j2

    n_as = n_tok * MOE_TOPK
    flat_e = expert.reshape(-1)
    flat_w = weight.reshape(-1)
    order = jnp.argsort(flat_e)
    se = flat_e[order]
    tok = order // MOE_TOPK
    counts = jnp.zeros((MOE_EXPERTS,), jnp.int32).at[flat_e].add(1)
    starts = jnp.cumsum(counts) - counts
    pcounts = (counts + MOE_BLOCK - 1) // MOE_BLOCK * MOE_BLOCK
    pends = jnp.cumsum(pcounts)
    pstarts = pends - pcounts
    dest = pstarts[se] + (jnp.arange(n_as, dtype=jnp.int32) - starts[se])
    n_blocks = -(-n_as // MOE_BLOCK) + MOE_EXPERTS
    xbuf = jnp.zeros((n_blocks * MOE_BLOCK, d), t.dtype).at[dest].set(t[tok])
    block_e = jnp.clip(jnp.searchsorted(pends, jnp.arange(n_blocks, dtype=jnp.int32) * MOE_BLOCK, side='right'),
                       0, MOE_EXPERTS - 1)

    def run(args):
        xb, e = args
        return (jax.nn.silu(xb @ w_gate[e]) * (xb @ w_up[e])) @ w_down[e]

    ybuf = lax.map(run, (xbuf.reshape(n_blocks, MOE_BLOCK, d), block_e)).reshape(n_blocks * MOE_BLOCK, d)
    y = ybuf[dest] * flat_w[order][:, None].astype(t.dtype)
    out = jnp.zeros((n_tok, d), t.dtype).at[tok].add(y)
    return out.reshape(bsz, s, d)

def setup_inputs(seed: int = 0) -> dict:
    key = jax.random.key(seed)
    ks = jax.random.split(key, 24)
    f32 = jnp.float32
    d = D_MODEL
    nrm = lambda k, shp: jax.random.normal(k, shp, f32)
    x = nrm(ks[0], (BATCH, SEQ, d))
    c = nrm(ks[1], (BATCH, d))
    offs = jax.random.randint(ks[2], (BATCH, 1), 0, 1024, dtype=jnp.int32)
    positions = (offs + jnp.arange(SEQ, dtype=jnp.int32)[None, :]).astype(jnp.int32)
    ada_w = nrm(ks[3], (DEPTH, d, 6 * d)) * (0.1 * d ** -0.5)
    ada_b = nrm(ks[4], (DEPTH, 6 * d)) * 0.01
    ln_g = 1.0 + 0.02 * nrm(ks[5], (DEPTH, 2, d))
    ln_b = 0.02 * nrm(ks[6], (DEPTH, 2, d))
    a_w_in = nrm(ks[7], (N_A_LAYERS, d, A_PROJ)) * d ** -0.5
    i_bias = 0.1 * nrm(ks[8], (N_A_LAYERS, A_HEADS))
    f_bias = jnp.linspace(3.0, 6.0, A_HEADS, dtype=f32)[None, :] + 0.1 * nrm(ks[9], (N_A_LAYERS, A_HEADS))
    a_b_gate = jnp.concatenate([i_bias, f_bias], axis=-1)
    a_norm_g = 1.0 + 0.02 * nrm(ks[10], (N_A_LAYERS, A_HEADS * A_DV))
    a_w_out = nrm(ks[11], (N_A_LAYERS, A_HEADS * A_DV, d)) * ((A_HEADS * A_DV) ** -0.5 * BETA)
    b_w_kv = nrm(ks[12], (d, 2 * B_GROUPS * B_WIDTH)) * d ** -0.5
    b_w_q = nrm(ks[13], (N_B_LAYERS, d, B_GROUPS * B_WIDTH)) * d ** -0.5
    b_w_o = nrm(ks[14], (N_B_LAYERS, B_WIDTH, d)) * (B_WIDTH ** -0.5 * BETA)
    moe_w_r1 = nrm(ks[15], (DEPTH, d, MOE_GROUPS)) * d ** -0.5
    moe_b_r1 = 0.01 * nrm(ks[16], (DEPTH, MOE_GROUPS))
    moe_w_r2 = nrm(ks[17], (DEPTH, d, MOE_EXPERTS)) * d ** -0.5
    moe_b_r2 = 0.01 * nrm(ks[18], (DEPTH, MOE_EXPERTS))
    moe_w_gate = nrm(ks[19], (DEPTH, MOE_EXPERTS, d, MOE_HIDDEN)) * d ** -0.5
    moe_w_up = nrm(ks[20], (DEPTH, MOE_EXPERTS, d, MOE_HIDDEN)) * d ** -0.5
    moe_w_down = nrm(ks[21], (DEPTH, MOE_EXPERTS, MOE_HIDDEN, d)) * (MOE_HIDDEN ** -0.5 * BETA)
    return {"x": x, "c": c, "positions": positions, "ada_w": ada_w, "ada_b": ada_b,
            "ln_g": ln_g, "ln_b": ln_b, "a_w_in": a_w_in, "a_b_gate": a_b_gate, "a_norm_g": a_norm_g,
            "a_w_out": a_w_out, "b_w_kv": b_w_kv, "b_w_q": b_w_q, "b_w_o": b_w_o,
            "moe_w_r1": moe_w_r1, "moe_b_r1": moe_b_r1, "moe_w_r2": moe_w_r2, "moe_b_r2": moe_b_r2,
            "moe_w_gate": moe_w_gate, "moe_w_up": moe_w_up, "moe_w_down": moe_w_down}

def reference(x, c, positions, ada_w, ada_b, ln_g, ln_b, a_w_in, a_b_gate, a_norm_g, a_w_out,
              b_w_kv, b_w_q, b_w_o, moe_w_r1, moe_b_r1, moe_w_r2, moe_b_r2, moe_w_gate, moe_w_up, moe_w_down):
    bsz, s, d = x.shape
    cond = jax.nn.silu(c)
    k_sh = None
    v_sh = None
    for l in range(DEPTH):
        mod = cond @ ada_w[l] + ada_b[l]
        sh1, sc1, g1, sh2, sc2, g2 = [m[:, None, :] for m in jnp.split(mod, 6, axis=-1)]
        h = x * (1.0 + sc1) + sh1
        if l < N_A_LAYERS:
            y = mlstm_mixer(h, a_w_in[l], a_b_gate[l], a_norm_g[l], a_w_out[l])
        else:
            y = dilated_mixer(h, positions, k_sh, v_sh, b_w_q[l - N_A_LAYERS], b_w_o[l - N_A_LAYERS])
        x = layer_norm(ALPHA * x + (1.0 + g1) * y, ln_g[l, 0], ln_b[l, 0])
        h = x * (1.0 + sc2) + sh2
        y = hier_moe(h, moe_w_r1[l], moe_b_r1[l], moe_w_r2[l], moe_b_r2[l],
                     moe_w_gate[l], moe_w_up[l], moe_w_down[l])
        x = layer_norm(ALPHA * x + (1.0 + g2) * y, ln_g[l, 1], ln_b[l, 1])
        if l == N_A_LAYERS - 1:
            kv = (x @ b_w_kv).reshape(bsz, s, 2, B_GROUPS, B_HEADS, B_HEAD_DIM)
            k_sh = rope(kv[:, :, 0], positions)
            v_sh = kv[:, :, 1]
    return x


_drawn_inputs = setup_inputs


def setup_inputs(seed=0):
    import zlib

    import numpy as np

    out = dict(_drawn_inputs(seed))
    spreads = {}
    factors = {'ada_b': 3.64, 'a_norm_g': 18.5, 'moe_b_r1': 8.0, 'moe_b_r2': 6.613}
    for name, (base, spread) in spreads.items():
        noise = np.random.default_rng([zlib.crc32(name.encode()), seed]).standard_normal(out[name].shape)
        drawn = base * np.exp(spread * noise) if base else spread * noise
        out[name] = __import__('jax').numpy.asarray(drawn.astype(out[name].dtype))
    for name, factor in factors.items():
        out[name] = (out[name] * factor).astype(out[name].dtype)
    return out
```

```python
from contextlib import ExitStack

import numpy as np

import concourse.bass as bass
from concourse import mybir

F32 = mybir.dt.float32
I32 = mybir.dt.int32
U32 = mybir.dt.uint32
ALU = mybir.AluOpType
ACT = mybir.ActivationFunctionType
AX_X = mybir.AxisListType.X
ds = bass.ds

P = 128
D = 1024
S = 2048
DEPTH = 2
NT = S // P
KD = D // P
ALPHA = (2.0 * DEPTH) ** 0.25
LN_EPS = 1e-5
AH, DQK, DV = 4, D // 8, D // 4
A_NORM_EPS = 1e-6
QK = AH * DQK
A_PROJ = 2 * QK + 2 * AH * DV + 2 * AH
WINDOWS, DILATIONS = (128, 512, 2048), (1, 4, 16)
G, BH, DH = 3, 8, 64
BW = BH * DH
QW = G * BW
HP = BH // 2
OW = 2 * (DH + 2)
MG, ME = 4, 8
NE = MG * ME
NR = MG + NE
HID = D // 4
NB = (2 * S + NE * (P - 1)) // P
NBP = 64
MACRO = 512
CH = 512
NEG = -1e30

C_ID, C_CAUSAL, C_BEFORE, C_ONES, C_BAND = 0, 128, 256, 384, 512
C_EXP, C_BLK, C_FREQ, C_SEL, C_TOK = 768, 800, 864, 896, 896 + AH * P
C_END = C_TOK + NT


def constant_table():
    t = np.zeros((P, C_END), np.float32)
    i = np.arange(P)
    t[:, C_ID:C_ID + P] = np.eye(P)
    t[:, C_CAUSAL:C_CAUSAL + P] = np.where(i[:, None] <= i[None, :], 0.0, NEG)
    t[:, C_BEFORE:C_BEFORE + P] = i[:, None] < i[None, :]
    t[:, C_ONES:C_ONES + P] = 1.0
    kj = np.arange(2 * P)
    t[:, C_BAND:C_BAND + 2 * P] = np.where((kj >= i[:, None]) & (kj <= i[:, None] + P), 0.0, NEG)
    t[:, C_EXP:C_EXP + NE] = np.arange(NE)
    t[:, C_BLK:C_BLK + NBP] = np.arange(NBP) * P
    t[:, C_FREQ:C_FREQ + DH // 2] = np.power(10000.0, -np.arange(DH // 2) * 2.0 / DH)
    for h in range(AH):
        t[h, C_SEL + h * P:C_SEL + (h + 1) * P] = 1.0
    t[:, C_TOK:C_TOK + NT] = i[:, None] + P * np.arange(NT)[None, :]
    return t


def settle(eng, waited):
    eng.sem_inc(waited, 1)


class Phase:

    def __init__(self, nc, name):
        self.nc, self.name, self.stack, self.sems = nc, name, ExitStack(), []

    def sb(self, name, shape, dtype=F32):
        return self.stack.enter_context(self.nc.sbuf_tensor(f"{self.name}_{name}", shape, dtype))

    def ps(self, name, shape, dtype=F32):
        return self.stack.enter_context(self.nc.psum_tensor(f"{self.name}_{name}", shape, dtype))

    def sem(self, name):
        s = self.stack.enter_context(self.nc.semaphore(f"{self.name}_{name}"))
        self.sems.append(s.num)
        return s

    def __enter__(self):
        self.stack.__enter__()
        return self

    def __exit__(self, *e):
        if e[0] is None:
            self.nc.all_engine_barrier(sems_to_clear=range(min(self.sems), max(self.sems) + 1))
        return self.stack.__exit__(*e)


def modulation(nc, d):
    NCH = 6 * D // CH
    with Phase(nc, "mod") as ph:
        c_sb = ph.sb("c", [P, KD])
        cond = ph.sb("cond", [P, KD])
        w = ph.sb("w", [P, 2, KD, CH])
        b = ph.sb("b", [1, 2, CH])
        row = ph.sb("row", [1, 2, CH])
        acc = [ph.ps(f"acc{j}", [P, CH]) for j in range(2)]
        c_in, cond_ready = ph.sem("c_in"), ph.sem("cond_ready")
        w_in = [ph.sem(f"w_in{j}") for j in range(2)]
        w_free, acc_ready, row_ready = ph.sem("w_free"), ph.sem("acc_ready"), ph.sem("row_ready")
        stored, waited = d["pool_dma"]("mod"), ph.sem("waited")
        w_dram = d["ada_w"].rearrange("l (p k) n -> l p k n", k=KD)
        with nc.Block() as block:
            @block.sync
            def _(sp):
                sp.dma_start(c_sb[:, :], d["c"].rearrange("b (p k) -> (b p) k", k=KD)).then_inc(c_in, 16)
                sp.sem_inc(w_free, 2)
                for l in range(DEPTH):
                    with sp.Fori(0, NCH // 2) as i:
                        for j in range(2):
                            n = l * NCH + i * 2 + j
                            sp.wait_ge(w_free, n + 1)
                            sp.dma_start(w[:, j, :, :], w_dram[l, :, :, ds((i * 2 + j) * CH, CH)]).then_inc(w_in[j], 16)
                            sp.dma_start(b[:, j, :], d["ada_b"][l:l + 1, ds((i * 2 + j) * CH, CH)]).then_inc(w_in[j], 16)

            @block.scalar
            def _(act):
                act.wait_ge(c_in, 16)
                nc.scalar.activation(cond[:, :], c_sb[:, :], ACT.Silu).then_inc(cond_ready, 1)

            @block.tensor
            def _(pe):
                pe.wait_ge(cond_ready, 1)
                for l in range(DEPTH):
                    with pe.Fori(0, NCH // 2) as i:
                        for j in range(2):
                            r = l * (NCH // 2) + i
                            pe.wait_ge(w_in[j], 32 * r + 32)
                            pe.wait_ge(row_ready, 2 * r + j + 1)
                            for k in range(KD):
                                mm = nc.tensor.matmul(acc[j][0:1, :], cond[:, k:k + 1], w[:, j, k, :],
                                                      start=(k == 0), stop=(k == KD - 1))
                            mm.then_inc(acc_ready, 1)

            @block.vector
            def _(dve):
                dve.sem_inc(row_ready, 2)
                for l in range(DEPTH):
                    with dve.Fori(0, NCH // 2) as i:
                        for j in range(2):
                            r = l * (NCH // 2) + i
                            dve.wait_ge(acc_ready, 2 * r + j + 1)
                            dve.wait_ge(stored[j], 16 * r)
                            nc.vector.tensor_tensor(row[:, j, :], acc[j][0:1, :], b[:, j, :], ALU.add).then_inc(row_ready, 1)

            @block.gpsimd
            def _(pool):
                for l in range(DEPTH):
                    with pool.Fori(0, NCH // 2) as i:
                        for j in range(2):
                            r = l * (NCH // 2) + i
                            pool.wait_ge(row_ready, 2 * r + j + 3)
                            settle(pool, waited)
                            pool.dma_start(d["mod"][l:l + 1, ds((i * 2 + j) * CH, CH)], row[:, j, :]).then_inc(stored[j], 16)
                            pool.sem_inc(w_free, 1)
                for j in range(2):
                    pool.wait_ge(stored[j], 16 * DEPTH * NCH // 2)


def load_mod_columns(eng, nc, d, cols, l, kinds, sem):
    for j, kind in enumerate(kinds):
        eng.dma_start(cols[:, j, :], d["mod"][l, kind * D:(kind + 1) * D].rearrange("(p k) -> p k", k=KD)).then_inc(sem, 16)


def project_mlstm(nc, d):
    NM, TPM = S // MACRO, MACRO // P
    NV = 2 * AH * DV // CH
    NQ = 2 * AH
    PER = NQ + TPM * NV
    SLOTS = 8
    with Phase(nc, "pa") as ph:
        w = ph.sb("w", [P, KD, A_PROJ])
        ident = ph.sb("ident", [P, P])
        cols = ph.sb("cols", [P, 2, KD])
        bias = ph.sb("bias", [AH, 2])
        x_sb = ph.sb("x", [P, 2, D])
        hT = ph.sb("hT", [P, KD, MACRO])
        out = ph.sb("out", [P, SLOTS, CH])
        gates = ph.sb("gates", [AH, 2, MACRO])
        tp = [[ph.ps(f"tp{j}{half}", [P, 4, P]) for half in range(2)] for j in range(2)]
        mm = [ph.ps(f"mm{j}", [P, CH]) for j in range(4)]
        w_in, c_in, cols_ready = ph.sem("w_in"), ph.sem("c_in"), ph.sem("cols_ready")
        x_in = d["pool_dma"]("pa")
        tp_ready, hT_act, hT_dve = ph.sem("tp_ready"), ph.sem("hT_act"), ph.sem("hT_dve")
        mm_ready, ev_act, ev_dve = ph.sem("mm_ready"), ph.sem("ev_act"), ph.sem("ev_dve")
        g_ready, gates_ready, g_out = ph.sem("g_ready"), ph.sem("gates_ready"), ph.sem("g_out")
        st, waited = [ph.sem(f"st{j}") for j in range(SLOTS)], ph.sem("waited")

        order = [("vo", t, n) for t in range(TPM) for n in range(NV)] + [("qk", n, 0) for n in range(NQ)]
        on_act = [kind == "vo" and b >= NV // 2 for kind, _, b in order]
        ACT_PER, DVE_PER = sum(on_act), PER - sum(on_act)
        nth = [sum(a == b for b in on_act[:j]) for j, a in enumerate(on_act)]

        def evacuated(eng, j, m):
            back = 1 if j < 0 else 0
            j %= PER
            per = ACT_PER if on_act[j] else DVE_PER
            eng.wait_ge(ev_act if on_act[j] else ev_dve, (m - back + 1) * per + nth[j] + 1)

        with nc.Block() as block:
            @block.sync
            def _(sp):
                load_mod_columns(sp, nc, d, cols, 0, (0, 1), c_in)
                sp.dma_start(ident[:, :], d["consts"][:, C_ID:C_ID + P]).then_inc(c_in, 16)
                for g in range(2):
                    sp.dma_start(bias[:, g:g + 1], d["a_b_gate"][0, g * AH:(g + 1) * AH].rearrange("(h o) -> h o", o=1)).then_inc(c_in, 16)
                sp.dma_start(w[:, :, :], d["a_w_in"][0].rearrange("(p k) n -> p k n", k=KD)).then_inc(w_in, 16)
                with sp.Fori(0, NM) as m:
                    for j in range(PER):
                        kind, a, b = order[j]
                        evacuated(sp, j, m)
                        settle(sp, waited)
                        src = out[:, j % SLOTS, :]
                        if kind == "qk":
                            sp.dma_start(d["qkT"][a, :, ds(m * MACRO, MACRO)], src).then_inc(st[j % SLOTS], 16)
                        else:
                            sp.dma_start(d["vo"][ds(m * MACRO + a * P, P), b * CH:(b + 1) * CH], src).then_inc(st[j % SLOTS], 16)
                    sp.wait_ge(gates_ready, 2 * m + 2)
                    settle(sp, waited)
                    for g in range(2):
                        sp.dma_start(d["gates"][g, :, ds(m * MACRO, MACRO)], gates[:, g, :]).then_inc(g_out, 16)
                for j in range(SLOTS):
                    sp.wait_ge(st[j], 16 * NM * PER // SLOTS)
                sp.wait_ge(g_out, 32 * NM)

            @block.tensor
            def _(pe):
                def transposes(m, t):
                    j = t % 2
                    pe.wait_ge(x_in[j], 16 * (m * (TPM // 2) + t // 2 + 1))
                    pe.wait_ge(hT_act, m * TPM + t + 1)
                    pe.wait_ge(hT_dve, m * TPM + t + 1)
                    if t == 0:
                        pe.wait_ge(gates_ready, 2 * m)
                    for k in range(KD):
                        ins = nc.tensor.transpose(tp[j][k // 4][:, k % 4, :], x_sb[:, j, k:D:KD], ident[:, :])
                    ins.then_inc(tp_ready, 1)

                def bank(m, j):
                    kind, a, b = order[j]
                    evacuated(pe, j - 4, m)
                    for k in range(KD):
                        if kind == "vo":
                            lhsT, rhs = hT[:, k, a * P:(a + 1) * P], w[:, k, 2 * QK + b * CH:2 * QK + (b + 1) * CH]
                        else:
                            lhsT, rhs = w[:, k, a * P:(a + 1) * P], hT[:, k, :]
                        ins = nc.tensor.matmul(mm[j % 4][:, :], lhsT, rhs, start=(k == 0), stop=(k == KD - 1))
                    ins.then_inc(mm_ready, 1)

                pe.wait_ge(c_in, 16 * 5)
                with pe.Fori(0, NM) as m:
                    transposes(m, 0)
                    for t in range(TPM):
                        if t + 1 < TPM:
                            transposes(m, t + 1)
                        pe.wait_ge(hT_act, m * TPM + t + 3)
                        pe.wait_ge(hT_dve, m * TPM + t + 3)
                        if t == 0:
                            pe.wait_ge(w_in, 16)
                        for n in range(NV):
                            bank(m, t * NV + n)
                    for n in range(NQ):
                        bank(m, TPM * NV + n)
                    for g in range(2):
                        for k in range(KD):
                            ins = nc.tensor.matmul(tp[0][g][0:AH, :, :].rearrange("p a b -> p (a b)"),
                                                   w[:, k, A_PROJ - 2 * AH + g * AH:A_PROJ - AH + g * AH], hT[:, k, :],
                                                   start=(k == 0), stop=(k == KD - 1))
                        ins.then_inc(g_ready, 1)

            @block.scalar
            def _(act):
                act.sem_inc(hT_act, 2)
                act.sem_inc(ev_act, ACT_PER)
                act.wait_ge(cols_ready, 1)
                with act.Fori(0, NM) as m:
                    def hT_half(t):
                        act.wait_ge(tp_ready, m * TPM + t + 1)
                        for k in range(4):
                            ins = nc.scalar.activation(hT[:, k, t * P:(t + 1) * P], tp[t % 2][0][:, k, :], ACT.Identity,
                                                       bias=cols[:, 0, k:k + 1], scale=cols[:, 1, k:k + 1])
                        ins.then_inc(hT_act, 1)

                    hT_half(0)
                    for t in range(TPM):
                        if t + 1 < TPM:
                            hT_half(t + 1)
                        for j in range(t * NV, (t + 1) * NV):
                            if on_act[j]:
                                act.wait_ge(mm_ready, m * PER + j + 1)
                                act.wait_ge(st[j % SLOTS], 16 * (m * (PER // SLOTS) + j // SLOTS))
                                nc.scalar.activation(out[:, j % SLOTS, :], mm[j % 4][:, :], ACT.Sigmoid).then_inc(ev_act, 1)

            @block.vector
            def _(dve):
                dve.sem_inc(hT_dve, 2)
                dve.sem_inc(ev_dve, DVE_PER)
                dve.wait_ge(c_in, 16 * 5)
                nc.vector.tensor_scalar(cols[:, 1, :], cols[:, 1, :], 1.0, None, ALU.add).then_inc(cols_ready, 1)
                dve.wait_ge(cols_ready, 1)
                with dve.Fori(0, NM) as m:
                    def hT_half(t):
                        dve.wait_ge(tp_ready, m * TPM + t + 1)
                        for k in range(4, KD):
                            ins = nc.vector.tensor_scalar(hT[:, k, t * P:(t + 1) * P], tp[t % 2][1][:, k - 4, :],
                                                          cols[:, 1, k:k + 1], cols[:, 0, k:k + 1], ALU.mult, ALU.add)
                        ins.then_inc(hT_dve, 1)

                    def evacuate(j):
                        kind, a, b = order[j]
                        if on_act[j]:
                            return
                        dve.wait_ge(mm_ready, m * PER + j + 1)
                        dve.wait_ge(st[j % SLOTS], 16 * (m * (PER // SLOTS) + j // SLOTS))
                        scale = DQK ** -0.5 if kind == "qk" and a >= AH else 1.0
                        nc.vector.tensor_scalar(out[:, j % SLOTS, :], mm[j % 4][:, :], scale, None, ALU.mult).then_inc(ev_dve, 1)

                    hT_half(0)
                    for t in range(TPM):
                        if t + 1 < TPM:
                            hT_half(t + 1)
                        for j in range(t * NV, (t + 1) * NV):
                            evacuate(j)
                    for j in range(TPM * NV, PER):
                        evacuate(j)
                    dve.wait_ge(g_out, 32 * m)
                    for g in range(2):
                        dve.wait_ge(g_ready, 2 * m + g + 1)
                        nc.vector.tensor_scalar(gates[:, g, :], tp[0][g][0:AH, :, :].rearrange("p a b -> p (a b)"), bias[:, g:g + 1], None,
                                                ALU.add).then_inc(gates_ready, 1)

            @block.gpsimd
            def _(pool):
                for j in range(2):
                    pool.dma_start(x_sb[:, j, :], d["x"][0, j * P:(j + 1) * P, :]).then_inc(x_in[j], 16)
                with pool.Fori(1, NT // 2) as i:
                    for j in range(2):
                        pool.wait_ge(tp_ready, 2 * i - 1 + j)
                        settle(pool, waited)
                        pool.dma_start(x_sb[:, j, :], d["x"][0, ds(i * 2 * P + j * P, P), :]).then_inc(x_in[j], 16)


QU, QEM, QWS = range(3)
NQT = 3


def gate_rows(nc, d):
    with Phase(nc, "gr") as ph:
        raw = ph.sb("raw", [AH, 2, S])
        t0 = ph.sb("t0", [AH, S])
        t1 = ph.sb("t1", [AH, S])
        lf = ph.sb("lf", [AH, S])
        keep = ph.sb("keep", [AH, S])
        b = ph.sb("b", [AH, S])
        m = ph.sb("m", [AH, S])
        rowbm = ph.sb("rowbm", [AH, S])
        u = ph.sb("u", [AH, S])
        small = ph.sb("small", [AH, 4, NT])
        quant = ph.sb("quant", [P, S])
        ident = ph.sb("ident", [P, P])
        sel = ph.sb("sel", [AH, AH, P])
        colq = ph.sb("colq", [P, NT, NQT, AH])
        decay = ph.sb("decay", [P, 2, AH, NT])
        tp = [ph.ps(f"tp{j}", [P, 4, P]) for j in range(4)]
        dc = ph.ps("dc", [P, 2, AH, NT])
        g_in, c_in, out_done = ph.sem("g_in"), ph.sem("c_in"), ph.sem("out_done")
        dve_done, act_done, pe_done, rows_ready = ph.sem("dve_done"), ph.sem("act_done"), ph.sem("pe_done"), ph.sem("rows_ready")
        cols_done = ph.sem("cols_done")

        def chunks(a):
            return a.rearrange("h (c t) -> h c t", t=P)

        with nc.Block() as block:
            @block.sync
            def _(sp):
                sp.dma_start(raw[:, :, :], d["gates"].rearrange("g h t -> h g t")).then_inc(g_in, 16)
                sp.dma_start(ident[:, :], d["consts"][:, C_ID:C_ID + P]).then_inc(c_in, 16)
                sp.dma_start(sel[:, :, :], d["consts"][0:AH, C_SEL:C_SEL + AH * P].rearrange("k (h p) -> k h p", h=AH)).then_inc(c_in, 16)
                sp.wait_ge(rows_ready, 1)
                sp.dma_start(d["rowbm"], rowbm[:, :]).then_inc(out_done, 16)
                sp.wait_ge(cols_done, 1)
                sp.dma_start(d["colq"], colq[:, :, :, :].rearrange("p c q h -> p (c q h)")).then_inc(out_done, 16)
                sp.dma_start(d["decay"], decay[:, :, :, :].rearrange("p a h c -> p (a h c)")).then_inc(out_done, 16)
                sp.wait_ge(out_done, 48)

            @block.scalar
            def _(act):
                act.wait_ge(g_in, 16)
                nc.scalar.activation(t0[:, :], raw[:, 1, :], ACT.Abs)
                act.drain()
                nc.scalar.activation(t0[:, :], t0[:, :], ACT.Exp, scale=-1.0)
                act.drain()
                nc.scalar.activation(t1[:, :], t0[:, :], ACT.Ln, bias=1.0).then_inc(act_done, 1)
                act.wait_ge(dve_done, 1)
                nc.scalar.activation(quant[0:AH, :], u[:, :], ACT.Copy)
                nc.scalar.activation(quant[32:32 + AH, :], m[:, :], ACT.Exp, scale=-1.0)
                act.wait_ge(dve_done, 2)
                nc.scalar.activation(quant[64:64 + AH, :], t1[:, :], ACT.Exp)
                nc.scalar.activation(small[:, 3, :], small[:, 1, :], ACT.Exp)
                act.drain().then_inc(rows_ready, 1)

            @block.vector
            def _(dve):
                nc.vector.memset(quant[:, :], 0.0)
                nc.vector.memset(keep[:, :], 1.0)
                dve.drain()
                nc.vector.memset(chunks(keep[:, :])[:, :, 0:1], 0.0)
                dve.wait_ge(g_in, 16)
                nc.vector.tensor_scalar(lf[:, :], raw[:, 1, :], 0.0, None, ALU.min)
                dve.drain()
                dve.wait_ge(act_done, 1)
                nc.vector.tensor_tensor(lf[:, :], lf[:, :], t1[:, :], ALU.subtract)
                dve.drain()
                nc.vector.tensor_tensor_scan(b[:, :], keep[:, :], lf[:, :], 0.0, ALU.mult, ALU.add)
                nc.vector.tensor_tensor_scan(m[:, :], lf[:, :], raw[:, 0, :], 0.0, ALU.add, ALU.max)
                nc.vector.memset(small[:, 0, 0:1], 0.0)
                dve.drain()
                nc.vector.tensor_tensor(u[:, :], raw[:, 0, :], b[:, :], ALU.subtract)
                nc.vector.tensor_tensor(rowbm[:, :], b[:, :], m[:, :], ALU.subtract)
                nc.vector.tensor_copy(small[:, 0, 1:NT], chunks(m[:, :])[:, 0:NT - 1, P - 1])
                dve.drain().then_inc(dve_done, 1)
                bm_last = chunks(rowbm[:, :])[:, :, P - 1:P]
                nc.vector.tensor_tensor(chunks(t0[:, :]), chunks(rowbm[:, :]), small[:, 0, :].rearrange("h (c o) -> h c o", o=1).to_broadcast([AH, NT, P]), ALU.add)
                nc.vector.tensor_tensor(chunks(t1[:, :]), chunks(u[:, :]), bm_last.to_broadcast([AH, NT, P]), ALU.add)
                dve.drain()
                nc.vector.tensor_copy(small[:, 1, :], chunks(t0[:, :])[:, :, P - 1])
                dve.drain().then_inc(dve_done, 1)
                for c in range(NT):
                    dve.wait_ge(pe_done, c + 1)
                    q = tp[c % 4][:, 0, :].rearrange("p (q h) -> p q h", q=4)[:, 0:NQT, 0:AH]
                    nc.vector.tensor_copy(colq[:, c, :, :], q).then_inc(dve_done, 1)
                dve.wait_ge(pe_done, NT + 1)
                nc.vector.tensor_copy(decay[:, :, :, :], dc[:, :, :, :])
                dve.drain().then_inc(cols_done, 1)

            @block.tensor
            def _(pe):
                pe.wait_ge(c_in, 32)
                pe.wait_ge(rows_ready, 1)
                for c in range(NT):
                    if c >= 4:
                        pe.wait_ge(dve_done, 2 + c - 3)
                    nc.tensor.transpose(tp[c % 4][:, 0, :], quant[:, c * P:(c + 1) * P], ident[:, :]).then_inc(pe_done, 1)
                for h in range(AH):
                    nc.tensor.matmul(dc[:, 0, h, :], sel[:, h, :], small[:, 0, :], start=True, stop=True)
                    ins = nc.tensor.matmul(dc[:, 1, h, :], sel[:, h, :], small[:, 3, :], start=True, stop=True)
                ins.then_inc(pe_done, 1)


def mlstm(nc, d):
    with Phase(nc, "ml") as ph:
        q = ph.sb("q", [P, 2, AH, P])
        kT = ph.sb("kT", [P, 2, AH, P])
        v = ph.sb("v", [P, 2, AH, DV])
        og = ph.sb("og", [P, 2, D])
        y = ph.sb("y", [P, 2, D])
        rowbm = ph.sb("rowbm", [AH, S])
        colq = ph.sb("colq", [P, NT, NQT, AH])
        decay = ph.sb("decay", [P, 2, AH, NT])
        cq = ph.sb("cq", [P, 2, NQT, AH])
        dk = ph.sb("dk", [P, 2, 2, AH])
        sel = ph.sb("sel", [AH, AH, P])
        ident = ph.sb("ident", [P, P])
        causal = ph.sb("causal", [P, P])
        ng = ph.sb("ng", [P, D])
        ones = ph.sb("ones", [P, 1])
        dw = ph.sb("dw", [P, AH, P])
        iwb = ph.sb("iwb", [P, AH, P])
        sc = ph.sb("sc", [P, 2, AH, P])
        qs = ph.sb("qs", [P, 2, AH, P])
        kw = ph.sb("kw", [P, 2, AH, P])
        C = ph.sb("C", [P, AH, DV])
        n = ph.sb("n", [P, AH])
        den = ph.sb("den", [P, AH])
        rden = ph.sb("rden", [P, AH])
        ht = ph.sb("ht", [P, AH, DV])
        stats = ph.sb("stats", [P, AH, 6])
        mv = ph.sb("mv", [P, AH, 2])
        rstd = ph.sb("rstd", [P, AH])
        lnv = ph.sb("lnv", [P, AH])
        bS, bR, bK, bD = ph.ps("bS", [P, AH, P]), ph.ps("bR", [P, AH, P]), ph.ps("bK", [P, AH, P]), ph.ps("bD", [P, CH])
        bN = [ph.ps(f"bN{i}", [P, 2, DV]) for i in range(2)]
        bU = [ph.ps(f"bU{i}", [P, 2, DV]) for i in range(2)]
        c_in, k_ready = ph.sem("c_in"), ph.sem("k_ready")
        qkv_in = [ph.sem(f"qkv_in{j}") for j in range(2)]
        og_in = [ph.sem(f"og_in{j}") for j in range(2)]
        stored = [ph.sem(f"stored{j}") for j in range(2)]
        scores_ready, dwin_ready, dw_ready, iw_ready, kw_ready = (ph.sem(x) for x in ("scores_ready", "dwin_ready", "dw_ready", "iw_ready", "kw_ready"))
        sc_ready, num_ready, upd_ready, state_ready = (ph.sem(x) for x in ("sc_ready", "num_ready", "upd_ready", "state_ready"))
        rden_ready, ht_ready, hn_ready, ng_done, y_ready, waited = (ph.sem(x) for x in ("rden_ready", "ht_ready", "hn_ready", "ng_done", "y_ready", "waited"))
        cq_ready, mv_ready, rstd_ready = ph.sem("cq_ready"), ph.sem("mv_ready"), ph.sem("rstd_ready")

        def steps(eng, first, step):
            first(0, 0)
            with eng.Fori(0, NT // 2 - 1) as i:
                for j in range(2):
                    step(i * 2 + j, j, True)
            step(NT - 2, 0, True)
            step(NT - 1, 1, False)

        with nc.Block() as block:
            @block.sync
            def _(sp):
                def load(c, j):
                    tok = ds(c * P, P)
                    sp.dma_start(q[:, j, :, :], d["qkT"][0:AH, :, tok].rearrange("h p t -> p h t")).then_inc(qkv_in[j], 16)
                    sp.dma_start(kT[:, j, :, :], d["qkT"][AH:2 * AH, :, tok].rearrange("h p t -> p h t")).then_inc(qkv_in[j], 16)
                    sp.dma_start(v[:, j, :, :].rearrange("p h e -> p (h e)"), d["vo"][tok, 0:D]).then_inc(qkv_in[j], 16)
                    sp.dma_start(og[:, j, :], d["vo"][tok, D:2 * D]).then_inc(og_in[j], 16)

                sp.dma_start(rowbm[:, :], d["rowbm"]).then_inc(c_in, 16)
                sp.dma_start(colq[:, :, :, :].rearrange("p c q h -> p (c q h)"), d["colq"]).then_inc(c_in, 16)
                sp.dma_start(decay[:, :, :, :].rearrange("p a h c -> p (a h c)"), d["decay"]).then_inc(c_in, 16)
                sp.dma_start(sel[:, :, :], d["consts"][0:AH, C_SEL:C_SEL + AH * P].rearrange("k (h p) -> k h p", h=AH)).then_inc(c_in, 16)
                sp.dma_start(ident[:, :], d["consts"][:, C_ID:C_ID + P]).then_inc(c_in, 16)
                sp.dma_start(causal[:, :], d["consts"][:, C_CAUSAL:C_CAUSAL + P]).then_inc(c_in, 16)
                sp.dma_start(ng[:, :], d["a_norm_g"][0:1, :].to_broadcast([P, D])).then_inc(c_in, 16)
                load(0, 0)
                load(1, 1)

                def step(c, j, more):
                    if more:
                        sp.wait_ge(upd_ready, c + 1)
                        settle(sp, waited)
                        tok = ds((c + 2) * P, P)
                        sp.dma_start(q[:, j, :, :], d["qkT"][0:AH, :, tok].rearrange("h p t -> p h t")).then_inc(qkv_in[j], 16)
                        sp.dma_start(kT[:, j, :, :], d["qkT"][AH:2 * AH, :, tok].rearrange("h p t -> p h t")).then_inc(qkv_in[j], 16)
                        sp.dma_start(v[:, j, :, :].rearrange("p h e -> p (h e)"), d["vo"][tok, 0:D]).then_inc(qkv_in[j], 16)
                    sp.wait_ge(y_ready, c + 1)
                    settle(sp, waited)
                    sp.dma_start(d["y"][ds(c * P, P), :], y[:, j, :]).then_inc(stored[j], 16)
                    if more:
                        sp.dma_start(og[:, j, :], d["vo"][ds((c + 2) * P, P), D:2 * D]).then_inc(og_in[j], 16)

                with sp.Fori(0, NT // 2 - 1) as i:
                    for j in range(2):
                        step(i * 2 + j, j, True)
                for c in range(NT - 2, NT):
                    step(c, c % 2, False)
                for j in range(2):
                    sp.wait_ge(stored[j], 16 * NT // 2)

            @block.tensor
            def _(pe):
                pe.wait_ge(c_in, 16 * 7)
                pe.wait_ge(k_ready, 1)

                def scores(c, j):
                    pe.wait_ge(sc_ready, c)
                    pe.wait_ge(iw_ready, c)
                    pe.wait_ge(kw_ready, c)
                    pe.wait_ge(qkv_in[j], 24 * (c - j) + 48)
                    for h in range(AH):
                        nc.tensor.matmul(bS[:, h, :], kT[:, j, h, :], q[:, j, h, :], start=True, stop=True)
                    for h in range(AH):
                        nc.tensor.transpose(bK[:, h, :], kT[:, j, h, :], ident[:, :])
                    for h in range(AH):
                        ins = nc.tensor.matmul(bR[:, h, :], sel[:, h, :], rowbm[:, ds(c * P, P)], start=True, stop=True)
                    ins.then_inc(scores_ready, 1)

                def step(c, j, more):
                    if more:
                        scores(c + 1, 1 - j)
                    pe.wait_ge(sc_ready, c + 1)
                    pe.wait_ge(kw_ready, c + 1)
                    pe.wait_ge(state_ready, c + 1)
                    pe.wait_ge(ht_ready, c)
                    for h in range(AH):
                        nc.tensor.matmul(bN[h // 2][:, h % 2, :], sc[:, j, h, :], v[:, j, h, :], start=True, stop=False)
                        nc.tensor.matmul(bN[h // 2][:, h % 2, :], qs[:, j, h, :], C[:, h, :], start=False, stop=True)
                        nc.tensor.matmul(bD[:, h:h + 1], sc[:, j, h, :], ones[:, :], start=True, stop=False)
                        ins = nc.tensor.matmul(bD[:, h:h + 1], qs[:, j, h, :], n[:, h:h + 1], start=False, stop=True)
                    for h in range(AH):
                        ins = nc.tensor.matmul(bD[:, AH + h:AH + h + 1], kw[:, j, h, :], ones[:, :], start=True, stop=True)
                    ins.then_inc(num_ready, 1)
                    for h in range(AH):
                        ins = nc.tensor.matmul(bU[h // 2][:, h % 2, :], kw[:, j, h, :], v[:, j, h, :], start=True, stop=True)
                    ins.then_inc(upd_ready, 1)

                steps(pe, scores, step)

            @block.scalar
            def _(act):
                act.wait_ge(c_in, 16 * 7)

                def prep(c, j):
                    act.wait_ge(cq_ready, c + 1)
                    act.wait_ge(scores_ready, c + 1)
                    for h in range(AH):
                        ins = nc.scalar.activation(iwb[:, h, :], bR[:, h, :], ACT.Exp, bias=dk[:, j, 0, h:h + 1])
                    ins.then_inc(iw_ready, 1)
                    for h in range(AH):
                        ins = nc.scalar.activation(kw[:, j, h, :], bK[:, h, :], ACT.Copy, scale=cq[:, j, QWS, h:h + 1])
                    ins.then_inc(kw_ready, 1)
                    act.wait_ge(dwin_ready, c + 1)
                    nc.scalar.activation(dw[:, :, :], dw[:, :, :], ACT.Exp).then_inc(dw_ready, 1)

                def step(c, j, more):
                    if more:
                        act.wait_ge(upd_ready, c)
                        act.wait_ge(sc_ready, c + 1)
                        prep(c + 1, 1 - j)
                    act.wait_ge(rden_ready, c + 1)
                    act.wait_ge(ng_done, c)
                    for h in range(AH):
                        ins = nc.scalar.activation(ht[:, h, :], bN[h // 2][:, h % 2, :], ACT.Copy, scale=rden[:, h:h + 1])
                    ins.then_inc(ht_ready, 1)
                    act.wait_ge(mv_ready, c + 1)
                    nc.scalar.activation(lnv[:, :], rstd[:, :], ACT.Ln)
                    act.drain()
                    nc.scalar.activation(rstd[:, :], lnv[:, :], ACT.Exp, scale=-0.5).then_inc(rstd_ready, 1)

                steps(act, prep, step)

            @block.vector
            def _(dve):
                nc.vector.memset(C[:, :, :], 0.0)
                nc.vector.memset(n[:, :], 0.0)
                nc.vector.memset(ones[:, :], 1.0)
                dve.drain().then_inc(k_ready, 1)
                dve.sem_inc(state_ready, 1)
                dve.wait_ge(c_in, 16 * 7)

                def prep(c, j):
                    nc.vector.tensor_copy(cq[:, j, :, :], colq[:, ds(c, 1), :, :])
                    nc.vector.tensor_copy(dk[:, j, :, :], decay[:, :, :, ds(c, 1)])
                    dve.drain().then_inc(cq_ready, 1)
                    dve.wait_ge(iw_ready, c + 1)
                    for h in range(AH):
                        ins = nc.vector.scalar_tensor_tensor(dw[:, h, :], bR[:, h, :], cq[:, j, QU, h:h + 1], causal[:, :], ALU.add, ALU.add)
                    ins.then_inc(dwin_ready, 1)
                    nc.vector.tensor_tensor(qs[:, j, :, :], q[:, j, :, :], iwb[:, :, :], ALU.mult)
                    dve.wait_ge(dw_ready, c + 1)
                    nc.vector.tensor_tensor(sc[:, j, :, :], bS[:, :, :], dw[:, :, :], ALU.mult).then_inc(sc_ready, 1)

                def step(c, j, more):
                    if more:
                        dve.wait_ge(upd_ready, c)
                        prep(c + 1, 1 - j)
                    dve.wait_ge(num_ready, c + 1)
                    nc.vector.scalar_tensor_tensor(den[:, :], bD[:, 0:AH], -1.0, cq[:, j, QEM, :], ALU.mult, ALU.max)
                    nc.vector.tensor_tensor(n[:, :], n[:, :], dk[:, j, 1, :], ALU.mult)
                    dve.drain()
                    nc.vector.tensor_tensor(den[:, :], bD[:, 0:AH], den[:, :], ALU.max)
                    dve.drain()
                    nc.vector.reciprocal(rden[:, :], den[:, :]).then_inc(rden_ready, 1)
                    nc.vector.tensor_tensor(n[:, :], n[:, :], bD[:, AH:2 * AH], ALU.add)
                    dve.wait_ge(upd_ready, c + 1)
                    for h in range(AH):
                        ins = nc.vector.scalar_tensor_tensor(C[:, h, :], C[:, h, :], dk[:, j, 1, h:h + 1], bU[h // 2][:, h % 2, :], ALU.mult, ALU.add)
                    ins.then_inc(state_ready, 1)
                    dve.wait_ge(ht_ready, c + 1)
                    for h in range(AH):
                        nc.vector.bn_stats(stats[:, h, :], ht[:, h, :])
                    dve.drain()
                    for h in range(AH):
                        nc.vector.bn_aggr(mv[:, h, :], stats[:, h, :])
                    dve.drain()
                    nc.vector.tensor_scalar(rstd[:, :], mv[:, :, 1], A_NORM_EPS, None, ALU.add).then_inc(mv_ready, 1)
                    dve.wait_ge(rstd_ready, c + 1)
                    for h in range(AH):
                        ins = nc.vector.tensor_scalar(ht[:, h, :], ht[:, h, :], mv[:, h, 0:1], rstd[:, h:h + 1], ALU.subtract, ALU.mult)
                    ins.then_inc(hn_ready, 1)
                    dve.wait_ge(og_in[j], 8 * (c - j) + 16)
                    dve.wait_ge(ng_done, c + 1)
                    nc.vector.tensor_tensor(y[:, j, :], y[:, j, :], og[:, j, :], ALU.mult).then_inc(y_ready, 1)

                steps(dve, prep, step)

            @block.gpsimd
            def _(pool):
                pool.wait_ge(c_in, 16 * 7)
                with pool.Fori(0, NT // 2) as i:
                    for j in range(2):
                        pool.wait_ge(hn_ready, i * 2 + j + 1)
                        pool.wait_ge(stored[j], 16 * i)
                        nc.gpsimd.tensor_tensor(y[:, j, :], ht[:, :, :].rearrange("p h e -> p (h e)"), ng[:, :], ALU.mult).then_inc(ng_done, 1)


def load_norm(eng, nc, d, norm, gain, l, which, sem):
    eng.dma_start(norm[:, 0, :], d["ln_g"][l, which:which + 1, :].to_broadcast([P, D])).then_inc(sem, 16)
    eng.dma_start(norm[:, 1, :], d["ln_b"][l, which:which + 1, :].to_broadcast([P, D])).then_inc(sem, 16)
    kind = 3 * which + 2
    eng.dma_start(gain[:, :], d["mod"][l:l + 1, kind * D:(kind + 1) * D].to_broadcast([P, D])).then_inc(sem, 16)


def after_mixer(nc, d, l):
    K = KD if l == 0 else BW // P
    W = K * P
    name = f"am{l}"
    with Phase(nc, name) as ph:
        w = ph.sb("w", [P, K, D])
        wr = ph.sb("wr", [P, KD, NR])
        br = ph.sb("br", [P, NR])
        ident = ph.sb("ident", [P, P])
        cols = ph.sb("cols", [P, 2, KD])
        norm = ph.sb("norm", [P, 2, D])
        gain = ph.sb("gain", [P, D])
        y = ph.sb("y", [P, 2, W])
        x = ph.sb("x", [P, 2, D])
        yT = ph.sb("yT", [P, 2, K, P])
        z = ph.sb("z", [P, 2, D])
        x1 = ph.sb("x1", [P, 2, D])
        hT = ph.sb("hT", [P, KD, P])
        stats = ph.sb("stats", [P, 2, 6])
        mv = ph.sb("mv", [P, 2])
        std = ph.sb("std", [P, 2])
        lg = ph.sb("lg", [P, 2, NR])
        if l:
            o = ph.sb("o", [P, 2, G, HP * OW])
            coef = ph.sb("coef", [P, G, BH])
            mx = ph.sb("mx", [P, BH])
            dn = ph.sb("dn", [P, BH])
            og = ph.sb("og", [P, G, BW])
        tp = [ph.ps(f"tp{i}", [P, 4, P]) for i in range(2)]
        acc = [[ph.ps(f"acc{j}{i}", [P, CH]) for i in range(2)] for j in range(2)]
        bl = ph.ps("bl", [P, NR])
        names = ("c_in", "cols_ready", "ytp_ready", "yT_ready", "acc_ready", "z_ready", "v_ready", "std_ready", "xn_ready", "xg_ready",
                 "x1_ready", "htp_ready", "hT_ready", "lg_acc", "lg_ready", "waited", "y_ready", "e_in", "e_ready")
        (c_in, cols_ready, ytp_ready, yT_ready, acc_ready, z_ready, v_ready, std_ready, xn_ready, xg_ready,
         x1_ready, htp_ready, hT_ready, lg_acc, lg_ready, waited, y_ready, e_in, e_ready) = (ph.sem(s) for s in names)
        y_in = [ph.sem(f"y_in{j}") for j in range(2)]
        x_in = [ph.sem(f"x_in{j}") for j in range(2)]
        stored = [ph.sem(f"stored{j}") for j in range(2)]
        x_dram = d["x"][0] if l == 0 else d["x2"]
        w_dram = (d["a_w_out"] if l == 0 else d["b_w_o"])[0].rearrange("(p k) n -> p k n", k=K)

        def steps(eng, step):
            step(0, 0, True, False)
            with eng.Fori(0, NT // 2 - 1) as i:
                for j in range(2):
                    step(i * 2 + j + 1, (j + 1) % 2, False, False)
            step(NT - 1, 1, False, True)

        with nc.Block() as block:
            @block.sync
            def _(sp):
                sp.dma_start(ident[:, :], d["consts"][:, C_ID:C_ID + P]).then_inc(c_in, 16)
                load_mod_columns(sp, nc, d, cols, l, (3, 4), c_in)
                load_norm(sp, nc, d, norm, gain, l, 0, c_in)
                sp.dma_start(wr[:, :, 0:MG], d["moe_w_r1"][l].rearrange("(p k) n -> p k n", k=KD)).then_inc(c_in, 16)
                sp.dma_start(wr[:, :, MG:NR], d["moe_w_r2"][l].rearrange("(p k) n -> p k n", k=KD)).then_inc(c_in, 16)
                sp.dma_start(br[:, 0:MG], d["moe_b_r1"][l:l + 1, :].to_broadcast([P, MG])).then_inc(c_in, 16)
                sp.dma_start(br[:, MG:NR], d["moe_b_r2"][l:l + 1, :].to_broadcast([P, NE])).then_inc(c_in, 16)
                sp.dma_start(w[:, :, :], w_dram).then_inc(c_in, 16)

                def load(c, j):
                    if l == 0:
                        sp.dma_start(y[:, j, :], d["y"][ds(c * P, P), :]).then_inc(y_in[j], 16)
                    else:
                        sp.dma_start(o[:, j, :, :], d["o"][:, ds(c * P, P), :].rearrange("g p n -> p g n")).then_inc(y_in[j], 16)
                    sp.dma_start(x[:, j, :], x_dram[ds(c * P, P), :]).then_inc(x_in[j], 16)

                def store(c, j):
                    sp.wait_ge(x1_ready, c + 1)
                    sp.wait_ge(lg_ready, c + 1)
                    settle(sp, waited)
                    sp.dma_start(d["x1"][ds(c * P, P), :], x1[:, j, :]).then_inc(stored[j], 16)
                    sp.dma_start(d["lg"][ds(c * P, P), :], lg[:, j, :]).then_inc(stored[j], 16)

                load(0, 0)
                load(1, 1)
                with sp.Fori(0, NT // 2 - 1) as i:
                    for j in range(2):
                        sp.wait_ge(ytp_ready, i * 2 + j + 1)
                        sp.wait_ge(z_ready, i * 2 + j + 1)
                        settle(sp, waited)
                        load(i * 2 + j + 2, j)
                        store(i * 2 + j, j)
                for j in range(2):
                    store(NT - 2 + j, j)
                for j in range(2):
                    sp.wait_ge(stored[j], 32 * NT // 2)

            @block.tensor
            def _(pe):
                pe.wait_ge(c_in, 16 * 11)

                def y_transposes(c, j):
                    if l:
                        pe.wait_ge(y_ready, c + 1)
                    else:
                        pe.wait_ge(y_in[j], 8 * (c - j) + 16)
                    if not (isinstance(c, int) and c < 2):
                        pe.wait_ge(hT_ready, c - 1)
                    for k in range(K):
                        ins = nc.tensor.transpose(tp[k // 4][:, k % 4, :], y[:, j, k:W:K], ident[:, :])
                    ins.then_inc(ytp_ready, 1)

                def logits(c):
                    pe.wait_ge(hT_ready, c + 1)
                    pe.wait_ge(lg_ready, c)
                    for k in range(KD):
                        ins = nc.tensor.matmul(bl[:, :], hT[:, k, :], wr[:, k, :], start=(k == 0), stop=(k == KD - 1))
                    ins.then_inc(lg_acc, 1)

                def step(c, j, first, last):
                    if not last:
                        y_transposes(c + 1, 1 - j)
                        out_product(c + 1, 1 - j)
                    if not first:
                        logits(c - 1)
                    pe.wait_ge(x1_ready, c + 1)
                    if not last:
                        pe.wait_ge(yT_ready, c + 2)
                    for k in range(KD):
                        ins = nc.tensor.transpose(tp[k // 4][:, k % 4, :], x1[:, j, k:D:KD], ident[:, :])
                    ins.then_inc(htp_ready, 1)

                def out_product(c, j):
                    pe.wait_ge(yT_ready, c + 1)
                    if not (isinstance(c, int) and c < 2):
                        pe.wait_ge(z_ready, c - 1)
                    for half in range(2):
                        for k in range(K):
                            ins = nc.tensor.matmul(acc[j][half][:, :], yT[:, j, k, :], w[:, k, half * CH:(half + 1) * CH],
                                                   start=(k == 0), stop=(k == K - 1))
                    ins.then_inc(acc_ready, 1)

                y_transposes(0, 0)
                out_product(0, 0)
                steps(pe, step)
                logits(NT - 1)

            @block.scalar
            def _(act):
                act.wait_ge(cols_ready, 1)

                def yT_copy(c, j):
                    act.wait_ge(ytp_ready, c + 1)
                    for i in range(K // 4):
                        ins = nc.scalar.activation(yT[:, j, i * 4:(i + 1) * 4, :], tp[i][:, :, :], ACT.Copy)
                    ins.then_inc(yT_ready, 1)

                def step(c, j, first, last):
                    if not last:
                        if not first:
                            act.wait_ge(acc_ready, c)
                        yT_copy(c + 1, 1 - j)
                    act.wait_ge(v_ready, c + 1)
                    nc.scalar.activation(std[:, 1:2], std[:, 0:1], ACT.Sqrt).then_inc(std_ready, 1)
                    act.wait_ge(htp_ready, c + 1)
                    act.wait_ge(lg_acc, c)
                    for k in range(KD):
                        ins = nc.scalar.activation(hT[:, k, :], tp[k // 4][:, k % 4, :], ACT.Identity,
                                                   bias=cols[:, 0, k:k + 1], scale=cols[:, 1, k:k + 1])
                    ins.then_inc(hT_ready, 1)

                def combine(c, j):
                    act.wait_ge(e_in, c + 1)
                    nc.scalar.activation(coef[:, :, :], coef[:, :, :], ACT.Exp).then_inc(e_ready, 1)

                if l:
                    combine(0, 0)
                yT_copy(0, 0)

                def both(c, j, first, last):
                    if l and not last:
                        combine(c + 1, 1 - j)
                    step(c, j, first, last)

                steps(act, both)

            @block.vector
            def _(dve):
                dve.wait_ge(c_in, 16 * 11)
                nc.vector.tensor_scalar(cols[:, 1, :], cols[:, 1, :], 1.0, None, ALU.add).then_inc(cols_ready, 1)
                nc.vector.tensor_scalar(gain[:, :], gain[:, :], 1.0, None, ALU.add)
                dve.drain()

                def combine(c, j):
                    dve.wait_ge(y_in[j], 8 * (c - j) + 16)
                    v = o[:, j, :, :].rearrange("p g (h e) -> p g h e", e=DH + 2)
                    m, den = v[:, :, :, DH], v[:, :, :, DH + 1]
                    nc.vector.tensor_tensor(mx[:, :], m[:, 0, :], m[:, 1, :], ALU.min)
                    dve.drain()
                    nc.vector.tensor_tensor(mx[:, :], mx[:, :], m[:, 2, :], ALU.min)
                    dve.drain()
                    for g in range(G):
                        ins = nc.vector.tensor_tensor(coef[:, g, :], mx[:, :], m[:, g, :], ALU.subtract)
                    ins.then_inc(e_in, 1)
                    dve.wait_ge(e_ready, c + 1)
                    for g in range(G):
                        nc.vector.tensor_tensor(og[:, g, 0:BH], coef[:, g, :], den[:, g, :], ALU.mult)
                    dve.drain()
                    nc.vector.tensor_tensor(dn[:, :], og[:, 0, 0:BH], og[:, 1, 0:BH], ALU.add)
                    dve.drain()
                    nc.vector.tensor_tensor(dn[:, :], dn[:, :], og[:, 2, 0:BH], ALU.add)
                    dve.drain()
                    nc.vector.reciprocal(dn[:, :], dn[:, :])
                    dve.drain()
                    for g in range(G):
                        nc.vector.tensor_tensor(coef[:, g, :], coef[:, g, :], dn[:, :], ALU.mult)
                    dve.drain()
                    for g in range(G):
                        nc.vector.tensor_tensor(og[:, g, :].rearrange("p (h e) -> p h e", e=DH), v[:, g, :, 0:DH],
                                                coef[:, g, :].rearrange("p (h o) -> p h o", o=1).to_broadcast([P, BH, DH]), ALU.mult)
                    dve.drain()
                    nc.vector.tensor_tensor(og[:, 0, :], og[:, 0, :], og[:, 1, :], ALU.add)
                    dve.drain()
                    nc.vector.tensor_tensor(y[:, j, :], og[:, 0, :], og[:, 2, :], ALU.add).then_inc(y_ready, 1)

                def logits(c, j):
                    dve.wait_ge(lg_acc, c + 1)
                    nc.vector.tensor_tensor(lg[:, j, :], bl[:, :], br[:, :], ALU.add).then_inc(lg_ready, 1)

                def step(c, j, first, last):
                    if l and not last:
                        dve.wait_ge(ytp_ready, c)
                        combine(c + 1, 1 - j)
                    dve.wait_ge(acc_ready, c + 1)
                    for half in range(2):
                        cut = slice(half * CH, (half + 1) * CH)
                        nc.vector.tensor_tensor(z[:, j, cut], acc[j][half][:, :], gain[:, cut], ALU.mult)
                    dve.drain()
                    dve.wait_ge(x_in[j], 8 * (c - j) + 16)
                    nc.vector.scalar_tensor_tensor(z[:, j, :], x[:, j, :], ALPHA, z[:, j, :], ALU.mult, ALU.add).then_inc(z_ready, 1)
                    dve.wait_ge(z_ready, c + 1)
                    for half in range(2):
                        nc.vector.bn_stats(stats[:, half, :], z[:, j, half * CH:(half + 1) * CH])
                    dve.drain()
                    nc.vector.bn_aggr(mv[:, :], stats[:, :, :].rearrange("p a b -> p (a b)"))
                    dve.drain()
                    nc.vector.tensor_scalar(std[:, 0:1], mv[:, 1:2], LN_EPS, None, ALU.add).then_inc(v_ready, 1)
                    dve.wait_ge(std_ready, c + 1)
                    nc.vector.reciprocal(std[:, 0:1], std[:, 1:2])
                    dve.drain()
                    nc.vector.tensor_scalar(z[:, j, :], z[:, j, :], mv[:, 0:1], std[:, 0:1], ALU.subtract, ALU.mult).then_inc(xn_ready, 1)
                    dve.wait_ge(xg_ready, c + 1)
                    nc.vector.tensor_tensor(x1[:, j, :], x1[:, j, :], norm[:, 1, :], ALU.add).then_inc(x1_ready, 1)
                    if not first:
                        logits(c - 1, 1 - j)

                if l:
                    combine(0, 0)
                steps(dve, step)
                logits(NT - 1, 1)

            @block.gpsimd
            def _(pool):
                pool.wait_ge(c_in, 16 * 11)
                with pool.Fori(0, NT // 2) as i:
                    for j in range(2):
                        pool.wait_ge(xn_ready, i * 2 + j + 1)
                        pool.wait_ge(stored[j], 32 * i)
                        pool.wait_ge(htp_ready, i * 2)
                        nc.gpsimd.tensor_tensor(x1[:, j, :], z[:, j, :], norm[:, 0, :], ALU.mult).then_inc(xg_ready, 1)


def route(nc, d, l):
    with Phase(nc, f"rt{l}") as ph:
        lg = ph.sb("lg", [P, NT, NR])
        iota = ph.sb("iota", [P, NE])
        blk = ph.sb("blk", [P, NBP])
        before = ph.sb("before", [P, P])
        ones = ph.sb("ones", [P, P])
        tokf = ph.sb("tokf", [P, NT])
        tok = ph.sb("tok", [P, NT], I32)
        zero = ph.sb("zero", [NBP, P], I32)
        gpad = ph.sb("gpad", [P, NT, 8])
        gval, gidx = ph.sb("gval", [P, NT, 8]), ph.sb("gidx", [P, NT, 8], U32)
        gf = ph.sb("gf", [P, NT])
        eg = ph.sb("eg", [P, NT, MG])
        pg = ph.sb("pg", [P, NT])
        oh4 = ph.sb("oh4", [P, NT, MG])
        pen = ph.sb("pen", [P, NT, MG])
        masked = ph.sb("masked", [P, NT, NE])
        val, idx = ph.sb("val", [P, NT, 8]), ph.sb("idx", [P, NT, 8], U32)
        ef = ph.sb("ef", [P, NT, 2])
        dif = ph.sb("dif", [P, NT])
        ex = ph.sb("ex", [P, NT])
        wt = ph.sb("wt", [P, NT, 2])
        oh = [ph.sb(f"oh{j}", [P, NT, NE]) for j in range(2)]
        both = ph.sb("both", [P, NT, NE])
        pre = ph.sb("pre", [P, NT + 1, NE])
        cnti = ph.sb("cnti", [P, NE], I32)
        pc = ph.sb("pc", [P, NE])
        pend = ph.sb("pend", [P, NE])
        pstart = ph.sb("pstart", [P, NE])
        dest = ph.sb("dest", [P, NT, NE])
        hit = ph.sb("hit", [P, NT, NE])
        destf = ph.sb("destf", [P, NT, 2])
        desti = ph.sb("desti", [P, NT, 2], I32)
        le = ph.sb("le", [P, NBP, NE])
        bef = ph.sb("bef", [P, NBP])
        bei = ph.sb("bei", [P, NBP], I32)
        rank, total = ph.ps("rank", [P, NT, NE]), ph.ps("total", [P, NT, NE])
        in_sem, e_in, e_out, d_in, d_out = (ph.sem(s) for s in ("in", "e_in", "e_out", "d_in", "d_out"))
        both_ready, rank_ready, tok_ready, zero_ready, zeroed = (ph.sem(s) for s in ("both_ready", "rank_ready", "tok_ready", "zero_ready", "zeroed"))
        dest_ready, blk_ready, out_done = (ph.sem(s) for s in ("dest_ready", "blk_ready", "out_done"))
        scattered = d["pool_dma"](f"rt{l}")[0]

        def over(a, shape):
            return a.rearrange("p (n o) -> p n o", o=1).to_broadcast(shape)

        def per_tile(a, n, k):
            return a.rearrange("p (o k) -> p o k", o=1).to_broadcast([P, n, k])

        with nc.Block() as block:
            @block.sync
            def _(sp):
                sp.dma_start(lg[:, :, :], d["lg"].rearrange("(c p) n -> p c n", p=P)).then_inc(in_sem, 16)
                for t, c, n in ((iota, C_EXP, NE), (blk, C_BLK, NBP), (before, C_BEFORE, P), (ones, C_ONES, P), (tokf, C_TOK, NT)):
                    sp.dma_start(t[:, :], d["consts"][:, c:c + n]).then_inc(in_sem, 16)
                sp.wait_ge(zero_ready, 1)
                sp.dma_start(d["slot_tok"].rearrange("(b p) o -> b (p o)", p=P), zero[:, :]).then_inc(zeroed, 16)
                sp.wait_ge(dest_ready, 1)
                sp.dma_start(d["dest"], desti[:, :, :].rearrange("p c j -> p (c j)")).then_inc(out_done, 16)
                sp.dma_start(d["wt"], wt[:, :, :].rearrange("p c j -> p (c j)")).then_inc(out_done, 16)
                sp.wait_ge(blk_ready, 1)
                sp.dma_start(d["block_e"], bei[0:1, :]).then_inc(out_done, 16)
                sp.wait_ge(out_done, 48)

            @block.scalar
            def _(act):
                act.wait_ge(e_in, 1)
                nc.scalar.activation(eg[:, :, :], eg[:, :, :], ACT.Exp).then_inc(e_out, 1)
                act.wait_ge(d_in, 1)
                nc.scalar.activation(ex[:, :], dif[:, :], ACT.Exp).then_inc(d_out, 1)

            @block.tensor
            def _(pe):
                pe.wait_ge(both_ready, 1)
                nc.tensor.matmul(rank[:, :, :], before[:, :], both[:, :, :], start=True, stop=True)
                nc.tensor.matmul(total[:, :, :], ones[:, :], both[:, :, :], start=True, stop=True).then_inc(rank_ready, 1)

            @block.vector
            def _(dve):
                v = nc.vector
                v.memset(zero[:, :], 0).then_inc(zero_ready, 1)
                v.memset(gpad[:, :, :], -3e38)
                dve.drain()
                dve.wait_ge(in_sem, 16 * 6)
                v.tensor_copy(tok[:, :], tokf[:, :]).then_inc(tok_ready, 1)
                v.tensor_copy(gpad[:, :, 0:MG], lg[:, :, 0:MG])
                dve.drain()
                for c in range(NT):
                    v.max(gval[:, c, :], gpad[:, c, :])
                dve.drain()
                for c in range(NT):
                    v.max_index(gidx[:, c, :], gval[:, c, :], gpad[:, c, :])
                v.tensor_tensor(eg[:, :, :], lg[:, :, 0:MG], over(gval[:, :, 0], [P, NT, MG]), ALU.subtract).then_inc(e_in, 1)
                dve.drain()
                v.tensor_copy(gf[:, :], gidx[:, :, 0])
                dve.drain()
                v.tensor_tensor(oh4[:, :, :], per_tile(iota[:, 0:MG], NT, MG), over(gf[:, :], [P, NT, MG]), ALU.is_equal)
                dve.drain()
                v.tensor_scalar(pen[:, :, :], oh4[:, :, :], -NEG, NEG, ALU.mult, ALU.add)
                m4 = masked[:, :, :].rearrange("p c (g e) -> p c g e", g=MG)
                wide = [P, NT, MG, ME]
                v.tensor_tensor(m4, lg[:, :, MG:NR].rearrange("p c (g e) -> p c g e", g=MG),
                                oh4[:, :, :].rearrange("p c (g o) -> p c g o", o=1).to_broadcast(wide), ALU.mult)
                dve.drain()
                v.tensor_tensor(m4, m4, pen[:, :, :].rearrange("p c (g o) -> p c g o", o=1).to_broadcast(wide), ALU.add)
                dve.drain()
                for c in range(NT):
                    v.max(val[:, c, :], masked[:, c, :])
                dve.drain()
                for c in range(NT):
                    v.max_index(idx[:, c, :], val[:, c, :], masked[:, c, :])
                v.tensor_tensor(dif[:, :], val[:, :, 1], val[:, :, 0], ALU.subtract).then_inc(d_in, 1)
                dve.drain()
                v.tensor_copy(ef[:, :, :], idx[:, :, 0:2])
                dve.drain()
                for j in range(2):
                    v.tensor_tensor(oh[j][:, :, :], per_tile(iota[:, :], NT, NE), over(ef[:, :, j], [P, NT, NE]), ALU.is_equal)
                dve.drain()
                v.tensor_tensor(both[:, :, :], oh[0][:, :, :], oh[1][:, :, :], ALU.add).then_inc(both_ready, 1)
                dve.wait_ge(e_out, 1)
                v.tensor_reduce(pg[:, :], eg[:, :, :], AX_X, ALU.add)
                dve.wait_ge(d_out, 1)
                v.tensor_scalar(dif[:, :], ex[:, :], 1.0, None, ALU.add)
                dve.drain()
                v.tensor_tensor(pg[:, :], pg[:, :], dif[:, :], ALU.mult)
                dve.drain()
                v.reciprocal(wt[:, :, 0], pg[:, :])
                dve.drain()
                v.tensor_tensor(wt[:, :, 1], wt[:, :, 0], ex[:, :], ALU.mult)
                v.memset(pre[:, 0, :], 0.0)
                dve.wait_ge(rank_ready, 1)
                for c in range(NT):
                    dve.drain()
                    v.tensor_tensor(pre[:, c + 1, :], pre[:, c, :], total[:, c, :], ALU.add)
                dve.drain()
                v.tensor_copy(cnti[:, :], pre[:, NT, :])
                dve.drain()
                v.tensor_scalar(cnti[:, :], cnti[:, :], float(P - 1), None, ALU.add)
                dve.drain()
                v.tensor_scalar(cnti[:, :], cnti[:, :], 7, 7, ALU.logical_shift_right, ALU.logical_shift_left)
                dve.drain()
                v.tensor_copy(pc[:, :], cnti[:, :])
                dve.drain()
                v.tensor_tensor_scan(pend[:, :], ones[:, 0:NE], pc[:, :], 0.0, ALU.mult, ALU.add)
                dve.drain()
                v.tensor_tensor(pstart[:, :], pend[:, :], pc[:, :], ALU.subtract)
                v.tensor_tensor(dest[:, :, :], rank[:, :, :], pre[:, 0:NT, :], ALU.add)
                dve.drain()
                v.tensor_tensor(dest[:, :, :], dest[:, :, :], per_tile(pstart[:, :], NT, NE), ALU.add)
                for j in range(2):
                    dve.drain()
                    v.tensor_tensor(hit[:, :, :], dest[:, :, :], oh[j][:, :, :], ALU.mult)
                    dve.drain()
                    v.tensor_reduce(destf[:, :, j], hit[:, :, :], AX_X, ALU.add)
                dve.drain()
                v.tensor_copy(desti[:, :, :], destf[:, :, :])
                dve.drain().then_inc(dest_ready, 1)
                v.tensor_tensor(le[:, :, :], per_tile(pend[:, :], NBP, NE), over(blk[:, :], [P, NBP, NE]), ALU.is_le)
                dve.drain()
                v.tensor_reduce(bef[:, :], le[:, :, :], AX_X, ALU.add)
                dve.drain()
                v.tensor_scalar(bef[:, :], bef[:, :], float(NE - 1), None, ALU.min)
                dve.drain()
                v.tensor_copy(bei[:, :], bef[:, :]).then_inc(blk_ready, 1)

            @block.gpsimd
            def _(pool):
                pool.wait_ge(tok_ready, 1)
                pool.wait_ge(dest_ready, 1)
                pool.wait_ge(zeroed, 16)
                for c in range(NT):
                    for j in range(2):
                        nc.gpsimd.indirect_dma_start(out=d["slot_tok"], out_offset=bass.IndirectOffsetOnAxis(ap=desti[:, c, j:j + 1], axis=0),
                                                     in_=tok[:, c:c + 1], in_offset=None).then_inc(scattered, 16)
                pool.wait_ge(scattered, 16 * 2 * NT)


def experts(nc, d, l):
    JH = HID // P
    with Phase(nc, f"ex{l}") as ph:
        ident = ph.sb("ident", [P, P])
        cols = ph.sb("cols", [P, 2, KD])
        slots = ph.sb("slots", [NBP, P], I32)
        slotf = ph.sb("slotf", [NBP, P])
        tok = ph.sb("tok", [P, NBP], I32)
        tokb = ph.sb("tokb", [P, 2], I32)
        be = ph.sb("be", [1, NBP], I32)
        xg = ph.sb("xg", [P, 2, D])
        hT = ph.sb("hT", [P, 2, KD, P])
        wgu = ph.sb("wgu", [P, 2, KD, 2, HID])
        wd = ph.sb("wd", [P, 2, JH, D])
        sg = ph.sb("sg", [P, HID])
        a = ph.sb("a", [P, HID])
        aT = ph.sb("aT", [P, JH, P])
        y = ph.sb("y", [P, 2, D])
        tp = [ph.ps(f"tp{i}", [P, 4, P]) for i in range(2)]
        gu = [ph.ps(f"gu{j}", [P, 2, HID]) for j in range(2)]
        at = ph.ps("at", [P, JH, P])
        acc = [ph.ps(f"acc{i}", [P, CH]) for i in range(2)]
        (c_in, s_in, cols_ready, slotf_ready, st_ready, tok_ready, htp_ready, hT_act, hT_dve, gu_ready, sg_ready, a_ready, atp_ready, aT_ready,
         acc_ready, y_act, y_dve, waited, free) = (ph.sem(s) for s in (
             "c_in", "s_in", "cols_ready", "slotf_ready", "st_ready", "tok_ready", "htp_ready", "hT_act", "hT_dve", "gu_ready", "sg_ready", "a_ready",
             "atp_ready", "aT_ready", "acc_ready", "y_act", "y_dve", "waited", "free"))
        gu_in, wd_in, stored = ([ph.sem(f"{n}{j}") for j in range(2)] for n in ("gu_in", "wd_in", "stored"))
        x_in = d["pool_dma"](f"ex{l}")
        views = [d[n][l].rearrange("e (p k) n -> e p k n", p=P) for n in ("moe_w_gate", "moe_w_up", "moe_w_down")]

        with nc.Block() as block:
            @block.sync
            def _(sp):
                sp.dma_start(be[:, :], d["block_e"]).then_inc(s_in, 16)
                sp.dma_start(slots[:, :], d["slot_tok"].rearrange("(b p) o -> b (p o)", p=P)).then_inc(s_in, 16)
                sp.dma_start(ident[:, :], d["consts"][:, C_ID:C_ID + P]).then_inc(c_in, 16)
                load_mod_columns(sp, nc, d, cols, l, (3, 4), c_in)
                sp.wait_ge(s_in, 32)

                def step(b, j, first):
                    if not (isinstance(b, int) and b < 2):
                        sp.wait_ge(gu_ready, b - 1)
                    e = sp.value_load(be[0:1, ds(b, 1)], min_val=0, max_val=NE - 1)
                    for n in range(2):
                        sp.dma_start(wgu[:, j, :, n, :], views[n][ds(e, 1), :, :, :].rearrange("e p k n -> p (e k) n")).then_inc(gu_in[j], 16)
                    if not (isinstance(b, int) and b < 2):
                        sp.wait_ge(acc_ready, b - 1)
                        settle(sp, waited)
                    sp.dma_start(wd[:, j, :, :], views[2][ds(e, 1), :, :, :].rearrange("e p k n -> p (e k) n")).then_inc(wd_in[j], 16)

                step(0, 0, True)
                step(1, 1, True)
                with sp.Fori(1, (NB - 1) // 2) as i:
                    for j in range(2):
                        step(i * 2 + j, j, False)
                step(NB - 1, 0, False)

            @block.gpsimd
            def _(pool):
                pool.wait_ge(tok_ready, 1)

                def step(b, j, first):
                    if not (isinstance(b, int) and b < 2):
                        pool.wait_ge(htp_ready, b - 1)
                    nc.gpsimd.tensor_copy(tokb[:, j:j + 1], tok[:, ds(b, 1)])
                    pool.drain()
                    nc.gpsimd.indirect_dma_start(out=xg[:, j, :], out_offset=None, in_=d["x1"],
                                                 in_offset=bass.IndirectOffsetOnAxis(ap=tokb[:, j:j + 1], axis=0)).then_inc(x_in[j], 16)

                step(0, 0, True)
                step(1, 1, True)
                with pool.Fori(1, (NB - 1) // 2) as i:
                    for j in range(2):
                        step(i * 2 + j, j, False)
                step(NB - 1, 0, False)

            @block.tensor
            def _(pe):
                pe.wait_ge(slotf_ready, 1)
                pe.wait_ge(c_in, 48)
                nc.tensor.transpose(at[:, 0, 0:NBP], slotf[:, :], ident[0:NBP, 0:NBP]).then_inc(st_ready, 1)

                def transposes(b, j):
                    pe.wait_ge(x_in[j], 8 * (b - j) + 16)
                    pe.wait_ge(hT_act, b)
                    pe.wait_ge(hT_dve, b)
                    for k in range(KD):
                        ins = nc.tensor.transpose(tp[k // 4][:, k % 4, :], xg[:, j, k:D:KD], ident[:, :])
                    ins.then_inc(htp_ready, 1)

                def gate_up(b, j, half):
                    if half == 0:
                        pe.wait_ge(hT_act, b + 1)
                        pe.wait_ge(hT_dve, b + 1)
                        pe.wait_ge(gu_in[j], 16 * (b - j) + 32)
                        if not (isinstance(b, int) and b < 2):
                            pe.wait_ge(a_ready, b - 1)
                    for k in range(half * 4, half * 4 + 4):
                        ins = nc.tensor.matmul(gu[j][:, :, :], hT[:, j, k, :], wgu[:, j, k, :, :], start=(k == 0), stop=(k == KD - 1))
                    if half:
                        ins.then_inc(gu_ready, 1)

                def act_transposes(b):
                    pe.wait_ge(a_ready, b + 1)
                    pe.wait_ge(aT_ready, b)
                    for k in range(JH):
                        ins = nc.tensor.transpose(at[:, k, :], a[:, k:HID:JH], ident[:, :])
                    ins.then_inc(atp_ready, 1)

                def down(b, j):
                    pe.wait_ge(aT_ready, b + 1)
                    pe.wait_ge(wd_in[j], 8 * (b - j) + 16)
                    pe.wait_ge(y_act, b)
                    pe.wait_ge(y_dve, b)
                    for half in range(2):
                        for k in range(JH):
                            ins = nc.tensor.matmul(acc[half][:, :], aT[:, k, :], wd[:, j, k, half * CH:(half + 1) * CH],
                                                   start=(k == 0), stop=(k == JH - 1))
                    ins.then_inc(acc_ready, 1)

                def step(b, j, first, last):
                    gate_up(b, j, 0)
                    if not first:
                        act_transposes(b - 1)
                    gate_up(b, j, 1)
                    if not last:
                        transposes(b + 1, 1 - j)
                    if not first:
                        down(b - 1, 1 - j)

                pe.wait_ge(tok_ready, 1)
                transposes(0, 0)
                step(0, 0, True, False)
                with pe.Fori(0, (NB - 3) // 2) as i:
                    for j in range(2):
                        step(i * 2 + j + 1, (j + 1) % 2, False, False)
                step(NB - 2, 1, False, False)
                step(NB - 1, 0, False, True)
                act_transposes(NB - 1)
                down(NB - 1, 0)

            @block.scalar
            def _(act):
                act.wait_ge(cols_ready, 1)

                def rows(b, j):
                    act.wait_ge(htp_ready, b + 1)
                    if not (isinstance(b, int) and b < 2):
                        act.wait_ge(gu_ready, b - 1)
                    for k in range(4):
                        ins = nc.scalar.activation(hT[:, j, k, :], tp[0][:, k, :], ACT.Identity, bias=cols[:, 0, k:k + 1], scale=cols[:, 1, k:k + 1])
                    ins.then_inc(hT_act, 1)

                def store(b, j):
                    act.wait_ge(acc_ready, b + 1)
                    act.wait_ge(stored[j], 8 * (b - j))
                    nc.scalar.activation(y[:, j, CH:D], acc[1][:, :], ACT.Copy).then_inc(y_act, 1)
                    act.wait_ge(y_act, b + 1)
                    act.wait_ge(y_dve, b + 1)
                    settle(act, waited)
                    act.dma_start(d["ybuf"][ds(b * P, P), :], y[:, j, :]).then_inc(stored[j], 16)

                def step(b, j, first, last):
                    act.wait_ge(gu_ready, b + 1)
                    act.wait_ge(a_ready, b)
                    nc.scalar.activation(sg[:, :], gu[j][:, 0, :], ACT.Silu).then_inc(sg_ready, 1)
                    if not last:
                        rows(b + 1, 1 - j)
                    if not first:
                        store(b - 1, 1 - j)

                rows(0, 0)
                step(0, 0, True, False)
                with act.Fori(0, (NB - 3) // 2) as i:
                    for j in range(2):
                        step(i * 2 + j + 1, (j + 1) % 2, False, False)
                step(NB - 2, 1, False, False)
                step(NB - 1, 0, False, True)
                store(NB - 1, 0)
                act.wait_ge(stored[0], 8 * (NB + 1))
                act.wait_ge(stored[1], 8 * (NB - 1))

            @block.vector
            def _(dve):
                dve.wait_ge(c_in, 48)
                nc.vector.tensor_scalar(cols[:, 1, :], cols[:, 1, :], 1.0, None, ALU.add).then_inc(cols_ready, 1)
                dve.wait_ge(s_in, 32)
                nc.vector.tensor_copy(slotf[:, :], slots[:, :]).then_inc(slotf_ready, 1)
                dve.wait_ge(st_ready, 1)
                nc.vector.tensor_copy(tok[:, :], at[:, 0, 0:NBP]).then_inc(tok_ready, 1)
                dve.wait_ge(cols_ready, 1)

                def rows(b, j):
                    dve.wait_ge(htp_ready, b + 1)
                    if not (isinstance(b, int) and b < 2):
                        dve.wait_ge(gu_ready, b - 1)
                    for k in range(4, KD):
                        ins = nc.vector.tensor_scalar(hT[:, j, k, :], tp[1][:, k - 4, :], cols[:, 1, k:k + 1], cols[:, 0, k:k + 1], ALU.mult, ALU.add)
                    ins.then_inc(hT_dve, 1)

                def output(b, j):
                    dve.wait_ge(acc_ready, b + 1)
                    dve.wait_ge(stored[j], 8 * (b - j))
                    nc.vector.tensor_copy(y[:, j, 0:CH], acc[0][:, :]).then_inc(y_dve, 1)

                def turned(b):
                    dve.wait_ge(atp_ready, b + 1)
                    dve.wait_ge(acc_ready, b)
                    nc.vector.tensor_copy(aT[:, :, :], at[:, :, :]).then_inc(aT_ready, 1)

                def step(b, j, first, last):
                    if not first:
                        turned(b - 1)
                    dve.wait_ge(sg_ready, b + 1)
                    dve.wait_ge(atp_ready, b)
                    nc.vector.tensor_tensor(a[:, :], sg[:, :], gu[j][:, 1, :], ALU.mult).then_inc(a_ready, 1)
                    if not last:
                        rows(b + 1, 1 - j)
                    if not first:
                        output(b - 1, 1 - j)

                rows(0, 0)
                step(0, 0, True, False)
                with dve.Fori(0, (NB - 3) // 2) as i:
                    for j in range(2):
                        step(i * 2 + j + 1, (j + 1) % 2, False, False)
                step(NB - 2, 1, False, False)
                step(NB - 1, 0, False, True)
                turned(NB - 1)
                output(NB - 1, 0)


def combine(nc, d, l):
    out = d["x2"] if l == 0 else d["out"][0]
    with Phase(nc, f"cb{l}") as ph:
        norm = ph.sb("norm", [P, 2, D])
        gain = ph.sb("gain", [P, D])
        dest = ph.sb("dest", [P, NT, 2], I32)
        wt = ph.sb("wt", [P, NT, 2])
        destb = ph.sb("destb", [P, 2, 2], I32)
        wb = ph.sb("wb", [P, 2])
        x = ph.sb("x", [P, 2, D])
        y0, y1 = ph.sb("y0", [P, 2, D]), ph.sb("y1", [P, 2, D])
        z = ph.sb("z", [P, 2, D])
        x2 = ph.sb("x2", [P, 2, D])
        stats = ph.sb("stats", [P, 2, 6])
        mv = ph.sb("mv", [P, 2])
        std = ph.sb("std", [P, 2])
        (c_in, gain_ready, y0_ready, z_ready, v_ready, std_ready, xn_ready, xg_ready, x2_ready, waited) = (
            ph.sem(s) for s in ("c_in", "gain_ready", "y0_ready", "z_ready", "v_ready", "std_ready", "xn_ready", "xg_ready", "x2_ready", "waited"))
        x_in, stored = ([ph.sem(f"{n}{j}") for j in range(2)] for n in ("x_in", "stored"))
        y_in = d["pool_dma"](f"cb{l}")
        with nc.Block() as block:
            @block.sync
            def _(sp):
                load_norm(sp, nc, d, norm, gain, l, 1, c_in)
                sp.dma_start(dest[:, :, :].rearrange("p c j -> p (c j)"), d["dest"]).then_inc(c_in, 16)
                sp.dma_start(wt[:, :, :].rearrange("p c j -> p (c j)"), d["wt"]).then_inc(c_in, 16)

                def store(c, j):
                    sp.wait_ge(x2_ready, c + 1)
                    settle(sp, waited)
                    sp.dma_start(out[ds(c * P, P), :], x2[:, j, :]).then_inc(stored[j], 16)

                for j in range(2):
                    sp.dma_start(x[:, j, :], d["x1"][j * P:(j + 1) * P, :]).then_inc(x_in[j], 16)
                with sp.Fori(0, NT // 2 - 1) as i:
                    for j in range(2):
                        sp.wait_ge(z_ready, i * 2 + j + 1)
                        settle(sp, waited)
                        sp.dma_start(x[:, j, :], d["x1"][ds((i * 2 + j + 2) * P, P), :]).then_inc(x_in[j], 16)
                        store(i * 2 + j, j)
                for j in range(2):
                    store(NT - 2 + j, j)
                for j in range(2):
                    sp.wait_ge(stored[j], 16 * NT // 2)

            @block.gpsimd
            def _(pool):
                pool.wait_ge(c_in, 80)

                def gather(c, j):
                    nc.gpsimd.tensor_copy(destb[:, j, :], dest[:, ds(c, 1), :])
                    pool.drain()
                    for n, y in enumerate((y0, y1)):
                        nc.gpsimd.indirect_dma_start(out=y[:, j, :], out_offset=None, in_=d["ybuf"],
                                                     in_offset=bass.IndirectOffsetOnAxis(ap=destb[:, j, n:n + 1], axis=0)).then_inc(y_in[j], 16)

                def step(c, j, more):
                    if more:
                        pool.wait_ge(z_ready, c + 1)
                        gather(c + 2, j)
                    pool.wait_ge(xn_ready, c + 1)
                    pool.wait_ge(stored[j], 8 * (c - j))
                    nc.gpsimd.tensor_tensor(x2[:, j, :], z[:, j, :], norm[:, 0, :], ALU.mult).then_inc(xg_ready, 1)

                gather(0, 0)
                gather(1, 1)
                with pool.Fori(0, NT // 2 - 1) as i:
                    for j in range(2):
                        step(i * 2 + j, j, True)
                for j in range(2):
                    step(NT - 2 + j, j, False)

            @block.scalar
            def _(act):
                with act.Fori(0, NT // 2) as i:
                    for j in range(2):
                        act.wait_ge(v_ready, i * 2 + j + 1)
                        nc.scalar.activation(std[:, 1:2], std[:, 0:1], ACT.Sqrt).then_inc(std_ready, 1)

            @block.vector
            def _(dve):
                dve.wait_ge(c_in, 80)
                nc.vector.tensor_scalar(gain[:, :], gain[:, :], 1.0, None, ALU.add)
                with dve.Fori(0, NT // 2) as i:
                    for j in range(2):
                        c = i * 2 + j
                        nc.vector.tensor_copy(wb[:, :], wt[:, ds(c, 1), :])
                        dve.drain()
                        dve.wait_ge(y_in[j], 32 * i + 32)
                        nc.vector.tensor_scalar(y0[:, j, :], y0[:, j, :], wb[:, 0:1], None, ALU.mult)
                        dve.drain()
                        nc.vector.scalar_tensor_tensor(y0[:, j, :], y1[:, j, :], wb[:, 1:2], y0[:, j, :], ALU.mult, ALU.add)
                        dve.drain()
                        nc.vector.tensor_tensor(z[:, j, :], y0[:, j, :], gain[:, :], ALU.mult)
                        dve.drain()
                        dve.wait_ge(x_in[j], 16 * i + 16)
                        nc.vector.scalar_tensor_tensor(z[:, j, :], x[:, j, :], ALPHA, z[:, j, :], ALU.mult, ALU.add).then_inc(z_ready, 1)
                        dve.wait_ge(z_ready, c + 1)
                        for half in range(2):
                            nc.vector.bn_stats(stats[:, half, :], z[:, j, half * CH:(half + 1) * CH])
                        dve.drain()
                        nc.vector.bn_aggr(mv[:, :], stats[:, :, :].rearrange("p a b -> p (a b)"))
                        dve.drain()
                        nc.vector.tensor_scalar(std[:, 0:1], mv[:, 1:2], LN_EPS, None, ALU.add).then_inc(v_ready, 1)
                        dve.wait_ge(std_ready, c + 1)
                        nc.vector.reciprocal(std[:, 0:1], std[:, 1:2])
                        dve.drain()
                        nc.vector.tensor_scalar(z[:, j, :], z[:, j, :], mv[:, 0:1], std[:, 0:1], ALU.subtract, ALU.mult).then_inc(xn_ready, 1)
                        dve.wait_ge(xg_ready, c + 1)
                        nc.vector.tensor_tensor(x2[:, j, :], x2[:, j, :], norm[:, 1, :], ALU.add).then_inc(x2_ready, 1)


TWO_PI = 2.0 * np.pi
PI_HI = 6.28125
PI_MID = float(np.round((TWO_PI - PI_HI) * 2 ** 20) / 2 ** 20)
PI_LO = float(TWO_PI - PI_HI - PI_MID)
ROUND = 1.5 * 2.0 ** 23


def project_rope(nc, d, which):
    kv = which == "kv"
    NBK = 2 * G if kv else G
    RING = 3
    NQH = G * HP
    HH = DH // 2
    with Phase(nc, f"p{which}") as ph:
        w = ph.sb("w", [P, KD, NBK * CH])
        ident = ph.sb("ident", [P, P])
        cols = ph.sb("cols", [P, 2, KD])
        pos = ph.sb("pos", [P, NT], I32)
        posf = ph.sb("posf", [P, NT])
        freq = ph.sb("freq", [P, HH])
        ang = ph.sb("ang", [P, NT, HH])
        turns = ph.sb("turns", [P, 2, NT, HH])
        cs = ph.sb("cs", [P, 2, NT, HH])
        csb = ph.sb("csb", [P, 2, HH])
        x = ph.sb("x", [P, 2, D])
        hT = ph.sb("hT", [P, 2, KD, P])
        part = ph.sb("part", [P, 4, G, BH, HH])
        roped = ph.sb("roped", [P, G, BH, 2, HH])
        rT = ph.sb("rT", [P, 2, G, 4, P])
        vo = ph.sb("vo", [P, 2, G, CH]) if kv else None
        tp = [ph.ps(f"tp{i}", [P, 4, P]) for i in range(2)]
        mm = [ph.ps(f"mm{i}", [P, CH]) for i in range(RING)]
        rt = [ph.ps(f"rt{i}", [P, 4, P]) for i in range(G)]
        (c_in, pos_in, cols_ready, r_ready, cs_ready, tp_ready, hT_act, hT_dve, mm_ready, ev_rope, ev_v, part_ready, roped_ready, rt_ready, rT_ready, waited) = (
            ph.sem(s) for s in ("c_in", "pos_in", "cols_ready", "r_ready", "cs_ready", "tp_ready", "hT_act", "hT_dve", "mm_ready", "ev_rope", "ev_v",
                                "part_ready", "roped_ready", "rt_ready", "rT_ready", "waited"))
        w_in = ph.sem("w_in")
        x_in, st_r, st_v = ([ph.sem(f"{n}{j}") for j in range(2)] for n in ("x_in", "st_r", "st_v"))
        NC_IN = 2 if kv else 4

        def steps(eng, step):
            step(0, 0, True, False)
            with eng.Fori(0, NT // 2 - 1) as i:
                for j in range(2):
                    step(i * 2 + j + 1, (j + 1) % 2, False, False)
            step(NT - 1, 1, False, True)

        with nc.Block() as block:
            @block.sync
            def _(sp):
                sp.dma_start(pos[:, :], d["positions"].rearrange("b (c p) -> p (b c)", p=P), allow_slow_non_contiguous=True).then_inc(pos_in, 16)
                sp.dma_start(freq[:, :], d["consts"][:, C_FREQ:C_FREQ + HH]).then_inc(c_in, 16)
                sp.dma_start(ident[:, :], d["consts"][:, C_ID:C_ID + P]).then_inc(c_in, 16)
                if not kv:
                    load_mod_columns(sp, nc, d, cols, 1, (0, 1), c_in)
                for j in range(2):
                    sp.dma_start(x[:, j, :], d["x2"][j * P:(j + 1) * P, :]).then_inc(x_in[j], 16)
                w_dram = d["b_w_kv"] if kv else d["b_w_q"][0]
                sp.dma_start(w[:, :, :], w_dram.rearrange("(p k) n -> p k n", k=KD)).then_inc(w_in, 16)

                def store(c, j):
                    if kv:
                        sp.wait_ge(ev_v, G * c + G)
                        settle(sp, waited)
                        sp.dma_start(d["v"][ds(c * P, P), :], vo[:, j, :, :].rearrange("p g n -> p (g n)")).then_inc(st_v[j], 16)

                def store_roped(c, j):
                    sp.wait_ge(rT_ready, G * c + G)
                    settle(sp, waited)
                    sp.dma_start(d["kT" if kv else "qT"][:, :, ds(c * P, P)].rearrange("g p t -> p g t"),
                                 rT[:, j, :, :, :].rearrange("p g h t -> p (g h) t")).then_inc(st_r[j], 16)

                def step(c, j, first, last):
                    if not first:
                        store_roped(c - 1, 1 - j)
                    store(c, j)

                step(0, 0, True, False)
                with sp.Fori(0, NT // 2 - 1) as i:
                    for j in range(2):
                        c, jj = i * 2 + j, j
                        sp.wait_ge(tp_ready, c + 1)
                        settle(sp, waited)
                        sp.dma_start(x[:, jj, :], d["x2"][ds((c + 2) * P, P), :]).then_inc(x_in[jj], 16)
                        step(c + 1, 1 - jj, False, False)
                step(NT - 1, 1, False, True)
                store_roped(NT - 1, 1)
                for j in range(2):
                    sp.wait_ge(st_r[j], 16 * NT // 2)
                    if kv:
                        sp.wait_ge(st_v[j], 16 * NT // 2)

            @block.tensor
            def _(pe):
                pe.wait_ge(c_in, 16 * NC_IN)

                def transposes(c, j):
                    pe.wait_ge(x_in[j], 8 * (c - j) + 16)
                    pe.wait_ge(hT_act, c)
                    pe.wait_ge(hT_dve, c)
                    for k in range(KD):
                        ins = nc.tensor.transpose(tp[k // 4][:, k % 4, :], x[:, j, k:D:KD], ident[:, :])
                    ins.then_inc(tp_ready, 1)

                def bank(c, j, n, first):
                    if n < RING:
                        if not first:
                            pe.wait_ge(ev_v if kv else ev_rope, G * (c - 1) + n + 1)
                    else:
                        pe.wait_ge(ev_rope, G * c + n - RING + 1)
                    for k in range(KD):
                        ins = nc.tensor.matmul(mm[n % RING][:, :], hT[:, j, k, :], w[:, k, n * CH:(n + 1) * CH], start=(k == 0), stop=(k == KD - 1))
                    ins.then_inc(mm_ready, 1)

                def roped_transposes(c):
                    pe.wait_ge(roped_ready, c + 1)
                    pe.wait_ge(rT_ready, G * c)
                    for g in range(G):
                        for h in range(4):
                            ins = nc.tensor.transpose(rt[g][:, h, :], roped[:, g, 2 * h:2 * h + 2, :, :].rearrange("p a b e -> p (a b e)"), ident[:, :])
                        ins.then_inc(rt_ready, 1)

                def step(c, j, first, last):
                    pe.wait_ge(hT_act, c + 1)
                    pe.wait_ge(hT_dve, c + 1)
                    if first:
                        pe.wait_ge(w_in, 16)
                    for n in range(NBK):
                        bank(c, j, n, first)
                        if n == 0 and not last:
                            transposes(c + 1, 1 - j)
                        if n == 1 and not first:
                            roped_transposes(c - 1)

                transposes(0, 0)
                steps(pe, step)
                roped_transposes(NT - 1)

            @block.scalar
            def _(act):
                act.wait_ge(r_ready, 1)
                nc.scalar.activation(cs[:, :, :, :], turns[:, :, :, :], ACT.Sin).then_inc(cs_ready, 1)
                act.wait_ge(cols_ready, 1)

                def rows(c, j):
                    act.wait_ge(tp_ready, c + 1)
                    if not (isinstance(c, int) and c == 0):
                        act.wait_ge(mm_ready, NBK * (c - 1))
                    for k in range(4):
                        ins = nc.scalar.activation(hT[:, j, k, :], tp[0][:, k, :], ACT.Identity, bias=cols[:, 0, k:k + 1], scale=cols[:, 1, k:k + 1])
                    ins.then_inc(hT_act, 1)

                def turned(c, j):
                    act.wait_ge(st_r[j], 8 * (c - j))
                    for g in range(G):
                        act.wait_ge(rt_ready, G * c + g + 1)
                        nc.scalar.activation(rT[:, j, g, :, :], rt[g][:, :, :], ACT.Copy).then_inc(rT_ready, 1)

                def step(c, j, first, last):
                    if not last:
                        rows(c + 1, 1 - j)
                    if not first:
                        turned(c - 1, 1 - j)
                    if kv:
                        act.wait_ge(st_v[j], 8 * (c - j))
                        for g in range(G):
                            act.wait_ge(mm_ready, NBK * c + G + g + 1)
                            nc.scalar.activation(vo[:, j, g, :], mm[(G + g) % RING][:, :], ACT.Copy).then_inc(ev_v, 1)

                rows(0, 0)
                steps(act, step)
                turned(NT - 1, 1)

            @block.vector
            def _(dve):
                v = nc.vector
                if kv:
                    v.memset(cols[:, 0, :], 0.0)
                    v.memset(cols[:, 1, :], 1.0)
                    dve.drain().then_inc(cols_ready, 1)
                    dve.wait_ge(c_in, 16 * NC_IN)
                else:
                    dve.wait_ge(c_in, 16 * NC_IN)
                    v.tensor_scalar(cols[:, 1, :], cols[:, 1, :], 1.0, None, ALU.add)
                    dve.drain().then_inc(cols_ready, 1)
                dve.wait_ge(pos_in, 16)
                v.tensor_copy(posf[:, :], pos[:, :])
                dve.drain()
                for c in range(NT):
                    v.tensor_scalar(ang[:, c, :], freq[:, :], posf[:, c:c + 1], None, ALU.mult)
                dve.drain()
                rem = cs
                v.tensor_scalar(turns[:, 0, :, :], ang[:, :, :], 1.0 / TWO_PI, None, ALU.mult)
                v.tensor_scalar(turns[:, 1, :, :], ang[:, :, :], 1.0 / TWO_PI, 0.25, ALU.mult, ALU.add)
                dve.drain()
                v.tensor_scalar(turns[:, :, :, :], turns[:, :, :, :], ROUND, None, ALU.add)
                dve.drain()
                v.tensor_scalar(turns[:, :, :, :], turns[:, :, :, :], ROUND, None, ALU.subtract)
                dve.drain()
                for n, piece in enumerate((PI_HI, PI_MID, PI_LO)):
                    for j in range(2):
                        v.scalar_tensor_tensor(rem[:, j, :, :], turns[:, j, :, :], -piece, ang[:, :, :] if n == 0 else rem[:, j, :, :], ALU.mult, ALU.add)
                    dve.drain()
                v.tensor_scalar(rem[:, 1, :, :], rem[:, 1, :, :], np.pi / 2, None, ALU.add)
                dve.drain()
                lim = 3.1415925
                v.tensor_scalar(turns[:, :, :, :], rem[:, :, :, :], lim, -lim, ALU.min, ALU.max)
                dve.drain().then_inc(r_ready, 1)

                def rows(c, j):
                    dve.wait_ge(tp_ready, c + 1)
                    if not (isinstance(c, int) and c == 0):
                        dve.wait_ge(mm_ready, NBK * (c - 1))
                    for k in range(4, KD):
                        ins = v.tensor_scalar(hT[:, j, k, :], tp[1][:, k - 4, :], cols[:, 1, k:k + 1], cols[:, 0, k:k + 1], ALU.mult, ALU.add)
                    ins.then_inc(hT_dve, 1)

                def step(c, j, first, last):
                    if not last:
                        rows(c + 1, 1 - j)
                    dve.wait_ge(roped_ready, c)
                    v.tensor_copy(csb[:, :, :], cs[:, :, ds(c, 1), :])
                    dve.drain()
                    sin, cos = (csb[:, a, :].rearrange("p (o e) -> p o e", o=1).to_broadcast([P, BH, HH]) for a in range(2))
                    for g in range(G):
                        dve.wait_ge(mm_ready, NBK * c + g + 1)
                        m = mm[g % RING][:, :].rearrange("p (h a e) -> p h a e", h=BH, a=2)
                        v.tensor_tensor(part[:, 0, g, :, :], m[:, :, 0, :], cos, ALU.mult)
                        v.tensor_tensor(part[:, 1, g, :, :], m[:, :, 1, :], sin, ALU.mult)
                        v.tensor_tensor(part[:, 2, g, :, :], m[:, :, 1, :], cos, ALU.mult)
                        v.tensor_tensor(part[:, 3, g, :, :], m[:, :, 0, :], sin, ALU.mult).then_inc(ev_rope, 1)

                rows(0, 0)
                dve.wait_ge(cs_ready, 1)
                steps(dve, step)

            @block.gpsimd
            def _(pool):
                with pool.Fori(0, NT) as c:
                    pool.wait_ge(ev_rope, G * c + G)
                    pool.wait_ge(rt_ready, G * c)
                    r = roped[:, :, :, :, :].rearrange("p g h a e -> p (g h) a e")
                    q = part[:, :, :, :, :].rearrange("p q g h e -> p q (g h) e")
                    nc.gpsimd.tensor_tensor(r[:, :, 0, :], q[:, 0], q[:, 1], ALU.subtract)
                    nc.gpsimd.tensor_tensor(r[:, :, 1, :], q[:, 2], q[:, 3], ALU.add)
                    pool.drain().then_inc(roped_ready, 1)


def attention(nc, d):
    NBLK = S // P
    UN = 2 * NBLK
    BODY = 2 * UN
    RS, RT, RB, GRP = 4, 2, 4, 8
    with Phase(nc, "at") as ph:
        ident = ph.sb("ident", [P, P])
        band = ph.sb("band", [P, 2 * P])
        q = ph.sb("q", [P, 2, S])
        k = ph.sb("k", [P, 2, S])
        v = ph.sb("v", [P, 2, NBLK, P])
        o = ph.sb("o", [P, 2, NBLK, 2, DH + 2])
        pr = ph.sb("pr", [P, RB, 2 * P])
        pT = ph.sb("pT", [P, RB, 2 * P])
        bs = [ph.ps(f"bs{i}", [P, 2 * P]) for i in range(RS)]
        bt = [ph.ps(f"bt{i}", [P, 2 * P]) for i in range(RT)]
        bo = [ph.ps(f"bo{i}", [P, GRP // 2, 2, DH]) for i in range(2)]
        (c_in, s_ready, m_ready, p_ready, t_ready, pT_act, pT_dve, pv_ready, o_ready, waited) = (
            ph.sem(s) for s in ("c_in", "s_ready", "m_ready", "p_ready", "t_ready", "pT_act", "pT_dve", "pv_ready", "o_ready", "waited"))
        in_sem, stored, used = ([ph.sem(f"{n}{j}") for j in range(2)] for n in ("in", "stored", "used"))

        def unit(g, u):
            par, j, hh = u // UN, (u % UN) // 2, u % 2
            dil = DILATIONS[g]
            nb = NBLK // dil
            return par, j, hh, j % nb > 0, (j % nb) * P * dil + j // nb, dil

        PIECES = [1 if dil == 1 or dil * P == S else dil for dil in DILATIONS]

        def by_block(a, g):
            dil = DILATIONS[g]
            if dil == 1:
                return [a.rearrange("(j i) c -> i j c", i=P)]
            if dil * P == S:
                return [a.rearrange("(i r) c -> i r c", i=P)]
            pieces = a.rearrange("(n i r) c -> r i n c", i=P, r=dil)
            return [pieces[r] for r in range(dil)]

        def split(a, g):
            n = NBLK // PIECES[g]
            return [a[:, r * n:(r + 1) * n] for r in range(PIECES[g])]

        def loads(g, i):
            return sum((2 + PIECES[h]) * (HP // 2) for h in range(g)) + (2 + PIECES[g]) * (i + 1)

        def stores(g, i):
            return sum(PIECES[h] * (HP // 2) for h in range(g)) + PIECES[g] * i

        def on_act(u):
            return u % 2 == 0

        def evacuated(eng, b, u):
            eng.wait_ge(pT_act if on_act(u) else pT_dve, (BODY // 2) * b + u // 2 + 1)

        def copy_out(u, g, copy):
            n = 2 * P if unit(g, u)[3] else P
            return copy(pT[:, u % RB, 0:n], bt[u % RT][:, 0:n])

        def bodies(eng, body):
            for g in range(G):
                with eng.Fori(0, HP // 2) as i:
                    body(g, i, g * (HP // 2) + i)

        with nc.Block() as block:
            @block.sync
            def _(sp):
                sp.dma_start(ident[:, :], d["consts"][:, C_ID:C_ID + P]).then_inc(c_in, 16)
                sp.dma_start(band[:, :], d["consts"][:, C_BAND:C_BAND + 2 * P]).then_inc(c_in, 16)

                def body(g, i, b):
                    for par in range(2):
                        hp = i * 2 + par
                        sp.wait_ge(used[par], b + 1)
                        settle(sp, waited)
                        sp.dma_start(q[:, par, :], d["qT"][ds(g * HP + hp, 1), :, :].rearrange("o p t -> p (o t)")).then_inc(in_sem[par], 16)
                        sp.dma_start(k[:, par, :], d["kT"][ds(g * HP + hp, 1), :, :].rearrange("o p t -> p (o t)")).then_inc(in_sem[par], 16)
                        for dst, src in zip(split(v[:, par, :, :], g), by_block(d["v"][:, ds(g * BW + hp * P, P)], g)):
                            sp.dma_start(dst, src).then_inc(in_sem[par], 16)

                bodies(sp, body)

            @block.tensor
            def _(pe):
                pe.wait_ge(c_in, 32)
                pe.sem_inc(used[0], 1)
                pe.sem_inc(used[1], 1)

                def body(g, i, b):
                    def scores(u):
                        par, j, hh, prev, t0, dil = unit(g, u)
                        if u % UN == 0:
                            pe.wait_ge(in_sem[par], 16 * loads(g, i))
                        if u >= RS:
                            pe.wait_ge(m_ready, BODY * b + u - RS + 1)
                        rows = slice(hh * DH, (hh + 1) * DH)
                        first = t0 - P * dil if prev else t0
                        n = 2 * P if prev else P
                        nc.tensor.matmul(bs[u % RS][:, 0:n], q[rows, par, t0:t0 + (P - 1) * dil + 1:dil], k[rows, par, first:first + (n - 1) * dil + 1:dil],
                                         start=True, stop=True).then_inc(s_ready, 1)

                    def turn(u):
                        prev = unit(g, u)[3]
                        pe.wait_ge(p_ready, BODY * b + u + 1)
                        if u >= RT:
                            evacuated(pe, b, u - RT)
                        for h in range(2 if prev else 1):
                            ins = nc.tensor.transpose(bt[u % RT][:, h * P:(h + 1) * P], pr[:, u % RB, h * P:(h + 1) * P], ident[:, :])
                        ins.then_inc(t_ready, 1)

                    def weigh(u):
                        par, j, hh, prev, t0, dil = unit(g, u)
                        evacuated(pe, b, u)
                        if u % GRP == 0:
                            pe.wait_ge(o_ready, (BODY // GRP) * b + u // GRP + 1)
                        out = bo[(u // GRP) % 2][:, (u % GRP) // 2, hh, :]
                        cols = slice(hh * DH, (hh + 1) * DH)
                        if prev:
                            nc.tensor.matmul(out, pT[:, u % RB, 0:P], v[:, par, j - 1, cols], start=True, stop=False)
                        ins = nc.tensor.matmul(out, pT[:, u % RB, P:2 * P] if prev else pT[:, u % RB, 0:P], v[:, par, j, cols], start=not prev, stop=True)
                        ins.then_inc(pv_ready, 1)
                        if u % UN == UN - 1:
                            pe.wait_ge(pv_ready, BODY * b + u + 1)
                            pe.sem_inc(used[par], 1)

                    scores(0)
                    scores(1)
                    for u in range(BODY):
                        if u + 2 < BODY:
                            scores(u + 2)
                        turn(u)
                        if u:
                            weigh(u - 1)
                    weigh(BODY - 1)

                bodies(pe, body)

            @block.scalar
            def _(act):
                act.sem_inc(o_ready, 2)

                def body(g, i, b):
                    def exp(u):
                        par, j, hh, prev, t0, dil = unit(g, u)
                        n = 2 * P if prev else P
                        act.wait_ge(m_ready, BODY * b + u + 1)
                        nc.scalar.activation(pr[:, u % RB, 0:n], pr[:, u % RB, 0:n], ACT.Exp, scale=-1.0, bias=o[:, par, j, hh, DH:DH + 1],
                                             accum_out=o[:, par, j, hh, DH + 1:DH + 2]).then_inc(p_ready, 1)

                    def output(u):
                        par, j = u // UN, (u % UN) // 2
                        act.wait_ge(pv_ready, BODY * b + u + 1)
                        nc.scalar.activation(o[:, par, j + 1 - GRP // 2:j + 1, :, 0:DH], bo[(u // GRP) % 2][:, :, :, :], ACT.Copy).then_inc(o_ready, 1)
                        if u % UN == UN - 1:
                            act.wait_ge(o_ready, (BODY // GRP) * b + u // GRP + 3)
                            act.wait_ge(p_ready, BODY * b + u + 1)
                            settle(act, waited)
                            src = o[:, par, :, :, :].rearrange("p j h e -> p j (h e)")
                            for s_, t_ in zip(split(src, g), by_block(d["o"][g][:, ds((i * 2 + par) * OW, OW)], g)):
                                act.dma_start(t_, s_).then_inc(stored[par], 16)

                    exp(0)
                    for u in range(BODY):
                        if u + 1 < BODY:
                            exp(u + 1)
                        if on_act(u):
                            act.wait_ge(t_ready, BODY * b + u + 1)
                            if u >= RB:
                                act.wait_ge(pv_ready, BODY * b + u - RB + 1)
                            copy_out(u, g, lambda dst, src: nc.scalar.activation(dst, src, ACT.Copy)).then_inc(pT_act, 1)
                        if u % GRP == 1 and u > 1:
                            output(u - 2)
                    output(BODY - 1)

                bodies(act, body)
                for par in range(2):
                    act.wait_ge(stored[par], 16 * sum(PIECES[g] * (HP // 2) for g in range(G)))

            @block.vector
            def _(dve):
                dve.wait_ge(c_in, 32)

                def body(g, i, b):
                    def mask(u):
                        par, j, hh, prev, t0, dil = unit(g, u)
                        n = 2 * P if prev else P
                        if u % UN == 0:
                            dve.wait_ge(stored[par], 16 * stores(g, i))
                        dve.wait_ge(s_ready, BODY * b + u + 1)
                        if u >= RB:
                            dve.wait_ge(t_ready, BODY * b + u - RB + 1)
                        settle(dve, waited)
                        nc.vector.tensor_tensor_reduce(out=pr[:, u % RB, 0:n], in0=bs[u % RS][:, 0:n], in1=band[:, 2 * P - n:2 * P], scale=-DH ** -0.5,
                                                       scalar=3e38, op0=ALU.add, op1=ALU.min, accum_out=o[:, par, j, hh, DH:DH + 1]).then_inc(m_ready, 1)

                    mask(0)
                    mask(1)
                    for u in range(BODY):
                        if u + 2 < BODY:
                            mask(u + 2)
                        if not on_act(u):
                            dve.wait_ge(t_ready, BODY * b + u + 1)
                            if u >= RB:
                                dve.wait_ge(pv_ready, BODY * b + u - RB + 1)
                            copy_out(u, g, nc.vector.tensor_copy).then_inc(pT_dve, 1)

                bodies(dve, body)


def trunk(nc, d):
    pool_dma = {n: [nc.semaphore(f"{n}_pool_dma{j}").__enter__() for j in range(2)] for n in ("mod", "pa", "rt0", "rt1", "ex0", "ex1", "cb0", "cb1")}
    d["pool_dma"] = pool_dma.__getitem__
    modulation(nc, d)
    project_mlstm(nc, d)
    gate_rows(nc, d)
    mlstm(nc, d)
    for l in range(DEPTH):
        if l == 1:
            project_rope(nc, d, "kv")
            project_rope(nc, d, "q")
            attention(nc, d)
        after_mixer(nc, d, l)
        route(nc, d, l)
        experts(nc, d, l)
        combine(nc, d, l)


SCRATCH = {
    "mod": ((DEPTH, 6 * D), F32),
    "qkT": ((2 * AH, DQK, S), F32), "vo": ((S, 2 * AH * DV), F32), "gates": ((2, AH, S), F32),
    "rowbm": ((AH, S), F32), "colq": ((P, NT * NQT * AH), F32), "decay": ((P, 2 * AH * NT), F32),
    "y": ((S, D), F32), "x1": ((S, D), F32), "x2": ((S, D), F32), "lg": ((S, NR), F32),
    "slot_tok": ((NBP * P, 1), I32), "dest": ((P, 2 * NT), I32), "wt": ((P, 2 * NT), F32), "block_e": ((1, NBP), I32),
    "ybuf": ((NB * P, D), F32),
    "kT": ((G * HP, P, S), F32), "qT": ((G * HP, P, S), F32), "v": ((S, QW), F32), "o": ((G, S, HP * OW), F32),
}


_INS = ["x", "c", "positions", "ada_w", "ada_b", "ln_g", "ln_b", "a_w_in", "a_b_gate", "a_norm_g", "a_w_out", "b_w_kv", "b_w_q", "b_w_o",
        "moe_w_r1", "moe_b_r1", "moe_w_r2", "moe_b_r2", "moe_w_gate", "moe_w_up", "moe_w_down"]


def kernel(**inputs):
    import numpy as _np
    import concourse.bacc as _bacc
    from concourse import mybir as _mybir
    from concourse.bass_utils import run_bass_kernel_spmd as _run

    nc = _bacc.Bacc("TRN2", target_bir_lowering=False, num_devices=1)
    arrays, d = {}, {}
    for name in _INS + ["consts"]:
        a = constant_table() if name == "consts" else _np.ascontiguousarray(inputs[name])
        arrays[f"in_{name}_dram"] = a
        d[name] = nc.dram_tensor(f"in_{name}_dram", a.shape, _mybir.dt.from_np(a.dtype), kind="ExternalInput").ap()
    d["out"] = nc.dram_tensor("out_0_dram", (1, S, D), F32, kind="ExternalOutput").ap()
    for name, (shape, dtype) in SCRATCH.items():
        d[name] = nc.dram_tensor(f"{name}_scratch", shape, dtype, kind="Internal").ap()
    trunk(nc, d)
    r = _run(nc, [arrays], core_ids=[0])
    return r.results[0]["out_0_dram"]
```

```python
from contextlib import ExitStack

import numpy as np

import concourse.bass as bass
from concourse import mybir

F32 = mybir.dt.float32
F32R = mybir.dt.float32r
I32 = mybir.dt.int32
U32 = mybir.dt.uint32
ALU = mybir.AluOpType
ACT = mybir.ActivationFunctionType
AX_X = mybir.AxisListType.X
ds = bass.ds

P = 128
D = 1024
S = 2048
DEPTH = 2
NT = S // P
KD = D // P
ALPHA = (2.0 * DEPTH) ** 0.25
LN_EPS = 1e-5
AH, DQK, DV = 4, D // 8, D // 4
A_NORM_EPS = 1e-6
QK = AH * DQK
A_PROJ = 2 * QK + 2 * AH * DV + 2 * AH
WINDOWS, DILATIONS = (128, 512, 2048), (1, 4, 16)
G, BH, DH = 3, 8, 64
BW = BH * DH
QW = G * BW
HP = BH // 2
OW = 2 * (DH + 2)
MG, ME = 4, 8
NE = MG * ME
NR = MG + NE
HID = D // 4
NB = (2 * S + NE * (P - 1)) // P
NBP = 64
MACRO = 512
CH = 512
NEG = -1e30

C_ID, C_CAUSAL, C_BEFORE, C_ONES, C_BAND = 0, 128, 256, 384, 512
C_EXP, C_BLK, C_FREQ, C_SEL, C_TOK = 768, 800, 864, 896, 896 + AH * P
C_END = C_TOK + NT


def constant_table():
    t = np.zeros((P, C_END), np.float32)
    i = np.arange(P)
    t[:, C_ID:C_ID + P] = np.eye(P)
    t[:, C_CAUSAL:C_CAUSAL + P] = np.where(i[:, None] <= i[None, :], 0.0, NEG)
    t[:, C_BEFORE:C_BEFORE + P] = i[:, None] < i[None, :]
    t[:, C_ONES:C_ONES + P] = 1.0
    kj = np.arange(2 * P)
    t[:, C_BAND:C_BAND + 2 * P] = np.where((kj >= i[:, None]) & (kj <= i[:, None] + P), 0.0, NEG)
    t[:, C_EXP:C_EXP + NE] = np.arange(NE)
    t[:, C_BLK:C_BLK + NBP] = np.arange(NBP) * P
    t[:, C_FREQ:C_FREQ + DH // 2] = np.power(10000.0, -np.arange(DH // 2) * 2.0 / DH)
    for h in range(AH):
        t[h, C_SEL + h * P:C_SEL + (h + 1) * P] = 1.0
    t[:, C_TOK:C_TOK + NT] = i[:, None] + P * np.arange(NT)[None, :]
    return t


def settle(eng, waited):
    eng.sem_inc(waited, 1)


class Phase:

    def __init__(self, nc, name):
        self.nc, self.name, self.stack, self.sems = nc, name, ExitStack(), []

    def sb(self, name, shape, dtype=F32):
        return self.stack.enter_context(self.nc.sbuf_tensor(f"{self.name}_{name}", shape, dtype))

    def ps(self, name, shape, dtype=F32):
        return self.stack.enter_context(self.nc.psum_tensor(f"{self.name}_{name}", shape, dtype))

    def sem(self, name):
        s = self.stack.enter_context(self.nc.semaphore(f"{self.name}_{name}"))
        self.sems.append(s.num)
        return s

    def __enter__(self):
        self.stack.__enter__()
        return self

    def __exit__(self, *e):
        if e[0] is None:
            self.nc.all_engine_barrier(sems_to_clear=range(min(self.sems), max(self.sems) + 1))
        return self.stack.__exit__(*e)


TWO_PI = 2.0 * np.pi
PI_HI = 6.28125
PI_MID = float(np.round((TWO_PI - PI_HI) * 2 ** 20) / 2 ** 20)
PI_LO = float(TWO_PI - PI_HI - PI_MID)
ROUND = 1.5 * 2.0 ** 23


class RopeTables:

    def __init__(self, nc, d, ph):
        HH = DH // 2
        self.nc, self.d = nc, d
        self.pos, self.posf = ph.sb("pos", [P, NT], I32), ph.sb("posf", [P, NT])
        self.freq = ph.sb("freq", [P, HH])
        self.ang = ph.sb("ang", [P, NT, HH])
        self.turns = ph.sb("turns", [P, 2, NT, HH])
        self.cs = ph.sb("cs", [P, 2, NT, HH])
        self.p_in, self.r_ready, self.cs_ready, self.cs_stored = ph.sem("p_in"), ph.sem("r_ready"), ph.sem("cs_ready"), ph.sem("cs_stored")

    def load(self, sp):
        d = self.d
        sp.dma_start(self.pos[:, :], d["positions"].rearrange("b (c p) -> p (b c)", p=P), allow_slow_non_contiguous=True).then_inc(self.p_in, 16)
        sp.dma_start(self.freq[:, :], d["consts"][:, C_FREQ:C_FREQ + DH // 2]).then_inc(self.p_in, 16)

    def finish(self, sp):
        sp.wait_ge(self.cs_ready, 1)
        sp.dma_start(self.d["cs"], self.cs[:, :, :, :].rearrange("p a c e -> p (a c e)")).then_inc(self.cs_stored, 16)
        sp.wait_ge(self.cs_stored, 16)

    def sines(self, act):
        act.wait_ge(self.r_ready, 1)
        self.nc.scalar.activation(self.cs[:, :, :, :], self.turns[:, :, :, :], ACT.Sin).then_inc(self.cs_ready, 1)

    def angles(self, dve):
        v, ang, turns, rem = self.nc.vector, self.ang, self.turns, self.cs
        dve.wait_ge(self.p_in, 32)
        v.tensor_copy(self.posf[:, :], self.pos[:, :])
        dve.drain()
        for c in range(NT):
            v.tensor_scalar(ang[:, c, :], self.freq[:, :], self.posf[:, c:c + 1], None, ALU.mult)
        dve.drain()
        v.tensor_scalar(turns[:, 0, :, :], ang[:, :, :], 1.0 / TWO_PI, None, ALU.mult)
        v.tensor_scalar(turns[:, 1, :, :], ang[:, :, :], 1.0 / TWO_PI, 0.25, ALU.mult, ALU.add)
        dve.drain()
        v.tensor_scalar(turns[:, :, :, :], turns[:, :, :, :], ROUND, None, ALU.add)
        dve.drain()
        v.tensor_scalar(turns[:, :, :, :], turns[:, :, :, :], ROUND, None, ALU.subtract)
        dve.drain()
        for n, piece in enumerate((PI_HI, PI_MID, PI_LO)):
            for j in range(2):
                v.scalar_tensor_tensor(rem[:, j, :, :], turns[:, j, :, :], -piece, ang[:, :, :] if n == 0 else rem[:, j, :, :], ALU.mult, ALU.add)
            dve.drain()
        v.tensor_scalar(rem[:, 1, :, :], rem[:, 1, :, :], np.pi / 2, None, ALU.add)
        dve.drain()
        lim = 3.1415925
        v.tensor_scalar(turns[:, :, :, :], rem[:, :, :, :], lim, -lim, ALU.min, ALU.max)
        dve.drain().then_inc(self.r_ready, 1)


def modulation(nc, d):
    NCH = 6 * D // CH
    WB, KP = 4, KD // 2
    with Phase(nc, "mod") as ph:
        c_sb = ph.sb("c", [P, KD])
        cond = ph.sb("cond", [P, KD])
        ones = ph.sb("ones", [P, 1])
        w = ph.sb("w", [P, WB, KD, CH])
        b = ph.sb("b", [1, WB, CH])
        part = ph.sb("part", [P, 2, CH])
        row = ph.sb("row", [1, 2, CH])
        acc = [ph.ps(f"acc{j}", [P, CH]) for j in range(2)]
        c_in, cond_ready, part_ready = ph.sem("c_in"), ph.sem("cond_ready"), ph.sem("part_ready")
        w_in = [ph.sem(f"w_in{j}") for j in range(WB)]
        acc_ready, row_ready = ph.sem("acc_ready"), ph.sem("row_ready")
        stored, waited = [ph.sem(f"stored{j}") for j in range(2)], ph.sem("waited")
        w_dram = d["ada_w"].rearrange("l (p k) n -> l p k n", k=KD)
        tables = RopeTables(nc, d, ph)

        def chunks(eng, step):
            for l in range(DEPTH):
                with eng.Fori(0, NCH // WB) as i:
                    for j in range(WB):
                        step(l, i * WB + j, i * WB + (l * NCH + j), j)

        with nc.Block() as block:
            @block.sync
            def _(sp):
                sp.dma_start(c_sb[:, :], d["c"].rearrange("b (p k) -> (b p) k", k=KD)).then_inc(c_in, 16)
                tables.load(sp)
                sp.sem_inc(row_ready, WB)

                def step(l, m, n, j):
                    sp.wait_ge(row_ready, n + 1)
                    sp.dma_start(w[:, j, :, :], w_dram[l, :, :, ds(m * CH, CH)]).then_inc(w_in[j], 16)
                    sp.dma_start(b[:, j, :], d["ada_b"][l:l + 1, ds(m * CH, CH)]).then_inc(w_in[j], 16)

                chunks(sp, step)
                tables.finish(sp)

            @block.scalar
            def _(act):
                act.wait_ge(c_in, 16)
                nc.scalar.activation(cond[:, :], c_sb[:, :], ACT.Silu).then_inc(cond_ready, 1)
                tables.sines(act)

                def step(l, m, n, j):
                    act.wait_ge(row_ready, n + (WB + 1))
                    settle(act, waited)
                    act.dma_start(d["mod"][l:l + 1, ds(m * CH, CH)], row[:, j % 2, :]).then_inc(stored[j % 2], 16)

                chunks(act, step)
                for j in range(2):
                    act.wait_ge(stored[j], 16 * DEPTH * NCH // 2 + 16)

            @block.tensor
            def _(pe):
                pe.wait_ge(cond_ready, 1)

                def step(l, m, n, j):
                    pe.wait_ge(w_in[j], (n - j) * (32 // WB) + 32)
                    pe.wait_ge(row_ready, n + (WB - 1))
                    out = acc[j % 2][0:1, :]
                    for k in range(KP):
                        nc.tensor.matmul(out, cond[:, k:k + 1], w[:, j, k, :], start=(k == 0), stop=False)
                    pe.wait_ge(part_ready, n + 2)
                    nc.tensor.matmul(out, ones[:, :], part[:, j % 2, :], start=False, stop=True).then_inc(acc_ready, 1)

                chunks(pe, step)

            @block.vector
            def _(dve):
                for j in range(2):
                    dve.sem_inc(stored[j], 16)
                nc.vector.memset(ones[:, :], 1.0)
                dve.drain().then_inc(part_ready, 1)
                tables.angles(dve)
                dve.wait_ge(cond_ready, 1)

                def step(l, m, n, j):
                    dve.wait_ge(w_in[j], (n - j) * (32 // WB) + 32)
                    for k in range(KP, KD):
                        last, out = k == KD - 1, part[:, j % 2, :]
                        if k == KP:
                            ins = nc.vector.tensor_scalar(out, w[:, j, k, :], cond[:, k:k + 1], None, ALU.mult)
                        else:
                            ins = nc.vector.scalar_tensor_tensor(out, w[:, j, k, :], cond[:, k:k + 1], out, ALU.mult, ALU.add)
                        if last:
                            ins.then_inc(part_ready, 1)
                        else:
                            dve.drain()
                    dve.wait_ge(acc_ready, n + 1)
                    dve.wait_ge(stored[j % 2], 8 * (n - j % 2) + 16)
                    nc.vector.tensor_tensor(row[:, j % 2, :], acc[j % 2][0:1, :], b[:, j, :], ALU.add).then_inc(row_ready, 1)

                chunks(dve, step)


def load_mod_columns(eng, nc, d, cols, l, kinds, sem):
    for j, kind in enumerate(kinds):
        eng.dma_start(cols[:, j, :], d["mod"][l, kind * D:(kind + 1) * D].rearrange("(p k) -> p k", k=KD)).then_inc(sem, 16)


def project_qk(nc, d):
    NM = S // MACRO
    NGT = 2 * AH
    WC = 2 * QK + NGT
    RING = AH
    with Phase(nc, "pqk") as ph:
        wst = ph.sb("wst", [P, KD, WC])
        ws = ph.sb("ws", [P, 2, KD, WC], F32R)
        bias = ph.sb("bias", [NGT, 1])
        full = ph.sb("full", [P, KD, MACRO])
        hT = ph.sb("hT", [P, 2, 2, KD, MACRO], F32R)
        out = ph.sb("out", [P, 2 * AH, MACRO])
        gates = ph.sb("gates", [NGT, MACRO])
        mm = [ph.ps(f"mm{i}", [P, MACRO]) for i in range(RING)]
        gt = ph.ps("gt", [P, MACRO])
        whi_ready, wlo_ready, mm_ready, q_ev, k_ev, g_ev, g_done = (
            ph.sem(s) for s in ("whi_ready", "wlo_ready", "mm_ready", "q_ev", "k_ev", "g_ev", "g_done"))
        b_in, st_q, st_k, st_g, waited = (ph.sem(s) for s in ("b_in", "st_q", "st_k", "st_g", "waited"))
        w_in = [ph.sem(f"w_in{k}") for k in range(KD)]
        h_in, hi_ready, lo_ready = ph.sem("h_in"), ph.sem("hi_ready"), ph.sem("lo_ready")
        w_dram = d["a_w_in"][0].rearrange("(p k) n -> p k n", k=KD)

        def macros(eng, step):
            step(0, 0)
            with eng.Fori(0, NM // 2 - 1) as i:
                for j in range(2):
                    step(i * 2 + j + 1, 1 - j)
            step(NM - 1, 1)

        with nc.Block() as block:
            @block.sync
            def _(sp):
                for k in range(KD):
                    sp.dma_start(wst[:, k, 0:2 * QK], w_dram[:, k, 0:2 * QK]).then_inc(w_in[k], 16)
                    sp.dma_start(wst[:, k, 2 * QK:WC], w_dram[:, k, A_PROJ - NGT:A_PROJ]).then_inc(w_in[k], 16)
                sp.dma_start(bias[:, :], d["a_b_gate"][0].rearrange("(h o) -> h o", o=1)).then_inc(b_in, 16)

                def store(m, j):
                    tok = ds(m * MACRO, MACRO)
                    sp.wait_ge(q_ev, AH * m + AH)
                    settle(sp, waited)
                    sp.dma_start(d["qkT"][0:AH, :, tok].rearrange("h p t -> p h t"), out[:, 0:AH, :]).then_inc(st_q, 16)
                    sp.wait_ge(k_ev, AH * m + AH)
                    settle(sp, waited)
                    sp.dma_start(d["qkT"][AH:2 * AH, :, tok].rearrange("h p t -> p h t"), out[:, AH:2 * AH, :]).then_inc(st_k, 16)
                    sp.wait_ge(g_ev, m + 1)
                    settle(sp, waited)
                    sp.dma_start(d["gates"].rearrange("g h t -> (g h) t")[:, tok], gates[:, :]).then_inc(st_g, 16)

                macros(sp, store)
                for s in (st_q, st_k, st_g):
                    sp.wait_ge(s, 16 * NM)

            @block.tensor
            def _(pe):
                def product(out_bank, cols, j, first=False):
                    for k in range(KD):
                        if first:
                            pe.wait_ge(wlo_ready, k + 1)
                        for n, (a, b) in enumerate(((0, 0), (0, 1), (1, 0))):
                            ins = nc.tensor.matmul(out_bank, ws[:, b, k, cols], hT[:, j, a, k, :], start=(k == 0 and n == 0), stop=(k == KD - 1 and n == 2))
                    return ins

                def step(m, j):
                    pe.wait_ge(hi_ready, m + 1)
                    pe.wait_ge(lo_ready, m + 1)
                    for h in range(2 * AH):
                        if h < AH:
                            wait_from(pe, k_ev, AH * (m - 1) + h + 1)
                        else:
                            pe.wait_ge(q_ev, AH * m + h - AH + 1)
                        product(mm[h % RING][:, :], slice(h * P, (h + 1) * P), j, isinstance(m, int) and m + h == 0).then_inc(mm_ready, 1)
                    wait_from(pe, g_ev, m)
                    product(gt[0:NGT, :], slice(2 * QK, WC), j).then_inc(g_done, 1)

                macros(pe, step)

            @block.scalar
            def _(act):
                def load(m):
                    act.dma_start(full[:, :, :], d["hT"][:, :, ds(m * MACRO, MACRO)].rearrange("k p t -> p k t")).then_inc(h_in, 16)

                def rows_hi(m, j):
                    act.wait_ge(h_in, 16 * m + 16)
                    wait_from(act, g_done, m - 1)
                    nc.scalar.activation(hT[:, j, 0, :, :], full[:, :, :], ACT.Copy).then_inc(hi_ready, 1)

                load(0)
                for k in range(KD):
                    act.wait_ge(w_in[k], 32)
                    nc.scalar.activation(ws[:, 0, k, :], wst[:, k, :], ACT.Copy).then_inc(whi_ready, 1)

                rows_hi(0, 0)

                def step(m, j):
                    if not (isinstance(m, int) and m == NM - 1):
                        act.wait_ge(lo_ready, m + 1)
                        settle(act, waited)
                        load(m + 1)
                        rows_hi(m + 1, 1 - j)
                    for h in range(AH):
                        act.wait_ge(mm_ready, 2 * AH * m + h + 1)
                        if h == 0:
                            wait_from(act, st_q, 16 * m)
                        nc.scalar.activation(out[:, h, :], mm[h][:, :], ACT.Copy).then_inc(q_ev, 1)

                macros(act, step)

            @block.vector
            def _(dve):
                for k in range(KD):
                    dve.wait_ge(whi_ready, k + 1)
                    nc.vector.tensor_tensor(ws[:, 1, k, :], wst[:, k, :], ws[:, 0, k, :], ALU.subtract).then_inc(wlo_ready, 1)
                dve.wait_ge(b_in, 16)

                def rows_lo(m, j):
                    dve.wait_ge(hi_ready, m + 1)
                    nc.vector.tensor_tensor(hT[:, j, 1, :, :], full[:, :, :], hT[:, j, 0, :, :], ALU.subtract).then_inc(lo_ready, 1)

                rows_lo(0, 0)

                def step(m, j):
                    if not (isinstance(m, int) and m == NM - 1):
                        rows_lo(m + 1, 1 - j)
                    for h in range(AH):
                        dve.wait_ge(mm_ready, 2 * AH * m + AH + h + 1)
                        if h == 0:
                            wait_from(dve, st_k, 16 * m)
                        nc.vector.tensor_scalar(out[:, AH + h, :], mm[h][:, :], DQK ** -0.5, None, ALU.mult).then_inc(k_ev, 1)
                    dve.wait_ge(g_done, m + 1)
                    wait_from(dve, st_g, 16 * m)
                    nc.vector.tensor_scalar(gates[:, :], gt[0:NGT, :], bias[:, 0:1], None, ALU.add).then_inc(g_ev, 1)

                macros(dve, step)


QU, QEM, QWS = range(3)
NQT = 3


def gate_rows(nc, d):
    with Phase(nc, "gr") as ph:
        raw = ph.sb("raw", [AH, 2, S])
        t0 = ph.sb("t0", [AH, S])
        t1 = ph.sb("t1", [AH, S])
        lf = ph.sb("lf", [AH, S])
        keep = ph.sb("keep", [AH, S])
        b = ph.sb("b", [AH, S])
        m = ph.sb("m", [AH, S])
        rowbm = ph.sb("rowbm", [AH, S])
        u = ph.sb("u", [AH, S])
        small = ph.sb("small", [AH, 4, NT])
        quant = ph.sb("quant", [P, S])
        ident = ph.sb("ident", [P, P])
        sel = ph.sb("sel", [AH, AH, P])
        colq = ph.sb("colq", [P, NT, NQT, AH])
        decay = ph.sb("decay", [P, 2, AH, NT])
        tp = [ph.ps(f"tp{j}", [P, 4, P]) for j in range(4)]
        dc = ph.ps("dc", [P, 2, AH, NT])
        g_in, c_in, out_done = ph.sem("g_in"), ph.sem("c_in"), ph.sem("out_done")
        dve_done, act_done, pe_done, rows_ready = ph.sem("dve_done"), ph.sem("act_done"), ph.sem("pe_done"), ph.sem("rows_ready")
        cols_done = ph.sem("cols_done")

        def chunks(a):
            return a.rearrange("h (c t) -> h c t", t=P)

        with nc.Block() as block:
            @block.sync
            def _(sp):
                sp.dma_start(raw[:, :, :], d["gates"].rearrange("g h t -> h g t")).then_inc(g_in, 16)
                sp.dma_start(ident[:, :], d["consts"][:, C_ID:C_ID + P]).then_inc(c_in, 16)
                sp.dma_start(sel[:, :, :], d["consts"][0:AH, C_SEL:C_SEL + AH * P].rearrange("k (h p) -> k h p", h=AH)).then_inc(c_in, 16)
                sp.wait_ge(rows_ready, 1)
                sp.dma_start(d["rowbm"], rowbm[:, :]).then_inc(out_done, 16)
                sp.wait_ge(cols_done, 1)
                sp.dma_start(d["colq"], colq[:, :, :, :].rearrange("p c q h -> p (c q h)")).then_inc(out_done, 16)
                sp.dma_start(d["decay"], decay[:, :, :, :].rearrange("p a h c -> p (a h c)")).then_inc(out_done, 16)
                sp.wait_ge(out_done, 48)

            @block.scalar
            def _(act):
                act.wait_ge(g_in, 16)
                nc.scalar.activation(t0[:, :], raw[:, 1, :], ACT.Abs)
                act.drain()
                nc.scalar.activation(t0[:, :], t0[:, :], ACT.Exp, scale=-1.0)
                act.drain()
                nc.scalar.activation(t1[:, :], t0[:, :], ACT.Ln, bias=1.0).then_inc(act_done, 1)
                act.wait_ge(dve_done, 1)
                nc.scalar.activation(quant[0:AH, :], u[:, :], ACT.Copy)
                nc.scalar.activation(quant[32:32 + AH, :], m[:, :], ACT.Exp, scale=-1.0)
                act.wait_ge(dve_done, 2)
                nc.scalar.activation(quant[64:64 + AH, :], t1[:, :], ACT.Exp)
                nc.scalar.activation(small[:, 3, :], small[:, 1, :], ACT.Exp)
                act.drain().then_inc(rows_ready, 1)

            @block.vector
            def _(dve):
                nc.vector.memset(quant[:, :], 0.0)
                nc.vector.memset(keep[:, :], 1.0)
                dve.drain()
                nc.vector.memset(chunks(keep[:, :])[:, :, 0:1], 0.0)
                dve.wait_ge(g_in, 16)
                nc.vector.tensor_scalar(lf[:, :], raw[:, 1, :], 0.0, None, ALU.min)
                dve.drain()
                dve.wait_ge(act_done, 1)
                nc.vector.tensor_tensor(lf[:, :], lf[:, :], t1[:, :], ALU.subtract)
                dve.drain()
                nc.vector.tensor_tensor_scan(b[:, :], keep[:, :], lf[:, :], 0.0, ALU.mult, ALU.add)
                nc.vector.tensor_tensor_scan(m[:, :], lf[:, :], raw[:, 0, :], 0.0, ALU.add, ALU.max)
                nc.vector.memset(small[:, 0, 0:1], 0.0)
                dve.drain()
                nc.vector.tensor_tensor(u[:, :], raw[:, 0, :], b[:, :], ALU.subtract)
                nc.vector.tensor_tensor(rowbm[:, :], b[:, :], m[:, :], ALU.subtract)
                nc.vector.tensor_copy(small[:, 0, 1:NT], chunks(m[:, :])[:, 0:NT - 1, P - 1])
                dve.drain().then_inc(dve_done, 1)
                bm_last = chunks(rowbm[:, :])[:, :, P - 1:P]
                nc.vector.tensor_tensor(chunks(t0[:, :]), chunks(rowbm[:, :]), small[:, 0, :].rearrange("h (c o) -> h c o", o=1).to_broadcast([AH, NT, P]), ALU.add)
                nc.vector.tensor_tensor(chunks(t1[:, :]), chunks(u[:, :]), bm_last.to_broadcast([AH, NT, P]), ALU.add)
                dve.drain()
                nc.vector.tensor_copy(small[:, 1, :], chunks(t0[:, :])[:, :, P - 1])
                dve.drain().then_inc(dve_done, 1)
                for c in range(NT):
                    dve.wait_ge(pe_done, c + 1)
                    q = tp[c % 4][:, 0, :].rearrange("p (q h) -> p q h", q=4)[:, 0:NQT, 0:AH]
                    nc.vector.tensor_copy(colq[:, c, :, :], q).then_inc(dve_done, 1)
                dve.wait_ge(pe_done, NT + 1)
                nc.vector.tensor_copy(decay[:, :, :, :], dc[:, :, :, :])
                dve.drain().then_inc(cols_done, 1)

            @block.tensor
            def _(pe):
                pe.wait_ge(c_in, 32)
                pe.wait_ge(rows_ready, 1)
                for c in range(NT):
                    if c >= 4:
                        pe.wait_ge(dve_done, 2 + c - 3)
                    nc.tensor.transpose(tp[c % 4][:, 0, :], quant[:, c * P:(c + 1) * P], ident[:, :]).then_inc(pe_done, 1)
                for h in range(AH):
                    nc.tensor.matmul(dc[:, 0, h, :], sel[:, h, :], small[:, 0, :], start=True, stop=True)
                    ins = nc.tensor.matmul(dc[:, 1, h, :], sel[:, h, :], small[:, 3, :], start=True, stop=True)
                ins.then_inc(pe_done, 1)


def wait_from(eng, sem, count):
    if not (isinstance(count, int) and count <= 0):
        eng.wait_ge(sem, count)


def skewed(eng, stages):
    most, least = max(lead for _, lead in stages), min(lead for _, lead in stages)
    first = 2 - least + (least % 2)
    last = NT - most - (NT - most - first) % 2

    def step(i, parity, whole):
        for stage, lead in stages:
            if whole or 0 <= i + lead < NT:
                stage(i + lead, (parity + lead) % 2)

    for i in range(-most, first):
        step(i, i % 2, False)
    with eng.Fori(0, (last - first) // 2) as n:
        for j in range(2):
            step(n * 2 + first + j, j, True)
    for i in range(last, NT - least):
        step(i, i % 2, False)


def mlstm(nc, d):
    with Phase(nc, "ml") as ph:
        q = ph.sb("q", [P, 2, AH, P])
        kT = ph.sb("kT", [P, 2, AH, P])
        v = ph.sb("v", [P, 2, AH, DV])
        og = ph.sb("og", [P, 2, D])
        y = ph.sb("y", [P, 2, D])
        rowbm = ph.sb("rowbm", [AH, S])
        colq = ph.sb("colq", [P, NT, NQT, AH])
        decay = ph.sb("decay", [P, 2, AH, NT])
        cq = ph.sb("cq", [P, 2, NQT, AH])
        dk = ph.sb("dk", [P, 2, 2, AH])
        sel = ph.sb("sel", [AH, AH, P])
        ident = ph.sb("ident", [P, P])
        causal = ph.sb("causal", [P, P])
        ng = ph.sb("ng", [P, D])
        ones = ph.sb("ones", [P, 1])
        dw = ph.sb("dw", [P, AH, P])
        iwb = ph.sb("iwb", [P, AH, P])
        sc = ph.sb("sc", [P, 2, AH, P])
        qs = ph.sb("qs", [P, 2, AH, P])
        kw = ph.sb("kw", [P, 2, AH, P])
        C = ph.sb("C", [P, AH, DV])
        n = ph.sb("n", [P, AH])
        den = ph.sb("den", [P, AH])
        rden = ph.sb("rden", [P, 2, AH])
        ht = ph.sb("ht", [P, 2, AH, DV])
        stats = ph.sb("stats", [P, AH, 6])
        mv = ph.sb("mv", [P, 2, AH, 2])
        std = ph.sb("std", [P, 2, 3, AH])
        bS, bR, bK, bD = ph.ps("bS", [P, AH, P]), ph.ps("bR", [P, AH, P]), ph.ps("bK", [P, AH, P]), ph.ps("bD", [P, CH])
        bN = [ph.ps(f"bN{i}", [P, 2, DV]) for i in range(2)]
        bU = [ph.ps(f"bU{i}", [P, 2, DV]) for i in range(2)]
        c_in, k_ready = ph.sem("c_in"), ph.sem("k_ready")
        qk_in = [ph.sem(f"qk_in{j}") for j in range(2)]
        v_in = [ph.sem(f"v_in{j}") for j in range(2)]
        og_in = [ph.sem(f"og_in{j}") for j in range(2)]
        stored = [ph.sem(f"stored{j}") for j in range(2)]
        scores_ready, dwin_ready, dw_ready, iw_ready, kw_ready = (ph.sem(x) for x in ("scores_ready", "dwin_ready", "dw_ready", "iw_ready", "kw_ready"))
        sc_ready, num_ready, upd_ready, state_ready = (ph.sem(x) for x in ("sc_ready", "num_ready", "upd_ready", "state_ready"))
        rden_ready, ht_ready, hn_ready, ng_done, y_ready, waited = (ph.sem(x) for x in ("rden_ready", "ht_ready", "hn_ready", "ng_done", "y_ready", "waited"))
        cq_ready, v_ready, std_ready = ph.sem("cq_ready"), ph.sem("v_ready"), ph.sem("std_ready")

        with nc.Block() as block:
            @block.sync
            def _(sp):
                def load_qk(c, j):
                    wait_from(sp, sc_ready, c - 1)
                    settle(sp, waited)
                    tok = ds(c * P, P)
                    sp.dma_start(q[:, j, :, :], d["qkT"][0:AH, :, tok].rearrange("h p t -> p h t")).then_inc(qk_in[j], 16)
                    sp.dma_start(kT[:, j, :, :], d["qkT"][AH:2 * AH, :, tok].rearrange("h p t -> p h t")).then_inc(qk_in[j], 16)

                def load_v(c, j):
                    wait_from(sp, upd_ready, c - 1)
                    settle(sp, waited)
                    sp.dma_start(v[:, j, :, :].rearrange("p h e -> p (h e)"), d["vo"][ds(c * P, P), 0:D]).then_inc(v_in[j], 16)

                def load_og(c, j):
                    wait_from(sp, y_ready, c - 1)
                    settle(sp, waited)
                    sp.dma_start(og[:, j, :], d["vo"][ds(c * P, P), D:2 * D]).then_inc(og_in[j], 16)

                def store(c, j):
                    sp.wait_ge(y_ready, c + 1)
                    settle(sp, waited)
                    sp.dma_start(d["y"][ds(c * P, P), :], y[:, j, :]).then_inc(stored[j], 16)

                sp.dma_start(rowbm[:, :], d["rowbm"]).then_inc(c_in, 16)
                sp.dma_start(colq[:, :, :, :].rearrange("p c q h -> p (c q h)"), d["colq"]).then_inc(c_in, 16)
                sp.dma_start(decay[:, :, :, :].rearrange("p a h c -> p (a h c)"), d["decay"]).then_inc(c_in, 16)
                sp.dma_start(sel[:, :, :], d["consts"][0:AH, C_SEL:C_SEL + AH * P].rearrange("k (h p) -> k h p", h=AH)).then_inc(c_in, 16)
                sp.dma_start(ident[:, :], d["consts"][:, C_ID:C_ID + P]).then_inc(c_in, 16)
                sp.dma_start(causal[:, :], d["consts"][:, C_CAUSAL:C_CAUSAL + P]).then_inc(c_in, 16)
                sp.dma_start(ng[:, :], d["a_norm_g"][0:1, :].to_broadcast([P, D])).then_inc(c_in, 16)
                skewed(sp, [(load_v, 2), (load_qk, 3), (load_og, 0), (store, -2)])
                for j in range(2):
                    sp.wait_ge(stored[j], 16 * NT // 2)

            @block.tensor
            def _(pe):
                pe.wait_ge(c_in, 16 * 7)
                pe.wait_ge(k_ready, 1)

                def scores(c, j):
                    wait_from(pe, sc_ready, c)
                    wait_from(pe, iw_ready, c)
                    wait_from(pe, kw_ready, c)
                    pe.wait_ge(qk_in[j], 16 * (c - j) + 32)
                    for h in range(AH):
                        ins = nc.tensor.matmul(bR[:, h, :], sel[:, h, :], rowbm[:, ds(c * P, P)], start=True, stop=True)
                    for h in range(AH):
                        nc.tensor.transpose(bK[:, h, :], kT[:, j, h, :], ident[:, :])
                    for h in range(AH):
                        ins = nc.tensor.matmul(bS[:, h, :], kT[:, j, h, :], q[:, j, h, :], start=True, stop=True)
                    ins.then_inc(scores_ready, 1)

                def numerators(c, j):
                    pe.wait_ge(sc_ready, c + 1)
                    pe.wait_ge(kw_ready, c + 1)
                    pe.wait_ge(v_in[j], 8 * (c - j) + 16)
                    wait_from(pe, state_ready, c)
                    wait_from(pe, ht_ready, c)
                    for h in range(AH):
                        nc.tensor.matmul(bN[h // 2][:, h % 2, :], sc[:, j, h, :], v[:, j, h, :], start=True, stop=False)
                        nc.tensor.matmul(bN[h // 2][:, h % 2, :], qs[:, j, h, :], C[:, h, :], start=False, stop=True)
                        nc.tensor.matmul(bD[:, h:h + 1], sc[:, j, h, :], ones[:, :], start=True, stop=False)
                        ins = nc.tensor.matmul(bD[:, h:h + 1], qs[:, j, h, :], n[:, h:h + 1], start=False, stop=True)
                    for h in range(AH):
                        ins = nc.tensor.matmul(bD[:, AH + h:AH + h + 1], kw[:, j, h, :], ones[:, :], start=True, stop=True)
                    ins.then_inc(num_ready, 1)
                    for h in range(AH):
                        ins = nc.tensor.matmul(bU[h // 2][:, h % 2, :], kw[:, j, h, :], v[:, j, h, :], start=True, stop=True)
                    ins.then_inc(upd_ready, 1)

                skewed(pe, [(scores, 1), (numerators, 0)])

            @block.scalar
            def _(act):
                act.wait_ge(c_in, 16 * 7)

                def weights(c, j):
                    act.wait_ge(cq_ready, c + 1)
                    act.wait_ge(scores_ready, c + 1)
                    wait_from(act, sc_ready, c)
                    for h in range(AH):
                        ins = nc.scalar.activation(iwb[:, h, :], bR[:, h, :], ACT.Exp, bias=dk[:, j, 0, h:h + 1])
                    ins.then_inc(iw_ready, 1)
                    wait_from(act, upd_ready, c - 1)
                    for h in range(AH):
                        ins = nc.scalar.activation(kw[:, j, h, :], bK[:, h, :], ACT.Copy, scale=cq[:, j, QWS, h:h + 1])
                    ins.then_inc(kw_ready, 1)

                def own_weights(c, j):
                    act.wait_ge(dwin_ready, c + 1)
                    nc.scalar.activation(dw[:, :, :], dw[:, :, :], ACT.Exp).then_inc(dw_ready, 1)

                def root(c, j):
                    act.wait_ge(v_ready, c + 1)
                    nc.scalar.activation(std[:, j, 1, :], std[:, j, 0, :], ACT.Sqrt).then_inc(std_ready, 1)

                def divide(c, j):
                    act.wait_ge(rden_ready, c + 1)
                    wait_from(act, ng_done, c - 1)
                    for h in range(AH):
                        ins = nc.scalar.activation(ht[:, j, h, :], bN[h // 2][:, h % 2, :], ACT.Copy, scale=rden[:, j, h:h + 1])
                    ins.then_inc(ht_ready, 1)

                skewed(act, [(weights, 1), (own_weights, 1), (divide, 0), (root, -1)])

            @block.vector
            def _(dve):
                nc.vector.memset(C[:, :, :], 0.0)
                nc.vector.memset(n[:, :], 0.0)
                nc.vector.memset(ones[:, :], 1.0)
                dve.drain().then_inc(k_ready, 1)
                dve.wait_ge(c_in, 16 * 7)

                def state(c, j):
                    dve.wait_ge(upd_ready, c + 1)
                    for h in range(AH):
                        ins = nc.vector.scalar_tensor_tensor(C[:, h, :], C[:, h, :], dk[:, j, 1, h:h + 1], bU[h // 2][:, h % 2, :], ALU.mult, ALU.add)
                    ins.then_inc(state_ready, 1)

                def columns(c, j):
                    wait_from(dve, state_ready, c - 1)
                    nc.vector.tensor_copy(cq[:, j, :, :], colq[:, ds(c, 1), :, :])
                    nc.vector.tensor_copy(dk[:, j, :, :], decay[:, :, :, ds(c, 1)])
                    dve.drain().then_inc(cq_ready, 1)

                def own_logs(c, j):
                    dve.wait_ge(iw_ready, c + 1)
                    for h in range(AH):
                        ins = nc.vector.scalar_tensor_tensor(dw[:, h, :], bR[:, h, :], cq[:, j, QU, h:h + 1], causal[:, :], ALU.add, ALU.add)
                    ins.then_inc(dwin_ready, 1)
                    wait_from(dve, num_ready, c - 1)
                    nc.vector.tensor_tensor(qs[:, j, :, :], q[:, j, :, :], iwb[:, :, :], ALU.mult)

                def weigh(c, j):
                    dve.wait_ge(dw_ready, c + 1)
                    nc.vector.tensor_tensor(sc[:, j, :, :], bS[:, :, :], dw[:, :, :], ALU.mult).then_inc(sc_ready, 1)

                def denominators(c, j):
                    dve.wait_ge(num_ready, c + 1)
                    nc.vector.scalar_tensor_tensor(den[:, :], bD[:, 0:AH], -1.0, cq[:, j, QEM, :], ALU.mult, ALU.max)
                    nc.vector.tensor_tensor(n[:, :], n[:, :], dk[:, j, 1, :], ALU.mult)
                    dve.drain()
                    nc.vector.tensor_tensor(den[:, :], bD[:, 0:AH], den[:, :], ALU.max)
                    dve.drain()
                    nc.vector.reciprocal(rden[:, j, :], den[:, :]).then_inc(rden_ready, 1)
                    nc.vector.tensor_tensor(n[:, :], n[:, :], bD[:, AH:2 * AH], ALU.add)

                def statistics(c, j):
                    dve.wait_ge(ht_ready, c + 1)
                    for h in range(AH):
                        nc.vector.bn_stats(stats[:, h, :], ht[:, j, h, :])
                    dve.drain()
                    for h in range(AH):
                        nc.vector.bn_aggr(mv[:, j, h, :], stats[:, h, :])
                    dve.drain()
                    nc.vector.tensor_scalar(std[:, j, 0, :], mv[:, j, :, 1], A_NORM_EPS, None, ALU.add).then_inc(v_ready, 1)

                def normalise(c, j):
                    dve.wait_ge(std_ready, c + 1)
                    nc.vector.reciprocal(std[:, j, 2, :], std[:, j, 1, :])
                    dve.drain()
                    for h in range(AH):
                        ins = nc.vector.tensor_scalar(ht[:, j, h, :], ht[:, j, h, :], mv[:, j, h, 0:1], std[:, j, 2, h:h + 1], ALU.subtract, ALU.mult)
                    ins.then_inc(hn_ready, 1)

                def gate(c, j):
                    dve.wait_ge(og_in[j], 8 * (c - j) + 16)
                    dve.wait_ge(ng_done, c + 1)
                    nc.vector.tensor_tensor(y[:, j, :], y[:, j, :], og[:, j, :], ALU.mult).then_inc(y_ready, 1)

                skewed(dve, [(statistics, -1), (own_logs, 1), (gate, -2), (weigh, 1), (denominators, 0), (state, 0), (columns, 2), (normalise, -1)])

            @block.gpsimd
            def _(pool):
                pool.wait_ge(c_in, 16 * 7)

                def norm_gain(c, j):
                    pool.wait_ge(hn_ready, c + 1)
                    wait_from(pool, stored[j], 8 * (c - j))
                    nc.gpsimd.tensor_tensor(y[:, j, :], ht[:, j, :, :].rearrange("p h e -> p (h e)"), ng[:, :], ALU.mult).then_inc(ng_done, 1)

                skewed(pool, [(norm_gain, -1)])


def load_norm(eng, nc, d, norm, gain, l, which, sem):
    eng.dma_start(norm[:, 0, :], d["ln_g"][l, which:which + 1, :].to_broadcast([P, D])).then_inc(sem, 16)
    eng.dma_start(norm[:, 1, :], d["ln_b"][l, which:which + 1, :].to_broadcast([P, D])).then_inc(sem, 16)
    kind = 3 * which + 2
    eng.dma_start(gain[:, :], d["mod"][l:l + 1, kind * D:(kind + 1) * D].to_broadcast([P, D])).then_inc(sem, 16)


def after_mixer(nc, d, l):
    K = KD if l == 0 else BW // P
    W = K * P
    name = f"am{l}"
    with Phase(nc, name) as ph:
        w = ph.sb("w", [P, K, D])
        ws = ph.sb("ws", [P, 2, K, D], F32R)
        wr = ph.sb("wr", [P, KD, NR])
        br = ph.sb("br", [P, NR])
        ident = ph.sb("ident", [P, P])
        cols = ph.sb("cols", [P, 2, KD])
        norm = ph.sb("norm", [P, 2, D])
        gain = ph.sb("gain", [P, D])
        y = ph.sb("y", [P, 2, W])
        x = ph.sb("x", [P, 2, D])
        yT = ph.sb("yT", [P, 2, 2, K, P], F32R)
        z = ph.sb("z", [P, 2, D])
        x1 = ph.sb("x1", [P, 2, D])
        hT = ph.sb("hT", [P, KD, P])
        stats = ph.sb("stats", [P, 2, 6])
        mv = ph.sb("mv", [P, 2, 2])
        std = ph.sb("std", [P, 2, 3])
        nb = ph.sb("nb", [P, 2, 1])
        lg = ph.sb("lg", [P, 2, NR])
        if l:
            o = ph.sb("o", [P, 2, G, HP * OW])
            coef = ph.sb("coef", [P, 2, G, BH])
            cd = ph.sb("cd", [P, G, BH])
            mx = ph.sb("mx", [P, BH])
            dn = ph.sb("dn", [P, BH])
            og = ph.sb("og", [P, G, BW])
        ytp = [ph.ps(f"ytp{i}", [P, 4, P]) for i in range(K // 4)]
        xtp = [ph.ps(f"xtp{i}", [P, 4, P]) for i in range(2)]
        acc = [[ph.ps(f"acc{j}{i}", [P, CH]) for i in range(2)] for j in range(2)]
        bl = ph.ps("bl", [P, NR]) if l else xtp[0][:, 0, 0:NR]
        names = ("c_in", "cols_ready", "whi_ready", "wlo_ready", "ytp_ready", "yhi_ready", "ylo_ready", "acc_ready", "z_ready", "v_ready", "std_ready", "nb_ready",
                 "xn_ready", "xg_ready", "x1_ready", "xtp_ready", "hT_ready", "lg_acc", "lg_ready", "waited", "y_ready", "e_in", "e_ready", "og_ready")
        (c_in, cols_ready, whi_ready, wlo_ready, ytp_ready, yhi_ready, ylo_ready, acc_ready, z_ready, v_ready, std_ready, nb_ready,
         xn_ready, xg_ready, x1_ready, xtp_ready, hT_ready, lg_acc, lg_ready, waited, y_ready, e_in, e_ready, og_ready) = (ph.sem(s) for s in names)
        w_in = [ph.sem(f"w_in{j}") for j in range(K)]
        y_in = [ph.sem(f"y_in{j}") for j in range(2)]
        x_in = [ph.sem(f"x_in{j}") for j in range(2)]
        x_st = [ph.sem(f"x_st{j}") for j in range(2)]
        l_st = [ph.sem(f"l_st{j}") for j in range(2)]
        x_dram = d["x"][0] if l == 0 else d["x2"]
        w_dram = (d["a_w_out"] if l == 0 else d["b_w_o"])[0].rearrange("(p k) n -> p k n", k=K)

        with nc.Block() as block:
            @block.sync
            def _(sp):
                def load_y(c, j):
                    wait_from(sp, og_ready if l else ytp_ready, c - 1)
                    settle(sp, waited)
                    if l == 0:
                        sp.dma_start(y[:, j, :], d["y"][ds(c * P, P), :]).then_inc(y_in[j], 16)
                    else:
                        sp.dma_start(o[:, j, :, :], d["o"][:, ds(c * P, P), :].rearrange("g p n -> p g n")).then_inc(y_in[j], 16)

                def load_x(c, j):
                    wait_from(sp, z_ready, c - 1)
                    settle(sp, waited)
                    sp.dma_start(x[:, j, :], x_dram[ds(c * P, P), :]).then_inc(x_in[j], 16)

                def store_x1(c, j):
                    sp.wait_ge(x1_ready, c + 1)
                    settle(sp, waited)
                    sp.dma_start(d["x1"][ds(c * P, P), :], x1[:, j, :]).then_inc(x_st[j], 16)

                def store_logits(c, j):
                    sp.wait_ge(lg_ready, c + 1)
                    settle(sp, waited)
                    sp.dma_start(d["lg"][ds(c * P, P), :], lg[:, j, :]).then_inc(l_st[j], 16)

                sp.dma_start(ident[:, :], d["consts"][:, C_ID:C_ID + P]).then_inc(c_in, 16)
                load_mod_columns(sp, nc, d, cols, l, (3, 4), c_in)
                load_norm(sp, nc, d, norm, gain, l, 0, c_in)
                sp.dma_start(wr[:, :, 0:MG], d["moe_w_r1"][l].rearrange("(p k) n -> p k n", k=KD)).then_inc(c_in, 16)
                sp.dma_start(wr[:, :, MG:NR], d["moe_w_r2"][l].rearrange("(p k) n -> p k n", k=KD)).then_inc(c_in, 16)
                sp.dma_start(br[:, 0:MG], d["moe_b_r1"][l:l + 1, :].to_broadcast([P, MG])).then_inc(c_in, 16)
                sp.dma_start(br[:, MG:NR], d["moe_b_r2"][l:l + 1, :].to_broadcast([P, NE])).then_inc(c_in, 16)
                for c in range(2):
                    load_y(c, c)
                for k in range(K):
                    sp.dma_start(w[:, k, :], w_dram[:, k, :]).then_inc(w_in[k], 16)

                def load_y_later(c, j):
                    if not (isinstance(c, int) and c < 2):
                        load_y(c, j)

                skewed(sp, [(load_y_later, 5 if l else 4), (load_x, 2), (store_logits, -2), (store_x1, -1)])
                for j in range(2):
                    sp.wait_ge(x_st[j], 16 * NT // 2)
                    sp.wait_ge(l_st[j], 16 * NT // 2)

            @block.tensor
            def _(pe):
                pe.wait_ge(c_in, 16 * 10)

                def y_transposes(c, j):
                    if l:
                        pe.wait_ge(y_ready, c + 1)
                    else:
                        pe.wait_ge(y_in[j], 8 * (c - j) + 16)
                    wait_from(pe, ylo_ready, c)
                    for k in range(K):
                        ins = nc.tensor.transpose(ytp[k // 4][:, k % 4, :], y[:, j, k:W:K], ident[:, :])
                    ins.then_inc(ytp_ready, 1)

                def out_half(c, j, half):
                    if half == 0:
                        pe.wait_ge(yhi_ready, c + 1)
                        pe.wait_ge(ylo_ready, c + 1)
                        wait_from(pe, z_ready, c - 1)
                    for k in range(K):
                        if half == 0 and isinstance(c, int) and c == 0:
                            pe.wait_ge(wlo_ready, k + 1)
                        for n, (a, b) in enumerate(((0, 0), (0, 1), (1, 0))):
                            ins = nc.tensor.matmul(acc[j][half][:, :], yT[:, j, a, k, :], ws[:, b, k, half * CH:(half + 1) * CH],
                                                   start=(k == 0 and n == 0), stop=(k == K - 1 and n == 2))
                    if half:
                        ins.then_inc(acc_ready, 1)

                def logits(c, j):
                    pe.wait_ge(hT_ready, c + 1)
                    wait_from(pe, lg_ready, c)
                    for k in range(KD):
                        ins = nc.tensor.matmul(bl[:, :], hT[:, k, :], wr[:, k, :], start=(k == 0), stop=(k == KD - 1))
                    ins.then_inc(lg_acc, 1)

                def x1_transposes(c, j):
                    pe.wait_ge(x1_ready, c + 1)
                    wait_from(pe, hT_ready, c)
                    if l == 0:
                        wait_from(pe, lg_ready, c)
                    for k in range(KD):
                        ins = nc.tensor.transpose(xtp[k // 4][:, k % 4, :], x1[:, j, k:D:KD], ident[:, :])
                    ins.then_inc(xtp_ready, 1)

                skewed(pe, [(lambda c, j: out_half(c, j, 0), 1), (y_transposes, 2), (logits, -2),
                            (lambda c, j: out_half(c, j, 1), 1), (x1_transposes, -1)])

            @block.scalar
            def _(act):
                def weights_hi():
                    for k in range(K):
                        act.wait_ge(w_in[k], 16)
                        nc.scalar.activation(ws[:, 0, k, :], w[:, k, :], ACT.Copy).then_inc(whi_ready, 1)

                weights_hi()
                act.wait_ge(cols_ready, 1)

                def branch_weights(c, j):
                    act.wait_ge(e_in, c + 1)
                    nc.scalar.activation(coef[:, j, :, :], coef[:, j, :, :], ACT.Exp).then_inc(e_ready, 1)

                def y_hi(c, j):
                    act.wait_ge(ytp_ready, c + 1)
                    wait_from(act, acc_ready, c - 1)
                    for i in range(K // 4):
                        ins = nc.scalar.activation(yT[:, j, 0, i * 4:(i + 1) * 4, :], ytp[i][:, :, :], ACT.Copy)
                    ins.then_inc(yhi_ready, 1)

                def root(c, j):
                    act.wait_ge(v_ready, c + 1)
                    nc.scalar.activation(std[:, j, 1:2], std[:, j, 0:1], ACT.Sqrt).then_inc(std_ready, 1)

                def normalise(c, j):
                    act.wait_ge(nb_ready, c + 1)
                    nc.scalar.activation(z[:, j, :], z[:, j, :], ACT.Identity, bias=nb[:, j, 0:1], scale=std[:, j, 2:3]).then_inc(xn_ready, 1)

                def modulate(c, j):
                    act.wait_ge(xtp_ready, c + 1)
                    wait_from(act, lg_acc, c)
                    for k in range(KD):
                        ins = nc.scalar.activation(hT[:, k, :], xtp[k // 4][:, k % 4, :], ACT.Identity,
                                                   bias=cols[:, 0, k:k + 1], scale=cols[:, 1, k:k + 1])
                    ins.then_inc(hT_ready, 1)

                skewed(act, [(modulate, -2), (y_hi, 2), (root, 0), (normalise, 0)] + ([(branch_weights, 4)] if l else []))

            @block.vector
            def _(dve):
                dve.wait_ge(c_in, 16 * 10)
                nc.vector.tensor_scalar(cols[:, 1, :], cols[:, 1, :], 1.0, None, ALU.add).then_inc(cols_ready, 1)
                nc.vector.tensor_scalar(gain[:, :], gain[:, :], 1.0, None, ALU.add)
                for k in range(K):
                    dve.wait_ge(whi_ready, k + 1)
                    nc.vector.tensor_tensor(ws[:, 1, k, :], w[:, k, :], ws[:, 0, k, :], ALU.subtract).then_inc(wlo_ready, 1)

                def branch_maxima(c, j):
                    dve.wait_ge(y_in[j], 8 * (c - j) + 16)
                    m = o[:, j, :, :].rearrange("p g (h e) -> p g h e", e=DH + 2)[:, :, :, DH]
                    nc.vector.tensor_tensor(mx[:, :], m[:, 0, :], m[:, 1, :], ALU.min)
                    dve.drain()
                    nc.vector.tensor_tensor(mx[:, :], mx[:, :], m[:, 2, :], ALU.min)
                    dve.drain()
                    for g in range(G):
                        ins = nc.vector.tensor_tensor(coef[:, j, g, :], mx[:, :], m[:, g, :], ALU.subtract)
                    ins.then_inc(e_in, 1)

                def branches(c, j):
                    v = o[:, j, :, :].rearrange("p g (h e) -> p g h e", e=DH + 2)
                    dve.wait_ge(e_ready, c + 1)
                    nc.vector.tensor_tensor(cd[:, :, :], coef[:, j, :, :], v[:, :, :, DH + 1], ALU.mult)
                    dve.drain()
                    nc.vector.tensor_tensor(dn[:, :], cd[:, 0, :], cd[:, 1, :], ALU.add)
                    dve.drain()
                    nc.vector.tensor_tensor(dn[:, :], dn[:, :], cd[:, 2, :], ALU.add)
                    dve.drain()
                    nc.vector.reciprocal(dn[:, :], dn[:, :])
                    dve.drain()
                    nc.vector.tensor_tensor(coef[:, j, :, :], coef[:, j, :, :], dn[:, :].rearrange("p (o h) -> p o h", o=1).to_broadcast([P, G, BH]), ALU.mult)
                    dve.drain()
                    wait_from(dve, y_ready, c)
                    for g in range(G):
                        ins = nc.vector.tensor_tensor(og[:, g, :].rearrange("p (h e) -> p h e", e=DH), v[:, g, :, 0:DH],
                                                      coef[:, j, g, :].rearrange("p (h o) -> p h o", o=1).to_broadcast([P, BH, DH]), ALU.mult)
                    ins.then_inc(og_ready, 1)

                def y_lo(c, j):
                    dve.wait_ge(yhi_ready, c + 1)
                    for i in range(K // 4):
                        ins = nc.vector.tensor_tensor(yT[:, j, 1, i * 4:(i + 1) * 4, :], ytp[i][:, :, :], yT[:, j, 0, i * 4:(i + 1) * 4, :], ALU.subtract)
                    ins.then_inc(ylo_ready, 1)

                def total(c, j):
                    dve.wait_ge(acc_ready, c + 1)
                    wait_from(dve, xg_ready, c - 1)
                    for half in range(2):
                        cut = slice(half * CH, (half + 1) * CH)
                        nc.vector.tensor_tensor(z[:, j, cut], acc[j][half][:, :], gain[:, cut], ALU.mult)
                    dve.drain()
                    dve.wait_ge(x_in[j], 8 * (c - j) + 16)
                    nc.vector.scalar_tensor_tensor(z[:, j, :], x[:, j, :], ALPHA, z[:, j, :], ALU.mult, ALU.add).then_inc(z_ready, 1)
                    dve.wait_ge(z_ready, c + 1)
                    for half in range(2):
                        nc.vector.bn_stats(stats[:, half, :], z[:, j, half * CH:(half + 1) * CH])
                    dve.drain()
                    nc.vector.bn_aggr(mv[:, j, :], stats[:, :, :].rearrange("p a b -> p (a b)"))
                    dve.drain()
                    nc.vector.tensor_scalar(std[:, j, 0:1], mv[:, j, 1:2], LN_EPS, None, ALU.add).then_inc(v_ready, 1)

                def scale(c, j):
                    dve.wait_ge(std_ready, c + 1)
                    nc.vector.reciprocal(std[:, j, 2:3], std[:, j, 1:2])
                    dve.drain()
                    nc.vector.tensor_scalar(nb[:, j, :], mv[:, j, 0:1], std[:, j, 2:3], -1.0, ALU.mult, ALU.mult).then_inc(nb_ready, 1)

                def finish(c, j):
                    dve.wait_ge(xg_ready, c + 1)
                    nc.vector.tensor_tensor(x1[:, j, :], x1[:, j, :], norm[:, 1, :], ALU.add).then_inc(x1_ready, 1)

                def bias_logits(c, j):
                    dve.wait_ge(lg_acc, c + 1)
                    wait_from(dve, l_st[j], 8 * (c - j))
                    nc.vector.tensor_tensor(lg[:, j, :], bl[:, :], br[:, :], ALU.add).then_inc(lg_ready, 1)

                skewed(dve, [(total, 0), (bias_logits, -2), (finish, -1), (y_lo, 2)] + ([(branches, 3), (branch_maxima, 4)] if l else []) + [(scale, 0)])

            @block.gpsimd
            def _(pool):
                pool.wait_ge(c_in, 16 * 10)

                def sum_branches(c, j):
                    pool.wait_ge(og_ready, c + 1)
                    wait_from(pool, ytp_ready, c - 1)
                    nc.gpsimd.tensor_tensor(og[:, 0, :], og[:, 0, :], og[:, 1, :], ALU.add)
                    pool.drain()
                    nc.gpsimd.tensor_tensor(y[:, j, :], og[:, 0, :], og[:, 2, :], ALU.add).then_inc(y_ready, 1)

                def gamma(c, j):
                    pool.wait_ge(xn_ready, c + 1)
                    wait_from(pool, x_st[j], 8 * (c - j))
                    wait_from(pool, xtp_ready, c - 1)
                    nc.gpsimd.tensor_tensor(x1[:, j, :], z[:, j, :], norm[:, 0, :], ALU.mult).then_inc(xg_ready, 1)

                skewed(pool, ([(sum_branches, 3)] if l else []) + [(gamma, 0)])


def route(nc, d, l):
    with Phase(nc, f"rt{l}") as ph:
        lg = ph.sb("lg", [P, NT, NR])
        iota = ph.sb("iota", [P, NE])
        blk = ph.sb("blk", [P, NBP])
        before = ph.sb("before", [P, P])
        ones = ph.sb("ones", [P, P])
        tokf = ph.sb("tokf", [P, NT])
        tok = ph.sb("tok", [P, NT], I32)
        zero = ph.sb("zero", [NBP, P], I32)
        gpad = ph.sb("gpad", [P, NT, 8])
        gval, gidx = ph.sb("gval", [P, NT, 8]), ph.sb("gidx", [P, NT, 8], U32)
        gf = ph.sb("gf", [P, NT])
        eg = ph.sb("eg", [P, NT, MG])
        pg = ph.sb("pg", [P, NT])
        oh4 = ph.sb("oh4", [P, NT, MG])
        pen = ph.sb("pen", [P, NT, MG])
        masked = ph.sb("masked", [P, NT, NE])
        val, idx = ph.sb("val", [P, NT, 8]), ph.sb("idx", [P, NT, 8], U32)
        ef = ph.sb("ef", [P, NT, 2])
        dif = ph.sb("dif", [P, NT])
        ex = ph.sb("ex", [P, NT])
        wt = ph.sb("wt", [P, NT, 2])
        oh = [ph.sb(f"oh{j}", [P, NT, NE]) for j in range(2)]
        both = ph.sb("both", [P, NT, NE])
        pre = ph.sb("pre", [P, NT + 1, NE])
        cnti = ph.sb("cnti", [P, NE], I32)
        pc = ph.sb("pc", [P, NE])
        pend = ph.sb("pend", [P, NE])
        pstart = ph.sb("pstart", [P, NE])
        dest = ph.sb("dest", [P, NT, NE])
        hit = ph.sb("hit", [P, NT, NE])
        destf = ph.sb("destf", [P, NT, 2])
        desti = ph.sb("desti", [P, NT, 2], I32)
        le = ph.sb("le", [P, NBP, NE])
        bef = ph.sb("bef", [P, NBP])
        bei = ph.sb("bei", [P, NBP], I32)
        rank, total = ph.ps("rank", [P, NT, NE]), ph.ps("total", [P, NT, NE])
        in_sem, e_in, e_out, d_in, d_out = (ph.sem(s) for s in ("in", "e_in", "e_out", "d_in", "d_out"))
        both_ready, rank_ready, tok_ready, zero_ready, zeroed = (ph.sem(s) for s in ("both_ready", "rank_ready", "tok_ready", "zero_ready", "zeroed"))
        dest_ready, blk_ready, out_done = (ph.sem(s) for s in ("dest_ready", "blk_ready", "out_done"))
        scattered = d["pool_dma"](f"rt{l}")[0]

        def over(a, shape):
            return a.rearrange("p (n o) -> p n o", o=1).to_broadcast(shape)

        def per_tile(a, n, k):
            return a.rearrange("p (o k) -> p o k", o=1).to_broadcast([P, n, k])

        with nc.Block() as block:
            @block.sync
            def _(sp):
                sp.dma_start(lg[:, :, :], d["lg"].rearrange("(c p) n -> p c n", p=P)).then_inc(in_sem, 16)
                for t, c, n in ((iota, C_EXP, NE), (blk, C_BLK, NBP), (before, C_BEFORE, P), (ones, C_ONES, P), (tokf, C_TOK, NT)):
                    sp.dma_start(t[:, :], d["consts"][:, c:c + n]).then_inc(in_sem, 16)
                sp.wait_ge(zero_ready, 1)
                sp.dma_start(d["slot_tok"].rearrange("(b p) o -> b (p o)", p=P), zero[:, :]).then_inc(zeroed, 16)
                sp.wait_ge(dest_ready, 1)
                sp.dma_start(d["dest"], desti[:, :, :].rearrange("p c j -> p (c j)")).then_inc(out_done, 16)
                sp.dma_start(d["wt"], wt[:, :, :].rearrange("p c j -> p (c j)")).then_inc(out_done, 16)
                sp.wait_ge(blk_ready, 1)
                sp.dma_start(d["block_e"], bei[0:1, :]).then_inc(out_done, 16)
                sp.wait_ge(out_done, 48)

            @block.scalar
            def _(act):
                act.wait_ge(e_in, 1)
                nc.scalar.activation(eg[:, :, :], eg[:, :, :], ACT.Exp).then_inc(e_out, 1)
                act.wait_ge(d_in, 1)
                nc.scalar.activation(ex[:, :], dif[:, :], ACT.Exp).then_inc(d_out, 1)

            @block.tensor
            def _(pe):
                pe.wait_ge(both_ready, 1)
                nc.tensor.matmul(rank[:, :, :], before[:, :], both[:, :, :], start=True, stop=True)
                nc.tensor.matmul(total[:, :, :], ones[:, :], both[:, :, :], start=True, stop=True).then_inc(rank_ready, 1)

            @block.vector
            def _(dve):
                v = nc.vector
                v.memset(zero[:, :], 0).then_inc(zero_ready, 1)
                v.memset(gpad[:, :, :], -3e38)
                dve.drain()
                dve.wait_ge(in_sem, 16 * 6)
                v.tensor_copy(tok[:, :], tokf[:, :]).then_inc(tok_ready, 1)
                v.tensor_copy(gpad[:, :, 0:MG], lg[:, :, 0:MG])
                dve.drain()
                for c in range(NT):
                    v.max(gval[:, c, :], gpad[:, c, :])
                dve.drain()
                for c in range(NT):
                    v.max_index(gidx[:, c, :], gval[:, c, :], gpad[:, c, :])
                v.tensor_tensor(eg[:, :, :], lg[:, :, 0:MG], over(gval[:, :, 0], [P, NT, MG]), ALU.subtract).then_inc(e_in, 1)
                dve.drain()
                v.tensor_copy(gf[:, :], gidx[:, :, 0])
                dve.drain()
                v.tensor_tensor(oh4[:, :, :], per_tile(iota[:, 0:MG], NT, MG), over(gf[:, :], [P, NT, MG]), ALU.is_equal)
                dve.drain()
                v.tensor_scalar(pen[:, :, :], oh4[:, :, :], -NEG, NEG, ALU.mult, ALU.add)
                m4 = masked[:, :, :].rearrange("p c (g e) -> p c g e", g=MG)
                wide = [P, NT, MG, ME]
                v.tensor_tensor(m4, lg[:, :, MG:NR].rearrange("p c (g e) -> p c g e", g=MG),
                                oh4[:, :, :].rearrange("p c (g o) -> p c g o", o=1).to_broadcast(wide), ALU.mult)
                dve.drain()
                v.tensor_tensor(m4, m4, pen[:, :, :].rearrange("p c (g o) -> p c g o", o=1).to_broadcast(wide), ALU.add)
                dve.drain()
                for c in range(NT):
                    v.max(val[:, c, :], masked[:, c, :])
                dve.drain()
                for c in range(NT):
                    v.max_index(idx[:, c, :], val[:, c, :], masked[:, c, :])
                v.tensor_tensor(dif[:, :], val[:, :, 1], val[:, :, 0], ALU.subtract).then_inc(d_in, 1)
                dve.drain()
                v.tensor_copy(ef[:, :, :], idx[:, :, 0:2])
                dve.drain()
                for j in range(2):
                    v.tensor_tensor(oh[j][:, :, :], per_tile(iota[:, :], NT, NE), over(ef[:, :, j], [P, NT, NE]), ALU.is_equal)
                dve.drain()
                v.tensor_tensor(both[:, :, :], oh[0][:, :, :], oh[1][:, :, :], ALU.add).then_inc(both_ready, 1)
                dve.wait_ge(e_out, 1)
                v.tensor_reduce(pg[:, :], eg[:, :, :], AX_X, ALU.add)
                dve.wait_ge(d_out, 1)
                v.tensor_scalar(dif[:, :], ex[:, :], 1.0, None, ALU.add)
                dve.drain()
                v.tensor_tensor(pg[:, :], pg[:, :], dif[:, :], ALU.mult)
                dve.drain()
                v.reciprocal(wt[:, :, 0], pg[:, :])
                dve.drain()
                v.tensor_tensor(wt[:, :, 1], wt[:, :, 0], ex[:, :], ALU.mult)
                v.memset(pre[:, 0, :], 0.0)
                dve.wait_ge(rank_ready, 1)
                for c in range(NT):
                    dve.drain()
                    v.tensor_tensor(pre[:, c + 1, :], pre[:, c, :], total[:, c, :], ALU.add)
                dve.drain()
                v.tensor_copy(cnti[:, :], pre[:, NT, :])
                dve.drain()
                v.tensor_scalar(cnti[:, :], cnti[:, :], float(P - 1), None, ALU.add)
                dve.drain()
                v.tensor_scalar(cnti[:, :], cnti[:, :], 7, 7, ALU.logical_shift_right, ALU.logical_shift_left)
                dve.drain()
                v.tensor_copy(pc[:, :], cnti[:, :])
                dve.drain()
                v.tensor_tensor_scan(pend[:, :], ones[:, 0:NE], pc[:, :], 0.0, ALU.mult, ALU.add)
                dve.drain()
                v.tensor_tensor(pstart[:, :], pend[:, :], pc[:, :], ALU.subtract)
                v.tensor_tensor(dest[:, :, :], rank[:, :, :], pre[:, 0:NT, :], ALU.add)
                dve.drain()
                v.tensor_tensor(dest[:, :, :], dest[:, :, :], per_tile(pstart[:, :], NT, NE), ALU.add)
                for j in range(2):
                    dve.drain()
                    v.tensor_tensor(hit[:, :, :], dest[:, :, :], oh[j][:, :, :], ALU.mult)
                    dve.drain()
                    v.tensor_reduce(destf[:, :, j], hit[:, :, :], AX_X, ALU.add)
                dve.drain()
                v.tensor_copy(desti[:, :, :], destf[:, :, :])
                dve.drain().then_inc(dest_ready, 1)
                v.tensor_tensor(le[:, :, :], per_tile(pend[:, :], NBP, NE), over(blk[:, :], [P, NBP, NE]), ALU.is_le)
                dve.drain()
                v.tensor_reduce(bef[:, :], le[:, :, :], AX_X, ALU.add)
                dve.drain()
                v.tensor_scalar(bef[:, :], bef[:, :], float(NE - 1), None, ALU.min)
                dve.drain()
                v.tensor_copy(bei[:, :], bef[:, :]).then_inc(blk_ready, 1)

            @block.gpsimd
            def _(pool):
                pool.wait_ge(tok_ready, 1)
                pool.wait_ge(dest_ready, 1)
                pool.wait_ge(zeroed, 16)
                for c in range(NT):
                    for j in range(2):
                        nc.gpsimd.indirect_dma_start(out=d["slot_tok"], out_offset=bass.IndirectOffsetOnAxis(ap=desti[:, c, j:j + 1], axis=0),
                                                     in_=tok[:, c:c + 1], in_offset=None).then_inc(scattered, 16)
                pool.wait_ge(scattered, 16 * 2 * NT)


def experts(nc, d, l):
    JH = HID // P
    with Phase(nc, f"ex{l}") as ph:
        ident = ph.sb("ident", [P, P])
        cols = ph.sb("cols", [P, 2, KD])
        slots = ph.sb("slots", [NBP, P], I32)
        slotf = ph.sb("slotf", [NBP, P])
        tok = ph.sb("tok", [P, NBP], I32)
        tokb = ph.sb("tokb", [P, 2], I32)
        be = ph.sb("be", [1, NBP], I32)
        xg = ph.sb("xg", [P, 2, D])
        hT = ph.sb("hT", [P, 2, KD, P])
        wgu = ph.sb("wgu", [P, 2, KD, 2, HID])
        wd = ph.sb("wd", [P, 2, JH, D])
        sg = ph.sb("sg", [P, HID])
        a = ph.sb("a", [P, HID])
        aT = ph.sb("aT", [P, JH, P])
        y = ph.sb("y", [P, 2, D])
        tp = [ph.ps(f"tp{i}", [P, 4, P]) for i in range(2)]
        gu = [ph.ps(f"gu{j}", [P, 2, HID]) for j in range(2)]
        at = ph.ps("at", [P, JH, P])
        acc = [ph.ps(f"acc{i}", [P, CH]) for i in range(2)]
        (c_in, s_in, cols_ready, slotf_ready, st_ready, tok_ready, htp_ready, hT_act, hT_dve, gu_ready, sg_ready, a_ready, atp_ready, aT_ready,
         acc_ready, y_act, y_dve, waited, free) = (ph.sem(s) for s in (
             "c_in", "s_in", "cols_ready", "slotf_ready", "st_ready", "tok_ready", "htp_ready", "hT_act", "hT_dve", "gu_ready", "sg_ready", "a_ready",
             "atp_ready", "aT_ready", "acc_ready", "y_act", "y_dve", "waited", "free"))
        gu_in, wd_in, stored = ([ph.sem(f"{n}{j}") for j in range(2)] for n in ("gu_in", "wd_in", "stored"))
        x_in = d["pool_dma"](f"ex{l}")
        views = [d[n][l].rearrange("e (p k) n -> e p k n", p=P) for n in ("moe_w_gate", "moe_w_up", "moe_w_down")]

        with nc.Block() as block:
            @block.sync
            def _(sp):
                for credited, by in ((a_ready, 1), (aT_ready, 1), (y_act, 1), (y_dve, 1), (acc_ready, 1), (stored[0], 16), (stored[1], 16)):
                    sp.sem_inc(credited, by)
                sp.dma_start(be[:, :], d["block_e"]).then_inc(s_in, 16)
                sp.dma_start(slots[:, :], d["slot_tok"].rearrange("(b p) o -> b (p o)", p=P)).then_inc(s_in, 16)
                sp.dma_start(ident[:, :], d["consts"][:, C_ID:C_ID + P]).then_inc(c_in, 16)
                load_mod_columns(sp, nc, d, cols, l, (3, 4), c_in)
                sp.wait_ge(s_in, 32)

                def step(b, j, first):
                    if not (isinstance(b, int) and b < 2):
                        sp.wait_ge(gu_ready, b - 1)
                    e = sp.value_load(be[0:1, ds(b, 1)], min_val=0, max_val=NE - 1)
                    for n in range(2):
                        sp.dma_start(wgu[:, j, :, n, :], views[n][ds(e, 1), :, :, :].rearrange("e p k n -> p (e k) n")).then_inc(gu_in[j], 16)
                    if not (isinstance(b, int) and b < 2):
                        sp.wait_ge(acc_ready, b)
                        settle(sp, waited)
                    sp.dma_start(wd[:, j, :, :], views[2][ds(e, 1), :, :, :].rearrange("e p k n -> p (e k) n")).then_inc(wd_in[j], 16)

                step(0, 0, True)
                step(1, 1, True)
                with sp.Fori(1, (NB - 1) // 2) as i:
                    for j in range(2):
                        step(i * 2 + j, j, False)
                step(NB - 1, 0, False)

            @block.gpsimd
            def _(pool):
                pool.wait_ge(tok_ready, 1)

                def step(b, j, first):
                    if not (isinstance(b, int) and b < 2):
                        pool.wait_ge(htp_ready, b - 1)
                    nc.gpsimd.tensor_copy(tokb[:, j:j + 1], tok[:, ds(b, 1)])
                    pool.drain()
                    nc.gpsimd.indirect_dma_start(out=xg[:, j, :], out_offset=None, in_=d["x1"],
                                                 in_offset=bass.IndirectOffsetOnAxis(ap=tokb[:, j:j + 1], axis=0)).then_inc(x_in[j], 16)

                step(0, 0, True)
                step(1, 1, True)
                with pool.Fori(1, (NB - 1) // 2) as i:
                    for j in range(2):
                        step(i * 2 + j, j, False)
                step(NB - 1, 0, False)

            @block.tensor
            def _(pe):
                pe.wait_ge(slotf_ready, 1)
                pe.wait_ge(c_in, 48)
                nc.tensor.transpose(at[:, 0, 0:NBP], slotf[:, :], ident[0:NBP, 0:NBP]).then_inc(st_ready, 1)

                def transposes(b, j):
                    pe.wait_ge(x_in[j], 8 * (b - j) + 16)
                    pe.wait_ge(hT_act, b)
                    pe.wait_ge(hT_dve, b)
                    for k in range(KD):
                        ins = nc.tensor.transpose(tp[k // 4][:, k % 4, :], xg[:, j, k:D:KD], ident[:, :])
                    ins.then_inc(htp_ready, 1)

                def gate_up(b, j, half):
                    if half == 0:
                        pe.wait_ge(hT_act, b + 1)
                        pe.wait_ge(hT_dve, b + 1)
                        pe.wait_ge(gu_in[j], 16 * (b - j) + 32)
                        if not (isinstance(b, int) and b < 2):
                            pe.wait_ge(a_ready, b)
                    for k in range(half * 4, half * 4 + 4):
                        ins = nc.tensor.matmul(gu[j][:, :, :], hT[:, j, k, :], wgu[:, j, k, :, :], start=(k == 0), stop=(k == KD - 1))
                    if half:
                        ins.then_inc(gu_ready, 1)

                def act_transposes(b):
                    pe.wait_ge(a_ready, b + 2)
                    pe.wait_ge(aT_ready, b + 1)
                    for k in range(JH):
                        ins = nc.tensor.transpose(at[:, k, :], a[:, k:HID:JH], ident[:, :])
                    ins.then_inc(atp_ready, 1)

                def down(b, j):
                    pe.wait_ge(aT_ready, b + 2)
                    pe.wait_ge(wd_in[j], 8 * (b - j) + 16)
                    pe.wait_ge(y_act, b + 1)
                    pe.wait_ge(y_dve, b + 1)
                    for half in range(2):
                        for k in range(JH):
                            ins = nc.tensor.matmul(acc[half][:, :], aT[:, k, :], wd[:, j, k, half * CH:(half + 1) * CH],
                                                   start=(k == 0), stop=(k == JH - 1))
                    ins.then_inc(acc_ready, 1)

                def step(b, j, first, last):
                    gate_up(b, j, 0)
                    if not first:
                        act_transposes(b - 1)
                    gate_up(b, j, 1)
                    if not last:
                        transposes(b + 1, 1 - j)
                    if not first:
                        down(b - 1, 1 - j)

                pe.wait_ge(tok_ready, 1)
                transposes(0, 0)
                step(0, 0, True, False)
                with pe.Fori(0, (NB - 3) // 2) as i:
                    for j in range(2):
                        step(i * 2 + j + 1, (j + 1) % 2, False, False)
                step(NB - 2, 1, False, False)
                step(NB - 1, 0, False, True)
                act_transposes(NB - 1)
                down(NB - 1, 0)

            @block.scalar
            def _(act):
                act.wait_ge(cols_ready, 1)

                def rows(b, j):
                    act.wait_ge(htp_ready, b + 1)
                    if not (isinstance(b, int) and b < 2):
                        act.wait_ge(gu_ready, b - 1)
                    for k in range(4):
                        ins = nc.scalar.activation(hT[:, j, k, :], tp[0][:, k, :], ACT.Identity, bias=cols[:, 0, k:k + 1], scale=cols[:, 1, k:k + 1])
                    ins.then_inc(hT_act, 1)

                def store(b, j):
                    act.wait_ge(acc_ready, b + 2)
                    act.wait_ge(stored[j], 8 * (b - j) + 16)
                    nc.scalar.activation(y[:, j, CH:D], acc[1][:, :], ACT.Copy).then_inc(y_act, 1)
                    act.wait_ge(y_act, b + 2)
                    act.wait_ge(y_dve, b + 2)
                    settle(act, waited)
                    act.dma_start(d["ybuf"][ds(b * P, P), :], y[:, j, :]).then_inc(stored[j], 16)

                def step(b, j, first, last):
                    act.wait_ge(gu_ready, b + 1)
                    act.wait_ge(a_ready, b + 1)
                    nc.scalar.activation(sg[:, :], gu[j][:, 0, :], ACT.Silu).then_inc(sg_ready, 1)
                    if not last:
                        rows(b + 1, 1 - j)
                    if not first:
                        store(b - 1, 1 - j)

                rows(0, 0)
                step(0, 0, True, False)
                with act.Fori(0, (NB - 3) // 2) as i:
                    for j in range(2):
                        step(i * 2 + j + 1, (j + 1) % 2, False, False)
                step(NB - 2, 1, False, False)
                step(NB - 1, 0, False, True)
                store(NB - 1, 0)
                act.wait_ge(stored[0], 8 * (NB + 1) + 16)
                act.wait_ge(stored[1], 8 * (NB - 1) + 16)

            @block.vector
            def _(dve):
                dve.wait_ge(c_in, 48)
                nc.vector.tensor_scalar(cols[:, 1, :], cols[:, 1, :], 1.0, None, ALU.add).then_inc(cols_ready, 1)
                dve.wait_ge(s_in, 32)
                nc.vector.tensor_copy(slotf[:, :], slots[:, :]).then_inc(slotf_ready, 1)
                dve.wait_ge(st_ready, 1)
                nc.vector.tensor_copy(tok[:, :], at[:, 0, 0:NBP]).then_inc(tok_ready, 1)
                dve.wait_ge(cols_ready, 1)

                def rows(b, j):
                    dve.wait_ge(htp_ready, b + 1)
                    if not (isinstance(b, int) and b < 2):
                        dve.wait_ge(gu_ready, b - 1)
                    for k in range(4, KD):
                        ins = nc.vector.tensor_scalar(hT[:, j, k, :], tp[1][:, k - 4, :], cols[:, 1, k:k + 1], cols[:, 0, k:k + 1], ALU.mult, ALU.add)
                    ins.then_inc(hT_dve, 1)

                def output(b, j):
                    dve.wait_ge(acc_ready, b + 2)
                    dve.wait_ge(stored[j], 8 * (b - j) + 16)
                    nc.vector.tensor_copy(y[:, j, 0:CH], acc[0][:, :]).then_inc(y_dve, 1)

                def turned(b):
                    dve.wait_ge(atp_ready, b + 1)
                    dve.wait_ge(acc_ready, b + 1)
                    nc.vector.tensor_copy(aT[:, :, :], at[:, :, :]).then_inc(aT_ready, 1)

                def step(b, j, first, last):
                    if not first:
                        turned(b - 1)
                    dve.wait_ge(sg_ready, b + 1)
                    dve.wait_ge(atp_ready, b)
                    nc.vector.tensor_tensor(a[:, :], sg[:, :], gu[j][:, 1, :], ALU.mult).then_inc(a_ready, 1)
                    if not last:
                        rows(b + 1, 1 - j)
                    if not first:
                        output(b - 1, 1 - j)

                rows(0, 0)
                step(0, 0, True, False)
                with dve.Fori(0, (NB - 3) // 2) as i:
                    for j in range(2):
                        step(i * 2 + j + 1, (j + 1) % 2, False, False)
                step(NB - 2, 1, False, False)
                step(NB - 1, 0, False, True)
                turned(NB - 1)
                output(NB - 1, 0)


class Combine:

    def __init__(self, nc, d, l, ph, lead=0, x2_used=None):
        alone = x2_used is None
        self.nc, self.alone, self.d, self.l, self.lead, self.x2_used = nc, alone, d, l, lead, x2_used
        self.out = d["x2"] if l == 0 else d["out"][0]
        self.norm, self.gain = ph.sb("norm", [P, 2, D]), ph.sb("gain", [P, D])
        self.dest, self.wt = ph.sb("dest", [P, NT, 2], I32), ph.sb("wt", [P, NT, 2])
        self.destb, self.wb = ph.sb("destb", [P, 2, 2], I32), ph.sb("wb", [P, 2, 2])
        self.x1 = ph.sb("x1", [P, 2, D])
        self.y = ph.sb("y", [P, 2, 2, D])
        self.z = ph.sb("z", [P, 2, D]) if alone else self.y[:, :, 0, :]
        self.x2 = ph.sb("x2", [P, 2, D])
        self.stats, self.mv = ph.sb("stats", [P, 2, 6]), ph.sb("mv", [P, 2, 2])
        self.std = ph.sb("std", [P, 2, 3])
        self.nb = ph.sb("nb", [P, 2, 1])
        self.cb_in, self.y0_ready, self.z_ready, self.v_ready, self.std_ready, self.nb_ready, self.xn_ready, self.xg_ready, self.x2_ready = (
            ph.sem(s) for s in ("cb_in", "y0_ready", "z_ready", "v_ready", "std_ready", "nb_ready", "xn_ready", "xg_ready", "x2_ready"))
        self.gained, self.y_used, self.waited = ph.sem("gained"), ph.sem("y_used"), ph.sem("cb_waited")
        self.x1_in, self.stored = ([ph.sem(f"{n}{j}") for j in range(2)] for n in ("x1_in", "stored"))
        self.y_in = d["pool_dma"](f"cb{l}")

    def sync_start(self, sp):
        d = self.d
        sp.dma_start(self.dest[:, :, :].rearrange("p c j -> p (c j)"), d["dest"]).then_inc(self.cb_in, 16)
        sp.dma_start(self.wt[:, :, :].rearrange("p c j -> p (c j)"), d["wt"]).then_inc(self.cb_in, 16)
        load_norm(sp, self.nc, d, self.norm, self.gain, self.l, 1, self.cb_in)

    def sync_stages(self, sp):
        def load(c, j):
            wait_from(sp, self.z_ready, c - 1)
            settle(sp, self.waited)
            sp.dma_start(self.x1[:, j, :], self.d["x1"][ds(c * P, P), :]).then_inc(self.x1_in[j], 16)

        def store(c, j):
            sp.wait_ge(self.x2_ready, c + 1)
            settle(sp, self.waited)
            sp.dma_start(self.out[ds(c * P, P), :], self.x2[:, j, :]).then_inc(self.stored[j], 16)

        return [(load, self.lead + 2), (store, self.lead - 1)]

    def sync_end(self, sp):
        for j in range(2):
            sp.wait_ge(self.stored[j], 16 * NT // 2)

    def pool_stages(self, pool):
        nc = self.nc

        def gather(c, j):
            wait_from(pool, self.y_used if self.alone else self.xg_ready, c - 1)
            nc.gpsimd.tensor_copy(self.destb[:, j, :], self.dest[:, ds(c, 1), :])
            pool.drain()
            for n in range(2):
                nc.gpsimd.indirect_dma_start(out=self.y[:, j, n, :], out_offset=None, in_=self.d["ybuf"],
                                             in_offset=bass.IndirectOffsetOnAxis(ap=self.destb[:, j, n:n + 1], axis=0)).then_inc(self.y_in[j], 16)

        def gamma(c, j):
            pool.wait_ge(self.xn_ready, c + 1)
            wait_from(pool, self.stored[j], 8 * (c - j))
            if self.x2_used:
                wait_from(pool, self.x2_used, c - 1)
            nc.gpsimd.tensor_tensor(self.x2[:, j, :], self.z[:, j, :], self.norm[:, 0, :], ALU.mult).then_inc(self.xg_ready, 1)

        if self.alone:
            return [(gather, self.lead + 2), (gamma, self.lead - 1)]
        return [(gamma, self.lead - 1), (gather, self.lead + 1)]

    def scalar_stages(self, act):
        nc, y, std = self.nc, self.y, self.std

        def first_expert(c, j):
            act.wait_ge(self.y_in[j], 16 * (c - j) + 32)
            nc.scalar.activation(self.wb[:, j, :], self.wt[:, ds(c, 1), :], ACT.Copy)
            act.drain()
            nc.scalar.activation(y[:, j, 0, :], y[:, j, 0, :], ACT.Copy, scale=self.wb[:, j, 0:1]).then_inc(self.y0_ready, 1)

        def root(c, j):
            act.wait_ge(self.v_ready, c + 1)
            nc.scalar.activation(std[:, j, 1:2], std[:, j, 0:1], ACT.Sqrt).then_inc(self.std_ready, 1)

        def normalise(c, j):
            act.wait_ge(self.nb_ready, c + 1)
            nc.scalar.activation(self.z[:, j, :], self.z[:, j, :], ACT.Identity, bias=self.nb[:, j, 0:1], scale=std[:, j, 2:3]).then_inc(self.xn_ready, 1)

        if self.alone:
            return [(root, self.lead), (first_expert, self.lead + 1), (normalise, self.lead)]
        return [(root, self.lead), (normalise, self.lead), (first_expert, self.lead + 1)]

    def vector_start(self, dve):
        dve.wait_ge(self.cb_in, 80)
        self.nc.vector.tensor_scalar(self.gain[:, :], self.gain[:, :], 1.0, None, ALU.add).then_inc(self.gained, 1)
        dve.wait_ge(self.gained, 1)

    def vector_stages(self, dve):
        v, std = self.nc.vector, self.std

        def total(c, j):
            z = self.z[:, j, :]
            dve.wait_ge(self.y0_ready, c + 1)
            if self.alone:
                wait_from(dve, self.xg_ready, c - 1)
            v.scalar_tensor_tensor(z, self.y[:, j, 1, :], self.wb[:, j, 1:2], self.y[:, j, 0, :], ALU.mult, ALU.add).then_inc(self.y_used, 1)
            dve.drain()
            v.tensor_tensor(z, z, self.gain[:, :], ALU.mult)
            dve.drain()
            dve.wait_ge(self.x1_in[j], 8 * (c - j) + 16)
            v.scalar_tensor_tensor(z, self.x1[:, j, :], ALPHA, z, ALU.mult, ALU.add).then_inc(self.z_ready, 1)
            dve.wait_ge(self.z_ready, c + 1)
            for half in range(2):
                v.bn_stats(self.stats[:, half, :], self.z[:, j, half * CH:(half + 1) * CH])
            dve.drain()
            v.bn_aggr(self.mv[:, j, :], self.stats[:, :, :].rearrange("p a b -> p (a b)"))
            dve.drain()
            v.tensor_scalar(std[:, j, 0:1], self.mv[:, j, 1:2], LN_EPS, None, ALU.add).then_inc(self.v_ready, 1)

        def scale(c, j):
            dve.wait_ge(self.std_ready, c + 1)
            v.reciprocal(std[:, j, 2:3], std[:, j, 1:2])
            dve.drain()
            v.tensor_scalar(self.nb[:, j, :], self.mv[:, j, 0:1], std[:, j, 2:3], -1.0, ALU.mult, ALU.mult).then_inc(self.nb_ready, 1)

        def finish(c, j):
            dve.wait_ge(self.xg_ready, c + 1)
            v.tensor_tensor(self.x2[:, j, :], self.x2[:, j, :], self.norm[:, 1, :], ALU.add).then_inc(self.x2_ready, 1)

        sums = [(finish, self.lead - 1), (total, self.lead)]
        return (sums[::-1] if self.alone else sums) + [(scale, self.lead)]


def combine(nc, d, l):
    with Phase(nc, f"cb{l}") as ph:
        cb = Combine(nc, d, l, ph)
        with nc.Block() as block:
            @block.sync
            def _(sp):
                cb.sync_start(sp)
                skewed(sp, cb.sync_stages(sp))
                cb.sync_end(sp)

            @block.gpsimd
            def _(pool):
                pool.wait_ge(cb.cb_in, 80)
                skewed(pool, cb.pool_stages(pool))

            @block.scalar
            def _(act):
                act.wait_ge(cb.cb_in, 80)
                skewed(act, cb.scalar_stages(act))

            @block.vector
            def _(dve):
                cb.vector_start(dve)
                skewed(dve, cb.vector_stages(dve))


def project(nc, d, which):
    first_layer = which == "vo"
    fused, roped_out, modulated = which == "k", which in ("k", "q"), which in ("vo", "q")
    HH = DH // 2
    NBK = 2 * AH * DV // CH if first_layer else G
    WC = NBK * CH
    with Phase(nc, f"p{which}") as ph:
        ws = ph.sb("ws", [P, 2, KD, WC], F32R)
        wst = ph.sb("wst", [P, 2, WC])
        ident = ph.sb("ident", [P, P])
        hT = ph.sb("hT", [P, 2, 2, KD, P], F32R)
        tp = [ph.ps(f"tp{i}", [P, 4, P]) for i in range(2)]
        mm = [ph.ps(f"mm{i}", [P, CH]) for i in range(NBK)]
        (c_in, cols_ready, whi_ready, wlo_ready, tp_ready, full_ready, hi_ready, lo_ready, mm_ready, ev, roped_ready, rt_ready, rT_ready, csb_ready, waited) = (
            ph.sem(s) for s in ("c_in", "cols_ready", "whi_ready", "wlo_ready", "tp_ready", "full_ready", "hi_ready", "lo_ready", "mm_ready", "ev",
                                "roped_ready", "rt_ready", "rT_ready", "csb_ready", "waited"))
        w_in, x_in, st = ([ph.sem(f"{n}{j}") for j in range(2)] for n in ("w_in", "x_in", "st"))
        if modulated:
            cols = ph.sb("cols", [P, 2, KD])
            full = ph.sb("full", [P, KD, P])
        if roped_out:
            cs = ph.sb("cs", [P, 2, NT, HH])
            csb = ph.sb("csb", [P, 2, HH])
            part = ph.sb("part", [P, 4, G, BH, HH])
            roped = ph.sb("roped", [P, G, BH, 2, HH])
            rT = ph.sb("rT", [P, G, 4, P])
            rt = [ph.ps(f"rt{i}", [P, 4, P]) for i in range(G)]
        else:
            vo = ph.sb("vo", [P, 2, NBK, CH])
        cb = Combine(nc, d, 0, ph, lead=3, x2_used=tp_ready) if fused else None
        x = cb.x2 if fused else ph.sb("x", [P, 2, D])
        x_dram = d["x"][0] if first_layer else d["x2"]
        w_dram, col0 = {"vo": (d.get("a_w_in"), 2 * QK), "k": (d.get("b_w_kv"), 0), "v": (d.get("b_w_kv"), QW), "q": (d.get("b_w_q"), 0)}[which]
        w_dram = w_dram if which in ("k", "v") else w_dram[0]
        out_dram = {"vo": "vo", "k": "kT", "v": "v", "q": "qT"}[which]
        full_st = ph.sem("full_st")
        w_rows = w_dram.rearrange("(p k) n -> p k n", k=KD)
        NC_IN = 1 + roped_out + 2 * modulated

        with nc.Block() as block:
            @block.sync
            def _(sp):
                if fused:
                    cb.sync_start(sp)
                sp.dma_start(ident[:, :], d["consts"][:, C_ID:C_ID + P]).then_inc(c_in, 16)
                if roped_out:
                    sp.dma_start(cs[:, :, :, :].rearrange("p a c e -> p (a c e)"), d["cs"]).then_inc(c_in, 16)
                if modulated:
                    load_mod_columns(sp, nc, d, cols, 0 if first_layer else 1, (0, 1), c_in)

                def load(c, j):
                    wait_from(sp, tp_ready, c - 1)
                    settle(sp, waited)
                    sp.dma_start(x[:, j, :], x_dram[ds(c * P, P), :]).then_inc(x_in[j], 16)

                def store(c, j):
                    sp.wait_ge(ev, NBK * c + NBK)
                    settle(sp, waited)
                    sp.dma_start(d[out_dram][ds(c * P, P), :], vo[:, j, :, :].rearrange("p g n -> p (g n)")).then_inc(st[j], 16)

                def store_rows(c, j):
                    sp.wait_ge(full_ready, c + 1)
                    settle(sp, waited)
                    sp.dma_start(d["hT"][:, :, ds(c * P, P)].rearrange("k p t -> p k t"), full[:, :, :]).then_inc(full_st, 16)

                def store_roped(c, j):
                    sp.wait_ge(rT_ready, G * c + G)
                    settle(sp, waited)
                    sp.dma_start(d[out_dram][:, :, ds(c * P, P)].rearrange("g p t -> p g t"),
                                 rT[:, :, :, :].rearrange("p g h t -> p (g h) t")).then_inc(st[0], 16)

                def weights():
                    for k in range(KD):
                        if k >= 2:
                            sp.wait_ge(wlo_ready, k - 1)
                        sp.dma_start(wst[:, k % 2, :], w_rows[:, k, col0:col0 + WC]).then_inc(w_in[k % 2], 16)

                if fused:
                    for c in range(2):
                        cb_load, cb_lead = cb.sync_stages(sp)[0]
                        cb_load(c, c)
                    weights()
                    stages = [(lambda c, j: None if isinstance(c, int) and c < 2 else cb_load(c, j), cb_lead), cb.sync_stages(sp)[1]]
                else:
                    for c in range(2):
                        load(c, c)
                    weights()
                    stages = [(lambda c, j: None if isinstance(c, int) and c < 2 else load(c, j), 3)]
                skewed(sp, stages + ([(store_rows, 1)] if first_layer else []) + [(store_roped, -1) if roped_out else (store, 0)])
                if fused:
                    cb.sync_end(sp)
                if first_layer:
                    sp.wait_ge(full_st, 16 * NT)
                for j in range(1 if roped_out else 2):
                    sp.wait_ge(st[j], 16 * NT if roped_out else 16 * NT // 2)

            @block.tensor
            def _(pe):
                pe.wait_ge(c_in, 16 * NC_IN)

                def transposes(c, j):
                    if fused:
                        pe.wait_ge(cb.x2_ready, c + 1)
                    else:
                        pe.wait_ge(x_in[j], 8 * (c - j) + 16)
                    wait_from(pe, full_ready if modulated else lo_ready, c)
                    for k in range(KD):
                        ins = nc.tensor.transpose(tp[k // 4][:, k % 4, :], x[:, j, k:D:KD], ident[:, :])
                    ins.then_inc(tp_ready, 1)

                def bank(c, j, g):
                    if g == 0:
                        pe.wait_ge(lo_ready, c + 1)
                        pe.wait_ge(hi_ready, c + 1)
                    wait_from(pe, ev, NBK * (c - 1) + g + 1)
                    for k in range(KD):
                        if g == 0 and isinstance(c, int) and c == 0:
                            pe.wait_ge(wlo_ready, k + 1)
                        for n, (a, b) in enumerate(((0, 0), (0, 1), (1, 0))):
                            ins = nc.tensor.matmul(mm[g][:, :], hT[:, j, a, k, :], ws[:, b, k, g * CH:(g + 1) * CH],
                                                   start=(k == 0 and n == 0), stop=(k == KD - 1 and n == 2))
                    ins.then_inc(mm_ready, 1)

                def roped_transposes(c, j):
                    pe.wait_ge(roped_ready, c + 1)
                    wait_from(pe, rT_ready, G * c)
                    for g in range(G):
                        for h in range(4):
                            ins = nc.tensor.transpose(rt[g][:, h, :], roped[:, g, 2 * h:2 * h + 2, :, :].rearrange("p a b e -> p (a b e)"), ident[:, :])
                        ins.then_inc(rt_ready, 1)

                skewed(pe, [(lambda c, j: bank(c, j, 0), 0), (transposes, 1), (lambda c, j: bank(c, j, 1), 0)]
                       + ([(roped_transposes, -1)] if roped_out else []) + [(lambda c, j: bank(c, j, 2), 0)]
                       + ([(lambda c, j: bank(c, j, 3), 0)] if NBK == 4 else []))

            @block.scalar
            def _(act):
                def weights_hi():
                    for k in range(KD):
                        act.wait_ge(w_in[k % 2], 16 * (k // 2 + 1))
                        nc.scalar.activation(ws[:, 0, k, :], wst[:, k % 2, :], ACT.Copy).then_inc(whi_ready, 1)

                def transposed(c, j):
                    act.wait_ge(tp_ready, c + 1)
                    if modulated:
                        wait_from(act, lo_ready, c)
                        if first_layer:
                            wait_from(act, full_st, 16 * c)
                        for k in range(KD):
                            ins = nc.scalar.activation(full[:, k, :], tp[k // 4][:, k % 4, :], ACT.Identity, bias=cols[:, 0, k:k + 1], scale=cols[:, 1, k:k + 1])
                        ins.then_inc(full_ready, 1)
                    else:
                        wait_from(act, mm_ready, NBK * (c - 1))
                        for i in range(2):
                            ins = nc.scalar.activation(hT[:, j, 0, i * 4:(i + 1) * 4, :], tp[i][:, :, :], ACT.Copy)
                        ins.then_inc(hi_ready, 1)

                def turned(c, j):
                    wait_from(act, st[0], 16 * c)
                    for g in range(G):
                        act.wait_ge(rt_ready, G * c + g + 1)
                        nc.scalar.activation(rT[:, g, :, :], rt[g][:, :, :], ACT.Copy).then_inc(rT_ready, 1)

                def values(c, j):
                    wait_from(act, st[j], 8 * (c - j))
                    for g in range(NBK):
                        act.wait_ge(mm_ready, NBK * c + g + 1)
                        gate = first_layer and g >= NBK // 2
                        nc.scalar.activation(vo[:, j, g, :], mm[g][:, :], ACT.Sigmoid if gate else ACT.Copy).then_inc(ev, 1)

                if modulated:
                    act.wait_ge(cols_ready, 1)
                if fused:
                    act.wait_ge(cb.cb_in, 80)
                weights_hi()
                skewed(act, [(transposed, 1)] + (cb.scalar_stages(act) if fused else []) + [(turned, -1) if roped_out else (values, 0)])

            @block.vector
            def _(dve):
                v = nc.vector
                if modulated:
                    dve.wait_ge(c_in, 16 * NC_IN)
                    v.tensor_scalar(cols[:, 1, :], cols[:, 1, :], 1.0, None, ALU.add)
                    dve.drain().then_inc(cols_ready, 1)
                if fused:
                    cb.vector_start(dve)
                if roped_out:
                    dve.wait_ge(c_in, 16 * NC_IN)
                for k in range(KD):
                    dve.wait_ge(whi_ready, k + 1)
                    v.tensor_tensor(ws[:, 1, k, :], wst[:, k % 2, :], ws[:, 0, k, :], ALU.subtract).then_inc(wlo_ready, 1)

                def split(c, j):
                    if modulated:
                        dve.wait_ge(full_ready, c + 1)
                        wait_from(dve, mm_ready, NBK * (c - 1))
                        v.tensor_copy(hT[:, j, 0, :, :], full[:, :, :]).then_inc(hi_ready, 1)
                    else:
                        dve.wait_ge(hi_ready, c + 1)
                        for i in range(2):
                            ins = v.tensor_tensor(hT[:, j, 1, i * 4:(i + 1) * 4, :], tp[i][:, :, :], hT[:, j, 0, i * 4:(i + 1) * 4, :], ALU.subtract)
                        ins.then_inc(lo_ready, 1)

                def rotate(c, j, g):
                    if g == 0:
                        wait_from(dve, roped_ready, c)
                        v.tensor_copy(csb[:, :, :], cs[:, :, ds(c, 1), :]).then_inc(csb_ready, 1)
                        dve.wait_ge(csb_ready, c + 1)
                    sin, cos = (csb[:, a, :].rearrange("p (o e) -> p o e", o=1).to_broadcast([P, BH, HH]) for a in range(2))
                    dve.wait_ge(mm_ready, G * c + g + 1)
                    m = mm[g][:, :].rearrange("p (h a e) -> p h a e", h=BH, a=2)
                    v.tensor_tensor(part[:, 0, g, :, :], m[:, :, 0, :], cos, ALU.mult)
                    v.tensor_tensor(part[:, 1, g, :, :], m[:, :, 1, :], sin, ALU.mult)
                    v.tensor_tensor(part[:, 2, g, :, :], m[:, :, 1, :], cos, ALU.mult)
                    v.tensor_tensor(part[:, 3, g, :, :], m[:, :, 0, :], sin, ALU.mult).then_inc(ev, 1)

                combining = cb.vector_stages(dve) if fused else []
                stages = combining[:1] + [(split, 1)]
                if roped_out:
                    stages += [(lambda c, j: rotate(c, j, 0), 0)] + combining[1:2] + [(lambda c, j: rotate(c, j, 1), 0)] + combining[2:] + [(lambda c, j: rotate(c, j, 2), 0)]
                skewed(dve, stages)

            @block.gpsimd
            def _(pool):
                def lo(c, j):
                    pool.wait_ge(hi_ready, c + 1)
                    nc.gpsimd.tensor_tensor(hT[:, j, 1, :, :], full[:, :, :], hT[:, j, 0, :, :], ALU.subtract).then_inc(lo_ready, 1)

                def rope_sums(c, j):
                    pool.wait_ge(ev, G * c + G)
                    wait_from(pool, rt_ready, G * c)
                    r = roped[:, :, :, :, :].rearrange("p g h a e -> p (g h) a e")
                    q = part[:, :, :, :, :].rearrange("p q g h e -> p q (g h) e")
                    nc.gpsimd.tensor_tensor(r[:, :, 0, :], q[:, 0], q[:, 1], ALU.subtract)
                    nc.gpsimd.tensor_tensor(r[:, :, 1, :], q[:, 2], q[:, 3], ALU.add)
                    pool.drain().then_inc(roped_ready, 1)

                if fused:
                    pool.wait_ge(cb.cb_in, 80)
                stages = (cb.pool_stages(pool) if fused else []) + ([(lo, 1)] if modulated else []) + ([(rope_sums, 0)] if roped_out else [])
                if stages:
                    skewed(pool, stages)


def attention(nc, d):
    NBLK = S // P
    UN = 2 * NBLK
    BODY = 2 * UN
    RS, RT, RB, GRP = 4, 2, 4, 8
    with Phase(nc, "at") as ph:
        ident = ph.sb("ident", [P, P])
        band = ph.sb("band", [P, 2 * P])
        q = ph.sb("q", [P, 2, S])
        k = ph.sb("k", [P, 2, S])
        v = ph.sb("v", [P, 2, NBLK, P])
        o = ph.sb("o", [P, 2, NBLK, 2, DH + 2])
        pr = ph.sb("pr", [P, RB, 2 * P])
        pT = ph.sb("pT", [P, RB, 2 * P])
        bs = [ph.ps(f"bs{i}", [P, 2 * P]) for i in range(RS)]
        bt = [ph.ps(f"bt{i}", [P, 2 * P]) for i in range(RT)]
        bo = [ph.ps(f"bo{i}", [P, GRP // 2, 2, DH]) for i in range(2)]
        (c_in, s_ready, m_ready, p_ready, t_ready, pT_act, pT_dve, pv_ready, o_ready, waited) = (
            ph.sem(s) for s in ("c_in", "s_ready", "m_ready", "p_ready", "t_ready", "pT_act", "pT_dve", "pv_ready", "o_ready", "waited"))
        in_sem, stored, used = ([ph.sem(f"{n}{j}") for j in range(2)] for n in ("in", "stored", "used"))

        def unit(g, u):
            par, j, hh = u // UN, (u % UN) // 2, u % 2
            dil = DILATIONS[g]
            nb = NBLK // dil
            return par, j, hh, j % nb > 0, (j % nb) * P * dil + j // nb, dil

        PIECES = [1 if dil == 1 or dil * P == S else dil for dil in DILATIONS]

        def by_block(a, g):
            dil = DILATIONS[g]
            if dil == 1:
                return [a.rearrange("(j i) c -> i j c", i=P)]
            if dil * P == S:
                return [a.rearrange("(i r) c -> i r c", i=P)]
            pieces = a.rearrange("(n i r) c -> r i n c", i=P, r=dil)
            return [pieces[r] for r in range(dil)]

        def split(a, g):
            n = NBLK // PIECES[g]
            return [a[:, r * n:(r + 1) * n] for r in range(PIECES[g])]

        def loads(g, i):
            return sum((2 + PIECES[h]) * (HP // 2) for h in range(g)) + (2 + PIECES[g]) * (i + 1)

        def stores(g, i):
            return sum(PIECES[h] * (HP // 2) for h in range(g)) + PIECES[g] * i

        def on_act(u):
            return u % 2 == 0

        def evacuated(eng, b, u):
            eng.wait_ge(pT_act if on_act(u) else pT_dve, (BODY // 2) * b + u // 2 + 1)

        def copy_out(u, g, copy):
            n = 2 * P if unit(g, u)[3] else P
            return copy(pT[:, u % RB, 0:n], bt[u % RT][:, 0:n])

        def bodies(eng, body):
            for g in range(G):
                with eng.Fori(0, HP // 2) as i:
                    body(g, i, g * (HP // 2) + i)

        with nc.Block() as block:
            @block.sync
            def _(sp):
                for par in range(2):
                    sp.sem_inc(stored[par], 16)
                sp.dma_start(ident[:, :], d["consts"][:, C_ID:C_ID + P]).then_inc(c_in, 16)
                sp.dma_start(band[:, :], d["consts"][:, C_BAND:C_BAND + 2 * P]).then_inc(c_in, 16)

                def body(g, i, b):
                    for par in range(2):
                        hp = i * 2 + par
                        sp.wait_ge(used[par], b + 1)
                        settle(sp, waited)
                        sp.dma_start(q[:, par, :], d["qT"][ds(g * HP + hp, 1), :, :].rearrange("o p t -> p (o t)")).then_inc(in_sem[par], 16)
                        sp.dma_start(k[:, par, :], d["kT"][ds(g * HP + hp, 1), :, :].rearrange("o p t -> p (o t)")).then_inc(in_sem[par], 16)
                        for dst, src in zip(split(v[:, par, :, :], g), by_block(d["v"][:, ds(g * BW + hp * P, P)], g)):
                            sp.dma_start(dst, src).then_inc(in_sem[par], 16)

                bodies(sp, body)

            @block.tensor
            def _(pe):
                pe.wait_ge(c_in, 32)
                pe.sem_inc(used[0], 1)
                pe.sem_inc(used[1], 1)

                def body(g, i, b):
                    def scores(u):
                        par, j, hh, prev, t0, dil = unit(g, u)
                        if u % UN == 0:
                            pe.wait_ge(in_sem[par], 16 * loads(g, i))
                        if u >= RS:
                            pe.wait_ge(m_ready, BODY * b + u - RS + 1)
                        rows = slice(hh * DH, (hh + 1) * DH)
                        first = t0 - P * dil if prev else t0
                        n = 2 * P if prev else P
                        nc.tensor.matmul(bs[u % RS][:, 0:n], q[rows, par, t0:t0 + (P - 1) * dil + 1:dil], k[rows, par, first:first + (n - 1) * dil + 1:dil],
                                         start=True, stop=True).then_inc(s_ready, 1)

                    def turn(u):
                        prev = unit(g, u)[3]
                        pe.wait_ge(p_ready, BODY * b + u + 1)
                        if u >= RT:
                            evacuated(pe, b, u - RT)
                        for h in range(2 if prev else 1):
                            ins = nc.tensor.transpose(bt[u % RT][:, h * P:(h + 1) * P], pr[:, u % RB, h * P:(h + 1) * P], ident[:, :])
                        ins.then_inc(t_ready, 1)

                    def weigh(u):
                        par, j, hh, prev, t0, dil = unit(g, u)
                        evacuated(pe, b, u)
                        if u % GRP == 0:
                            pe.wait_ge(o_ready, (BODY // GRP) * b + u // GRP + 1)
                        out = bo[(u // GRP) % 2][:, (u % GRP) // 2, hh, :]
                        cols = slice(hh * DH, (hh + 1) * DH)
                        if prev:
                            nc.tensor.matmul(out, pT[:, u % RB, 0:P], v[:, par, j - 1, cols], start=True, stop=False)
                        ins = nc.tensor.matmul(out, pT[:, u % RB, P:2 * P] if prev else pT[:, u % RB, 0:P], v[:, par, j, cols], start=not prev, stop=True)
                        ins.then_inc(pv_ready, 1)
                        if u % UN == UN - 1:
                            pe.wait_ge(pv_ready, BODY * b + u + 1)
                            pe.sem_inc(used[par], 1)

                    scores(0)
                    scores(1)
                    for u in range(BODY):
                        if u + 2 < BODY:
                            scores(u + 2)
                        turn(u)
                        if u:
                            weigh(u - 1)
                    weigh(BODY - 1)

                bodies(pe, body)

            @block.scalar
            def _(act):
                act.sem_inc(o_ready, 2)

                def body(g, i, b):
                    def exp(u):
                        par, j, hh, prev, t0, dil = unit(g, u)
                        n = 2 * P if prev else P
                        act.wait_ge(m_ready, BODY * b + u + 1)
                        nc.scalar.activation(pr[:, u % RB, 0:n], pr[:, u % RB, 0:n], ACT.Exp, scale=-1.0, bias=o[:, par, j, hh, DH:DH + 1],
                                             accum_out=o[:, par, j, hh, DH + 1:DH + 2]).then_inc(p_ready, 1)

                    def output(u):
                        par, j = u // UN, (u % UN) // 2
                        act.wait_ge(pv_ready, BODY * b + u + 1)
                        nc.scalar.activation(o[:, par, j + 1 - GRP // 2:j + 1, :, 0:DH], bo[(u // GRP) % 2][:, :, :, :], ACT.Copy).then_inc(o_ready, 1)
                        if u % UN == UN - 1:
                            act.wait_ge(o_ready, (BODY // GRP) * b + u // GRP + 3)
                            act.wait_ge(p_ready, BODY * b + u + 1)
                            settle(act, waited)
                            src = o[:, par, :, :, :].rearrange("p j h e -> p j (h e)")
                            for s_, t_ in zip(split(src, g), by_block(d["o"][g][:, ds((i * 2 + par) * OW, OW)], g)):
                                act.dma_start(t_, s_).then_inc(stored[par], 16)

                    exp(0)
                    for u in range(BODY):
                        if u + 1 < BODY:
                            exp(u + 1)
                        if on_act(u):
                            act.wait_ge(t_ready, BODY * b + u + 1)
                            if u >= RB:
                                act.wait_ge(pv_ready, BODY * b + u - RB + 1)
                            copy_out(u, g, lambda dst, src: nc.scalar.activation(dst, src, ACT.Copy)).then_inc(pT_act, 1)
                        if u % GRP == 1 and u > 1:
                            output(u - 2)
                    output(BODY - 1)

                bodies(act, body)
                for par in range(2):
                    act.wait_ge(stored[par], 16 * sum(PIECES[g] * (HP // 2) for g in range(G)) + 16)

            @block.vector
            def _(dve):
                dve.wait_ge(c_in, 32)

                def body(g, i, b):
                    def mask(u):
                        par, j, hh, prev, t0, dil = unit(g, u)
                        n = 2 * P if prev else P
                        if u % UN == 0:
                            dve.wait_ge(stored[par], 16 * stores(g, i) + 16)
                        dve.wait_ge(s_ready, BODY * b + u + 1)
                        if u >= RB:
                            dve.wait_ge(t_ready, BODY * b + u - RB + 1)
                        settle(dve, waited)
                        nc.vector.tensor_tensor_reduce(out=pr[:, u % RB, 0:n], in0=bs[u % RS][:, 0:n], in1=band[:, 2 * P - n:2 * P], scale=-DH ** -0.5,
                                                       scalar=3e38, op0=ALU.add, op1=ALU.min, accum_out=o[:, par, j, hh, DH:DH + 1]).then_inc(m_ready, 1)

                    mask(0)
                    mask(1)
                    for u in range(BODY):
                        if u + 2 < BODY:
                            mask(u + 2)
                        if not on_act(u):
                            dve.wait_ge(t_ready, BODY * b + u + 1)
                            if u >= RB:
                                dve.wait_ge(pv_ready, BODY * b + u - RB + 1)
                            copy_out(u, g, nc.vector.tensor_copy).then_inc(pT_dve, 1)

                bodies(dve, body)


def trunk(nc, d):
    pool_dma = {n: [nc.semaphore(f"{n}_pool_dma{j}").__enter__() for j in range(2)] for n in ("rt0", "rt1", "ex0", "ex1", "cb0", "cb1")}
    d["pool_dma"] = pool_dma.__getitem__
    modulation(nc, d)
    project(nc, d, "vo")
    project_qk(nc, d)
    gate_rows(nc, d)
    mlstm(nc, d)
    for l in range(DEPTH):
        if l == 1:
            project(nc, d, "k")
            project(nc, d, "v")
            project(nc, d, "q")
            attention(nc, d)
        after_mixer(nc, d, l)
        route(nc, d, l)
        experts(nc, d, l)
    combine(nc, d, DEPTH - 1)


SCRATCH = {
    "mod": ((DEPTH, 6 * D), F32),
    "hT": ((KD, P, S), F32),
    "qkT": ((2 * AH, DQK, S), F32), "vo": ((S, 2 * AH * DV), F32), "gates": ((2, AH, S), F32),
    "rowbm": ((AH, S), F32), "colq": ((P, NT * NQT * AH), F32), "decay": ((P, 2 * AH * NT), F32),
    "y": ((S, D), F32), "x1": ((S, D), F32), "x2": ((S, D), F32), "lg": ((S, NR), F32),
    "slot_tok": ((NBP * P, 1), I32), "dest": ((P, 2 * NT), I32), "wt": ((P, 2 * NT), F32), "block_e": ((1, NBP), I32),
    "ybuf": ((NB * P, D), F32),
    "kT": ((G * HP, P, S), F32), "qT": ((G * HP, P, S), F32), "cs": ((P, NT * DH), F32), "v": ((S, QW), F32), "o": ((G, S, HP * OW), F32),
}


_INS = ["x", "c", "positions", "ada_w", "ada_b", "ln_g", "ln_b", "a_w_in", "a_b_gate", "a_norm_g", "a_w_out", "b_w_kv", "b_w_q", "b_w_o",
        "moe_w_r1", "moe_b_r1", "moe_w_r2", "moe_b_r2", "moe_w_gate", "moe_w_up", "moe_w_down"]


def kernel(**inputs):
    import numpy as _np
    import concourse.bacc as _bacc
    from concourse import mybir as _mybir
    from concourse.bass_utils import run_bass_kernel_spmd as _run

    nc = _bacc.Bacc("TRN2", target_bir_lowering=False, num_devices=1)
    arrays, d = {}, {}
    for name in _INS + ["consts"]:
        a = constant_table() if name == "consts" else _np.ascontiguousarray(inputs[name])
        arrays[f"in_{name}_dram"] = a
        d[name] = nc.dram_tensor(f"in_{name}_dram", a.shape, _mybir.dt.from_np(a.dtype), kind="ExternalInput").ap()
    d["out"] = nc.dram_tensor("out_0_dram", (1, S, D), F32, kind="ExternalOutput").ap()
    for name, (shape, dtype) in SCRATCH.items():
        d[name] = nc.dram_tensor(f"{name}_scratch", shape, dtype, kind="Internal").ap()
    trunk(nc, d)
    r = _run(nc, [arrays], core_ids=[0])
    return r.results[0]["out_0_dram"]
```

```python
from contextlib import ExitStack

import numpy as np

import concourse.bass as bass
from concourse import mybir

F32 = mybir.dt.float32
F32R = mybir.dt.float32r
I32 = mybir.dt.int32
U32 = mybir.dt.uint32
ALU = mybir.AluOpType
ACT = mybir.ActivationFunctionType
AX_X = mybir.AxisListType.X
ds = bass.ds

P = 128
D = 1024
S = 2048
DEPTH = 2
NT = S // P
KD = D // P
ALPHA = (2.0 * DEPTH) ** 0.25
LN_EPS = 1e-5
AH, DQK, DV = 4, D // 8, D // 4
A_NORM_EPS = 1e-6
QK = AH * DQK
A_PROJ = 2 * QK + 2 * AH * DV + 2 * AH
WINDOWS, DILATIONS = (128, 512, 2048), (1, 4, 16)
assert all(w // dil == P for w, dil in zip(WINDOWS, DILATIONS))
G, BH, DH = 3, 8, 64
BW = BH * DH
QW = G * BW
HP = BH // 2
OW = 2 * (DH + 2)
MG, ME = 4, 8
NE = MG * ME
NR = MG + NE
HID = D // 4
NB = (2 * S + NE * (P - 1)) // P
NBP = 64
MACRO = 512
CH = 512
NEG = -1e30

C_ID, C_CAUSAL, C_BEFORE, C_ONES, C_BAND = 0, 128, 256, 384, 512
C_EXP, C_BLK, C_FREQ, C_SEL, C_TOK = 768, 800, 864, 896, 896 + AH * P
C_ROW = C_TOK + NT
C_END = C_ROW + P


def constant_table():
    t = np.zeros((P, C_END), np.float32)
    i = np.arange(P)
    t[:, C_ID:C_ID + P] = np.eye(P)
    t[:, C_CAUSAL:C_CAUSAL + P] = np.where(i[:, None] <= i[None, :], 0.0, NEG)
    t[:, C_BEFORE:C_BEFORE + P] = i[:, None] < i[None, :]
    t[:, C_ONES:C_ONES + P] = 1.0
    kj = np.arange(2 * P)
    t[:, C_BAND:C_BAND + 2 * P] = np.where((kj >= i[:, None]) & (kj <= i[:, None] + P), 0.0, NEG)
    t[:, C_EXP:C_EXP + NE] = np.arange(NE)
    t[:, C_BLK:C_BLK + NBP] = np.arange(NBP) * P
    t[:, C_FREQ:C_FREQ + DH // 2] = np.power(10000.0, -np.arange(DH // 2) * 2.0 / DH)
    for h in range(AH):
        t[h, C_SEL + h * P:C_SEL + (h + 1) * P] = 1.0
    t[:, C_TOK:C_TOK + NT] = i[:, None] + P * np.arange(NT)[None, :]
    t[:, C_ROW:C_ROW + P] = i
    return t


def settle(eng, waited):
    eng.sem_inc(waited, 1)


def wait_from(eng, sem, count):
    if not (isinstance(count, int) and count <= 0):
        eng.wait_ge(sem, count)


def skewed(eng, stages):
    most, least = max(lead for _, lead in stages), min(lead for _, lead in stages)
    first = 2 - least + (least % 2)
    last = NT - most - (NT - most - first) % 2

    def step(i, parity, whole):
        for stage, lead in stages:
            if whole or 0 <= i + lead < NT:
                stage(i + lead, (parity + lead) % 2)

    for i in range(-most, first):
        step(i, i % 2, False)
    with eng.Fori(0, (last - first) // 2) as n:
        for j in range(2):
            step(n * 2 + first + j, j, True)
    for i in range(last, NT - least):
        step(i, i % 2, False)


class Phase:

    def __init__(self, nc, name):
        self.nc, self.name, self.stack, self.sems = nc, name, ExitStack(), []

    def sb(self, name, shape, dtype=F32):
        return self.stack.enter_context(self.nc.sbuf_tensor(f"{self.name}_{name}", shape, dtype))

    def ps(self, name, shape, dtype=F32):
        return self.stack.enter_context(self.nc.psum_tensor(f"{self.name}_{name}", shape, dtype))

    def sem(self, name):
        s = self.stack.enter_context(self.nc.semaphore(f"{self.name}_{name}"))
        self.sems.append(s.num)
        return s

    def __enter__(self):
        self.stack.__enter__()
        return self

    def __exit__(self, *e):
        if e[0] is None:
            self.nc.all_engine_barrier(sems_to_clear=range(min(self.sems), max(self.sems) + 1))
        return self.stack.__exit__(*e)


TWO_PI = 2.0 * np.pi
PI_HI = 6.28125
PI_MID = float(np.round((TWO_PI - PI_HI) * 2 ** 20) / 2 ** 20)
PI_LO = float(TWO_PI - PI_HI - PI_MID)
ROUND = 1.5 * 2.0 ** 23


class RopeTables:

    def __init__(self, nc, d, ph):
        HH = DH // 2
        self.nc, self.d = nc, d
        self.pos, self.posf = ph.sb("pos", [P, NT], I32), ph.sb("posf", [P, NT])
        self.freq = ph.sb("freq", [P, HH])
        self.ang = ph.sb("ang", [P, NT, HH])
        self.turns = ph.sb("turns", [P, 2, NT, HH])
        self.cs = ph.sb("cs", [P, 2, NT, HH])
        self.p_in, self.r_ready, self.cs_ready, self.cs_stored = ph.sem("p_in"), ph.sem("r_ready"), ph.sem("cs_ready"), ph.sem("cs_stored")

    def load(self, sp):
        d = self.d
        sp.dma_start(self.pos[:, :], d["positions"].rearrange("b (c p) -> p (b c)", p=P), allow_slow_non_contiguous=True).then_inc(self.p_in, 16)
        sp.dma_start(self.freq[:, :], d["consts"][:, C_FREQ:C_FREQ + DH // 2]).then_inc(self.p_in, 16)

    def finish(self, sp):
        sp.wait_ge(self.cs_ready, 1)
        sp.dma_start(self.d["cs"], self.cs[:, :, :, :].rearrange("p a c e -> p (a c e)")).then_inc(self.cs_stored, 16)
        sp.wait_ge(self.cs_stored, 16)

    def sines(self, act):
        act.wait_ge(self.r_ready, 1)
        self.nc.scalar.activation(self.cs[:, :, :, :], self.turns[:, :, :, :], ACT.Sin).then_inc(self.cs_ready, 1)

    def angles(self, dve):
        v, ang, turns, rem = self.nc.vector, self.ang, self.turns, self.cs
        dve.wait_ge(self.p_in, 32)
        v.tensor_copy(self.posf[:, :], self.pos[:, :])
        dve.drain()
        for c in range(NT):
            v.tensor_scalar(ang[:, c, :], self.freq[:, :], self.posf[:, c:c + 1], None, ALU.mult)
        dve.drain()
        v.tensor_scalar(turns[:, 0, :, :], ang[:, :, :], 1.0 / TWO_PI, None, ALU.mult)
        v.tensor_scalar(turns[:, 1, :, :], ang[:, :, :], 1.0 / TWO_PI, 0.25, ALU.mult, ALU.add)
        dve.drain()
        v.tensor_scalar(turns[:, :, :, :], turns[:, :, :, :], ROUND, None, ALU.add)
        dve.drain()
        v.tensor_scalar(turns[:, :, :, :], turns[:, :, :, :], ROUND, None, ALU.subtract)
        dve.drain()
        for n, piece in enumerate((PI_HI, PI_MID, PI_LO)):
            for j in range(2):
                v.scalar_tensor_tensor(rem[:, j, :, :], turns[:, j, :, :], -piece, ang[:, :, :] if n == 0 else rem[:, j, :, :], ALU.mult, ALU.add)
            dve.drain()
        v.tensor_scalar(rem[:, 1, :, :], rem[:, 1, :, :], np.pi / 2, None, ALU.add)
        dve.drain()
        lim = 3.1415925
        v.tensor_scalar(turns[:, :, :, :], rem[:, :, :, :], lim, -lim, ALU.min, ALU.max)
        dve.drain().then_inc(self.r_ready, 1)


def modulation(nc, d):
    NCH = 6 * D // CH
    WB, KP = 4, KD // 2
    with Phase(nc, "mod") as ph:
        c_sb = ph.sb("c", [P, KD])
        cond = ph.sb("cond", [P, KD])
        ones = ph.sb("ones", [P, 1])
        w = ph.sb("w", [P, WB, KD, CH])
        b = ph.sb("b", [1, WB, CH])
        part = ph.sb("part", [P, 2, CH])
        row = ph.sb("row", [1, 2, CH])
        acc = [ph.ps(f"acc{j}", [P, CH]) for j in range(2)]
        c_in, cond_ready, part_ready = ph.sem("c_in"), ph.sem("cond_ready"), ph.sem("part_ready")
        w_in = [ph.sem(f"w_in{j}") for j in range(WB)]
        acc_ready, row_ready = ph.sem("acc_ready"), ph.sem("row_ready")
        stored, waited = [ph.sem(f"stored{j}") for j in range(2)], ph.sem("waited")
        w_dram = d["ada_w"][0].rearrange("(p k) n -> p k n", k=KD)
        tables = RopeTables(nc, d, ph)

        def chunks(eng, step):
            with eng.Fori(0, NCH // WB) as i:
                for j in range(WB):
                    step(i * WB + j, j)

        with nc.Block() as block:
            @block.sync
            def _(sp):
                sp.dma_start(c_sb[:, :], d["c"].rearrange("b (p k) -> (b p) k", k=KD)).then_inc(c_in, 16)
                tables.load(sp)
                sp.sem_inc(row_ready, WB)

                def step(n, j):
                    sp.wait_ge(row_ready, n + 1)
                    sp.dma_start(w[:, j, :, :], w_dram[:, :, ds(n * CH, CH)]).then_inc(w_in[j], 16)
                    sp.dma_start(b[:, j, :], d["ada_b"][0:1, ds(n * CH, CH)]).then_inc(w_in[j], 16)

                chunks(sp, step)
                tables.finish(sp)

            @block.scalar
            def _(act):
                act.wait_ge(c_in, 16)
                nc.scalar.activation(cond[:, :], c_sb[:, :], ACT.Silu).then_inc(cond_ready, 1)
                tables.sines(act)

                def step(n, j):
                    act.wait_ge(row_ready, n + (WB + 1))
                    settle(act, waited)
                    act.dma_start(d["mod"][0:1, ds(n * CH, CH)], row[:, j % 2, :]).then_inc(stored[j % 2], 16)

                chunks(act, step)
                for j in range(2):
                    act.wait_ge(stored[j], 16 * NCH // 2 + 16)

            @block.tensor
            def _(pe):
                pe.wait_ge(cond_ready, 1)

                def step(n, j):
                    pe.wait_ge(w_in[j], (n - j) * (32 // WB) + 32)
                    pe.wait_ge(row_ready, n + (WB - 1))
                    out = acc[j % 2][0:1, :]
                    for k in range(KP):
                        nc.tensor.matmul(out, cond[:, k:k + 1], w[:, j, k, :], start=(k == 0), stop=False)
                    pe.wait_ge(part_ready, n + 2)
                    nc.tensor.matmul(out, ones[:, :], part[:, j % 2, :], start=False, stop=True).then_inc(acc_ready, 1)

                chunks(pe, step)

            @block.vector
            def _(dve):
                for j in range(2):
                    dve.sem_inc(stored[j], 16)
                nc.vector.memset(ones[:, :], 1.0)
                dve.drain().then_inc(part_ready, 1)
                tables.angles(dve)
                dve.wait_ge(cond_ready, 1)

                def step(n, j):
                    dve.wait_ge(w_in[j], (n - j) * (32 // WB) + 32)
                    for k in range(KP, KD):
                        last, out = k == KD - 1, part[:, j % 2, :]
                        if k == KP:
                            ins = nc.vector.tensor_scalar(out, w[:, j, k, :], cond[:, k:k + 1], None, ALU.mult)
                        else:
                            ins = nc.vector.scalar_tensor_tensor(out, w[:, j, k, :], cond[:, k:k + 1], out, ALU.mult, ALU.add)
                        if last:
                            ins.then_inc(part_ready, 1)
                        else:
                            dve.drain()
                    dve.wait_ge(acc_ready, n + 1)
                    dve.wait_ge(stored[j % 2], 8 * (n - j % 2) + 16)
                    nc.vector.tensor_tensor(row[:, j % 2, :], acc[j % 2][0:1, :], b[:, j, :], ALU.add).then_inc(row_ready, 1)

                chunks(dve, step)


def load_mod_columns(eng, nc, d, cols, l, kinds, sem):
    for j, kind in enumerate(kinds):
        eng.dma_start(cols[:, j, :], d["mod"][l, kind * D:(kind + 1) * D].rearrange("(p k) -> p k", k=KD)).then_inc(sem, 16)


def project_qk(nc, d):
    NM = S // MACRO
    NGT = 2 * AH
    WC = 2 * QK + NGT
    RING = AH
    with Phase(nc, "pqk") as ph:
        wst = ph.sb("wst", [P, KD, WC])
        ws = ph.sb("ws", [P, 2, KD, WC], F32R)
        bias = ph.sb("bias", [NGT, 1])
        full = ph.sb("full", [P, KD, MACRO])
        hT = ph.sb("hT", [P, 2, 2, KD, MACRO], F32R)
        out = ph.sb("out", [P, 2 * AH, MACRO])
        gates = ph.sb("gates", [NGT, MACRO])
        mm = [ph.ps(f"mm{i}", [P, MACRO]) for i in range(RING)]
        gt = ph.ps("gt", [P, MACRO])
        whi_ready, wlo_ready, mm_ready, q_ev, k_ev, g_ev, g_done = (
            ph.sem(s) for s in ("whi_ready", "wlo_ready", "mm_ready", "q_ev", "k_ev", "g_ev", "g_done"))
        b_in, st_q, st_k, st_g, waited = (ph.sem(s) for s in ("b_in", "st_q", "st_k", "st_g", "waited"))
        WK = 2
        NP = KD // WK
        wq_in, wk_in = [ph.sem(f"wq_in{g}") for g in range(NP)], [ph.sem(f"wk_in{g}") for g in range(NP)]
        h_in, hi_ready, lo_ready = ph.sem("h_in"), ph.sem("hi_ready"), ph.sem("lo_ready")
        w_dram = d["a_w_in"][0].rearrange("(p k) n -> p k n", k=KD)

        def macros(eng, step):
            step(0, 0)
            with eng.Fori(0, NM // 2 - 1) as i:
                for j in range(2):
                    step(i * 2 + j + 1, 1 - j)
            step(NM - 1, 1)

        with nc.Block() as block:
            @block.sync
            def _(sp):
                for g, k in enumerate(range(0, KD, WK)):
                    sp.dma_start(wst[:, k:k + WK, 0:QK], w_dram[:, k:k + WK, 0:QK]).then_inc(wq_in[g], 16)
                for g, k in enumerate(range(0, KD, WK)):
                    sp.dma_start(wst[:, k:k + WK, QK:2 * QK], w_dram[:, k:k + WK, QK:2 * QK]).then_inc(wk_in[g], 16)
                    sp.dma_start(wst[:, k:k + WK, 2 * QK:WC], w_dram[:, k:k + WK, A_PROJ - NGT:A_PROJ]).then_inc(wk_in[g], 16)
                sp.dma_start(bias[:, :], d["a_b_gate"][0].rearrange("(h o) -> h o", o=1)).then_inc(b_in, 16)

                def store(m, j):
                    tok = ds(m * MACRO, MACRO)
                    sp.wait_ge(q_ev, AH * m + AH)
                    settle(sp, waited)
                    sp.dma_start(d["qkT"][0:AH, :, tok].rearrange("h p t -> p h t"), out[:, 0:AH, :]).then_inc(st_q, 16)
                    sp.wait_ge(k_ev, AH * m + AH)
                    settle(sp, waited)
                    sp.dma_start(d["qkT"][AH:2 * AH, :, tok].rearrange("h p t -> p h t"), out[:, AH:2 * AH, :]).then_inc(st_k, 16)
                    sp.wait_ge(g_ev, m + 1)
                    settle(sp, waited)
                    sp.dma_start(d["gates"].rearrange("g h t -> (g h) t")[:, tok], gates[:, :]).then_inc(st_g, 16)

                macros(sp, store)
                for s in (st_q, st_k, st_g):
                    sp.wait_ge(s, 16 * NM)

            @block.tensor
            def _(pe):
                def product(out_bank, cols, j, pieces=None):
                    for k in range(KD):
                        if pieces is not None and k % WK == 0:
                            pe.wait_ge(wlo_ready, pieces + k // WK + 1)
                        for n, (a, b) in enumerate(((0, 0), (0, 1), (1, 0))):
                            ins = nc.tensor.matmul(out_bank, ws[:, b, k, cols], hT[:, j, a, k, :], start=(k == 0 and n == 0), stop=(k == KD - 1 and n == 2))
                    return ins

                def step(m, j):
                    pe.wait_ge(hi_ready, m + 1)
                    pe.wait_ge(lo_ready, m + 1)
                    for h in range(2 * AH):
                        if h < AH:
                            wait_from(pe, k_ev, AH * (m - 1) + h + 1)
                        else:
                            pe.wait_ge(q_ev, AH * m + h - AH + 1)
                        product(mm[h % RING][:, :], slice(h * P, (h + 1) * P), j, h // AH * NP if isinstance(m, int) and m == 0 and h % AH == 0 else None).then_inc(mm_ready, 1)
                    wait_from(pe, g_ev, m)
                    product(gt[0:NGT, :], slice(2 * QK, WC), j).then_inc(g_done, 1)

                macros(pe, step)

            @block.scalar
            def _(act):


                def rows_hi(m, j):
                    act.wait_ge(h_in, 16 * m + 16)
                    wait_from(act, g_done, m - 1)
                    nc.scalar.activation(hT[:, j, 0, :, :], full[:, :, :], ACT.Copy).then_inc(hi_ready, 1)

                def load(m):
                    act.dma_start(full[:, :, :], d["hT"][:, :, ds(m * MACRO, MACRO)].rearrange("k p t -> p k t")).then_inc(h_in, 16)

                load(0)
                for g in range(NP):
                    act.wait_ge(wq_in[g], 16)
                    rows = slice(g * WK, (g + 1) * WK)
                    nc.scalar.activation(ws[:, 0, rows, 0:QK], wst[:, rows, 0:QK], ACT.Copy).then_inc(whi_ready, 1)
                rows_hi(0, 0)
                for g in range(NP):
                    act.wait_ge(wk_in[g], 32)
                    rows = slice(g * WK, (g + 1) * WK)
                    nc.scalar.activation(ws[:, 0, rows, QK:WC], wst[:, rows, QK:WC], ACT.Copy).then_inc(whi_ready, 1)

                def step(m, j):
                    if not (isinstance(m, int) and m == NM - 1):
                        act.wait_ge(lo_ready, m + 1)
                        settle(act, waited)
                        load(m + 1)
                        rows_hi(m + 1, 1 - j)
                    for h in range(AH):
                        act.wait_ge(mm_ready, 2 * AH * m + h + 1)
                        if h == 0:
                            wait_from(act, st_q, 16 * m)
                        nc.scalar.activation(out[:, h, :], mm[h][:, :], ACT.Copy).then_inc(q_ev, 1)

                macros(act, step)

            @block.vector
            def _(dve):
                def weights_lo(cut, before):
                    for g in range(NP):
                        dve.wait_ge(whi_ready, before + g + 1)
                        rows = slice(g * WK, (g + 1) * WK)
                        nc.vector.tensor_tensor(ws[:, 1, rows, cut], wst[:, rows, cut], ws[:, 0, rows, cut], ALU.subtract).then_inc(wlo_ready, 1)

                def rows_lo(m, j):
                    dve.wait_ge(hi_ready, m + 1)
                    nc.vector.tensor_tensor(hT[:, j, 1, :, :], full[:, :, :], hT[:, j, 0, :, :], ALU.subtract).then_inc(lo_ready, 1)

                weights_lo(slice(0, QK), 0)
                rows_lo(0, 0)
                weights_lo(slice(QK, WC), NP)
                dve.wait_ge(b_in, 16)

                def step(m, j):
                    if not (isinstance(m, int) and m == NM - 1):
                        rows_lo(m + 1, 1 - j)
                    for h in range(AH):
                        dve.wait_ge(mm_ready, 2 * AH * m + AH + h + 1)
                        if h == 0:
                            wait_from(dve, st_k, 16 * m)
                        nc.vector.tensor_scalar(out[:, AH + h, :], mm[h][:, :], DQK ** -0.5, None, ALU.mult).then_inc(k_ev, 1)
                    dve.wait_ge(g_done, m + 1)
                    wait_from(dve, st_g, 16 * m)
                    nc.vector.tensor_scalar(gates[:, :], gt[0:NGT, :], bias[:, 0:1], None, ALU.add).then_inc(g_ev, 1)

                macros(dve, step)


QU, QEM, QWS = range(3)
NQT = 3


def gate_rows(nc, d):
    with Phase(nc, "gr") as ph:
        raw = ph.sb("raw", [AH, 2, S])
        t0 = ph.sb("t0", [AH, S])
        t1 = ph.sb("t1", [AH, S])
        lf = ph.sb("lf", [AH, S])
        keep = ph.sb("keep", [AH, S])
        b = ph.sb("b", [AH, S])
        m = ph.sb("m", [AH, S])
        rowbm = ph.sb("rowbm", [AH, S])
        u = ph.sb("u", [AH, S])
        small = ph.sb("small", [AH, 4, NT])
        quant = ph.sb("quant", [P, S])
        ident = ph.sb("ident", [P, P])
        sel = ph.sb("sel", [AH, AH, P])
        colq = ph.sb("colq", [P, NT, NQT, AH])
        decay = ph.sb("decay", [P, 2, AH, NT])
        tp = [ph.ps(f"tp{j}", [P, 4, P]) for j in range(4)]
        dc = ph.ps("dc", [P, 2, AH, NT])
        g_in, c_in, out_done = ph.sem("g_in"), ph.sem("c_in"), ph.sem("out_done")
        dve_done, act_done, pe_done, rows_ready = ph.sem("dve_done"), ph.sem("act_done"), ph.sem("pe_done"), ph.sem("rows_ready")
        cols_done = ph.sem("cols_done")

        def chunks(a):
            return a.rearrange("h (c t) -> h c t", t=P)

        with nc.Block() as block:
            @block.sync
            def _(sp):
                sp.dma_start(raw[:, :, :], d["gates"].rearrange("g h t -> h g t")).then_inc(g_in, 16)
                sp.dma_start(ident[:, :], d["consts"][:, C_ID:C_ID + P]).then_inc(c_in, 16)
                sp.dma_start(sel[:, :, :], d["consts"][0:AH, C_SEL:C_SEL + AH * P].rearrange("k (h p) -> k h p", h=AH)).then_inc(c_in, 16)
                sp.wait_ge(rows_ready, 1)
                sp.dma_start(d["rowbm"], rowbm[:, :]).then_inc(out_done, 16)
                sp.wait_ge(cols_done, 1)
                sp.dma_start(d["colq"], colq[:, :, :, :].rearrange("p c q h -> p (c q h)")).then_inc(out_done, 16)
                sp.dma_start(d["decay"], decay[:, :, :, :].rearrange("p a h c -> p (a h c)")).then_inc(out_done, 16)
                sp.wait_ge(out_done, 48)

            @block.scalar
            def _(act):
                act.wait_ge(g_in, 16)
                nc.scalar.activation(t0[:, :], raw[:, 1, :], ACT.Abs)
                act.drain()
                nc.scalar.activation(t0[:, :], t0[:, :], ACT.Exp, scale=-1.0)
                act.drain()
                nc.scalar.activation(t1[:, :], t0[:, :], ACT.Ln, bias=1.0).then_inc(act_done, 1)
                act.wait_ge(dve_done, 1)
                nc.scalar.activation(quant[0:AH, :], u[:, :], ACT.Copy)
                nc.scalar.activation(quant[32:32 + AH, :], m[:, :], ACT.Exp, scale=-1.0)
                act.wait_ge(dve_done, 2)
                nc.scalar.activation(quant[64:64 + AH, :], t1[:, :], ACT.Exp)
                nc.scalar.activation(small[:, 3, :], small[:, 1, :], ACT.Exp)
                act.drain().then_inc(rows_ready, 1)

            @block.vector
            def _(dve):
                nc.vector.memset(quant[:, :], 0.0)
                nc.vector.memset(keep[:, :], 1.0)
                dve.drain()
                nc.vector.memset(chunks(keep[:, :])[:, :, 0:1], 0.0)
                dve.wait_ge(g_in, 16)
                nc.vector.tensor_scalar(lf[:, :], raw[:, 1, :], 0.0, None, ALU.min)
                dve.drain()
                dve.wait_ge(act_done, 1)
                nc.vector.tensor_tensor(lf[:, :], lf[:, :], t1[:, :], ALU.subtract)
                dve.drain()
                nc.vector.tensor_tensor_scan(b[:, :], keep[:, :], lf[:, :], 0.0, ALU.mult, ALU.add)
                nc.vector.tensor_tensor_scan(m[:, :], lf[:, :], raw[:, 0, :], 0.0, ALU.add, ALU.max)
                nc.vector.memset(small[:, 0, 0:1], 0.0)
                dve.drain()
                nc.vector.tensor_tensor(u[:, :], raw[:, 0, :], b[:, :], ALU.subtract)
                nc.vector.tensor_tensor(rowbm[:, :], b[:, :], m[:, :], ALU.subtract)
                nc.vector.tensor_copy(small[:, 0, 1:NT], chunks(m[:, :])[:, 0:NT - 1, P - 1])
                dve.drain().then_inc(dve_done, 1)
                bm_last = chunks(rowbm[:, :])[:, :, P - 1:P]
                nc.vector.tensor_tensor(chunks(t0[:, :]), chunks(rowbm[:, :]), small[:, 0, :].rearrange("h (c o) -> h c o", o=1).to_broadcast([AH, NT, P]), ALU.add)
                nc.vector.tensor_tensor(chunks(t1[:, :]), chunks(u[:, :]), bm_last.to_broadcast([AH, NT, P]), ALU.add)
                dve.drain()
                nc.vector.tensor_copy(small[:, 1, :], chunks(t0[:, :])[:, :, P - 1])
                dve.drain().then_inc(dve_done, 1)
                for c in range(NT):
                    dve.wait_ge(pe_done, c + 1)
                    q = tp[c % 4][:, 0, :].rearrange("p (q h) -> p q h", q=4)[:, 0:NQT, 0:AH]
                    nc.vector.tensor_copy(colq[:, c, :, :], q).then_inc(dve_done, 1)
                dve.wait_ge(pe_done, NT + 1)
                nc.vector.tensor_copy(decay[:, :, :, :], dc[:, :, :, :])
                dve.drain().then_inc(cols_done, 1)

            @block.tensor
            def _(pe):
                pe.wait_ge(c_in, 32)
                pe.wait_ge(rows_ready, 1)
                for c in range(NT):
                    if c >= 4:
                        pe.wait_ge(dve_done, 2 + c - 3)
                    nc.tensor.transpose(tp[c % 4][:, 0, :], quant[:, c * P:(c + 1) * P], ident[:, :]).then_inc(pe_done, 1)
                for h in range(AH):
                    nc.tensor.matmul(dc[:, 0, h, :], sel[:, h, :], small[:, 0, :], start=True, stop=True)
                    ins = nc.tensor.matmul(dc[:, 1, h, :], sel[:, h, :], small[:, 3, :], start=True, stop=True)
                ins.then_inc(pe_done, 1)


def mlstm(nc, d):
    with Phase(nc, "ml") as ph:
        q = ph.sb("q", [P, 2, AH, P])
        kT = ph.sb("kT", [P, 2, AH, P])
        v = ph.sb("v", [P, 2, AH, DV])
        og = ph.sb("og", [P, 2, D])
        y = ph.sb("y", [P, 2, D])
        rowbm = ph.sb("rowbm", [AH, S])
        colq = ph.sb("colq", [P, NT, NQT, AH])
        decay = ph.sb("decay", [P, 2, AH, NT])
        cq = ph.sb("cq", [P, 2, NQT, AH])
        dk = ph.sb("dk", [P, 2, 2, AH])
        sel = ph.sb("sel", [AH, AH, P])
        ident = ph.sb("ident", [P, P])
        causal = ph.sb("causal", [P, P])
        ng = ph.sb("ng", [P, D])
        ones = ph.sb("ones", [P, 1])
        dw = ph.sb("dw", [P, AH, P])
        iwb = ph.sb("iwb", [P, AH, P])
        sc = ph.sb("sc", [P, 2, AH, P])
        qs = ph.sb("qs", [P, 2, AH, P])
        kw = ph.sb("kw", [P, 2, AH, P])
        C = ph.sb("C", [P, AH, DV])
        n = ph.sb("n", [P, AH])
        den = ph.sb("den", [P, AH])
        rden = ph.sb("rden", [P, 2, AH])
        ht = ph.sb("ht", [P, 2, AH, DV])
        stats = ph.sb("stats", [P, AH, 6])
        mv = ph.sb("mv", [P, 2, AH, 2])
        std = ph.sb("std", [P, 2, 3, AH])
        bS, bR, bK, bD = ph.ps("bS", [P, AH, P]), ph.ps("bR", [P, AH, P]), ph.ps("bK", [P, AH, P]), ph.ps("bD", [P, CH])
        bN = [ph.ps(f"bN{i}", [P, 2, DV]) for i in range(2)]
        bU = [ph.ps(f"bU{i}", [P, 2, DV]) for i in range(2)]
        c_in, k_ready = ph.sem("c_in"), ph.sem("k_ready")
        qk_in = [ph.sem(f"qk_in{j}") for j in range(2)]
        v_in = [ph.sem(f"v_in{j}") for j in range(2)]
        og_in = [ph.sem(f"og_in{j}") for j in range(2)]
        stored = [ph.sem(f"stored{j}") for j in range(2)]
        scores_ready, dwin_ready, dw_ready, iw_ready, kw_ready = (ph.sem(x) for x in ("scores_ready", "dwin_ready", "dw_ready", "iw_ready", "kw_ready"))
        sc_ready, num_ready, upd_ready, state_ready = (ph.sem(x) for x in ("sc_ready", "num_ready", "upd_ready", "state_ready"))
        rden_ready, ht_ready, hn_ready, ng_done, y_ready, waited = (ph.sem(x) for x in ("rden_ready", "ht_ready", "hn_ready", "ng_done", "y_ready", "waited"))
        cq_ready, v_ready, std_ready = ph.sem("cq_ready"), ph.sem("v_ready"), ph.sem("std_ready")

        with nc.Block() as block:
            @block.sync
            def _(sp):
                def load_qk(c, j):
                    wait_from(sp, sc_ready, c - 1)
                    settle(sp, waited)
                    tok = ds(c * P, P)
                    sp.dma_start(q[:, j, :, :], d["qkT"][0:AH, :, tok].rearrange("h p t -> p h t")).then_inc(qk_in[j], 16)
                    sp.dma_start(kT[:, j, :, :], d["qkT"][AH:2 * AH, :, tok].rearrange("h p t -> p h t")).then_inc(qk_in[j], 16)

                def load_v(c, j):
                    wait_from(sp, upd_ready, c - 1)
                    settle(sp, waited)
                    sp.dma_start(v[:, j, :, :].rearrange("p h e -> p (h e)"), d["vo"][ds(c * P, P), 0:D]).then_inc(v_in[j], 16)

                def load_og(c, j):
                    wait_from(sp, y_ready, c - 1)
                    settle(sp, waited)
                    sp.dma_start(og[:, j, :], d["vo"][ds(c * P, P), D:2 * D]).then_inc(og_in[j], 16)

                def store(c, j):
                    sp.wait_ge(y_ready, c + 1)
                    settle(sp, waited)
                    sp.dma_start(d["y"][ds(c * P, P), :], y[:, j, :]).then_inc(stored[j], 16)

                sp.dma_start(rowbm[:, :], d["rowbm"]).then_inc(c_in, 16)
                sp.dma_start(colq[:, :, :, :].rearrange("p c q h -> p (c q h)"), d["colq"]).then_inc(c_in, 16)
                sp.dma_start(decay[:, :, :, :].rearrange("p a h c -> p (a h c)"), d["decay"]).then_inc(c_in, 16)
                sp.dma_start(sel[:, :, :], d["consts"][0:AH, C_SEL:C_SEL + AH * P].rearrange("k (h p) -> k h p", h=AH)).then_inc(c_in, 16)
                sp.dma_start(ident[:, :], d["consts"][:, C_ID:C_ID + P]).then_inc(c_in, 16)
                sp.dma_start(causal[:, :], d["consts"][:, C_CAUSAL:C_CAUSAL + P]).then_inc(c_in, 16)
                sp.dma_start(ng[:, :], d["a_norm_g"][0:1, :].to_broadcast([P, D])).then_inc(c_in, 16)
                skewed(sp, [(load_v, 2), (load_qk, 3), (load_og, 0), (store, -2)])
                for j in range(2):
                    sp.wait_ge(stored[j], 16 * NT // 2)

            @block.tensor
            def _(pe):
                pe.wait_ge(c_in, 16 * 7)
                pe.wait_ge(k_ready, 1)

                def scores(c, j):
                    wait_from(pe, sc_ready, c)
                    wait_from(pe, iw_ready, c)
                    wait_from(pe, kw_ready, c)
                    pe.wait_ge(qk_in[j], 16 * (c - j) + 32)
                    for h in range(AH):
                        ins = nc.tensor.matmul(bR[:, h, :], sel[:, h, :], rowbm[:, ds(c * P, P)], start=True, stop=True)
                    for h in range(AH):
                        nc.tensor.transpose(bK[:, h, :], kT[:, j, h, :], ident[:, :])
                    for h in range(AH):
                        ins = nc.tensor.matmul(bS[:, h, :], kT[:, j, h, :], q[:, j, h, :], start=True, stop=True)
                    ins.then_inc(scores_ready, 1)

                def numerators(c, j):
                    pe.wait_ge(sc_ready, c + 1)
                    pe.wait_ge(kw_ready, c + 1)
                    pe.wait_ge(v_in[j], 8 * (c - j) + 16)
                    wait_from(pe, state_ready, c)
                    wait_from(pe, ht_ready, c)
                    for h in range(AH):
                        nc.tensor.matmul(bN[h // 2][:, h % 2, :], sc[:, j, h, :], v[:, j, h, :], start=True, stop=False)
                        nc.tensor.matmul(bN[h // 2][:, h % 2, :], qs[:, j, h, :], C[:, h, :], start=False, stop=True)
                        nc.tensor.matmul(bD[:, h:h + 1], sc[:, j, h, :], ones[:, :], start=True, stop=False)
                        ins = nc.tensor.matmul(bD[:, h:h + 1], qs[:, j, h, :], n[:, h:h + 1], start=False, stop=True)
                    for h in range(AH):
                        ins = nc.tensor.matmul(bD[:, AH + h:AH + h + 1], kw[:, j, h, :], ones[:, :], start=True, stop=True)
                    ins.then_inc(num_ready, 1)
                    for h in range(AH):
                        ins = nc.tensor.matmul(bU[h // 2][:, h % 2, :], kw[:, j, h, :], v[:, j, h, :], start=True, stop=True)
                    ins.then_inc(upd_ready, 1)

                skewed(pe, [(scores, 1), (numerators, 0)])

            @block.scalar
            def _(act):
                act.wait_ge(c_in, 16 * 7)

                def weights(c, j):
                    act.wait_ge(cq_ready, c + 1)
                    act.wait_ge(scores_ready, c + 1)
                    wait_from(act, sc_ready, c)
                    for h in range(AH):
                        ins = nc.scalar.activation(iwb[:, h, :], bR[:, h, :], ACT.Exp, bias=dk[:, j, 0, h:h + 1])
                    ins.then_inc(iw_ready, 1)
                    wait_from(act, upd_ready, c - 1)
                    for h in range(AH):
                        ins = nc.scalar.activation(kw[:, j, h, :], bK[:, h, :], ACT.Copy, scale=cq[:, j, QWS, h:h + 1])
                    ins.then_inc(kw_ready, 1)

                def own_weights(c, j):
                    act.wait_ge(dwin_ready, c + 1)
                    nc.scalar.activation(dw[:, :, :], dw[:, :, :], ACT.Exp).then_inc(dw_ready, 1)

                def root(c, j):
                    act.wait_ge(v_ready, c + 1)
                    nc.scalar.activation(std[:, j, 1, :], std[:, j, 0, :], ACT.Sqrt).then_inc(std_ready, 1)

                def divide(c, j):
                    act.wait_ge(rden_ready, c + 1)
                    wait_from(act, ng_done, c - 1)
                    for h in range(AH):
                        ins = nc.scalar.activation(ht[:, j, h, :], bN[h // 2][:, h % 2, :], ACT.Copy, scale=rden[:, j, h:h + 1])
                    ins.then_inc(ht_ready, 1)

                skewed(act, [(weights, 1), (own_weights, 1), (divide, 0), (root, -1)])

            @block.vector
            def _(dve):
                nc.vector.memset(C[:, :, :], 0.0)
                nc.vector.memset(n[:, :], 0.0)
                nc.vector.memset(ones[:, :], 1.0)
                dve.drain().then_inc(k_ready, 1)
                dve.wait_ge(c_in, 16 * 7)

                def state(c, j):
                    dve.wait_ge(upd_ready, c + 1)
                    for h in range(AH):
                        ins = nc.vector.scalar_tensor_tensor(C[:, h, :], C[:, h, :], dk[:, j, 1, h:h + 1], bU[h // 2][:, h % 2, :], ALU.mult, ALU.add)
                    ins.then_inc(state_ready, 1)

                def columns(c, j):
                    wait_from(dve, state_ready, c - 1)
                    nc.vector.tensor_copy(cq[:, j, :, :], colq[:, ds(c, 1), :, :])
                    nc.vector.tensor_copy(dk[:, j, :, :], decay[:, :, :, ds(c, 1)])
                    dve.drain().then_inc(cq_ready, 1)

                def own_logs(c, j):
                    dve.wait_ge(iw_ready, c + 1)
                    for h in range(AH):
                        ins = nc.vector.scalar_tensor_tensor(dw[:, h, :], bR[:, h, :], cq[:, j, QU, h:h + 1], causal[:, :], ALU.add, ALU.add)
                    ins.then_inc(dwin_ready, 1)
                    wait_from(dve, num_ready, c - 1)
                    nc.vector.tensor_tensor(qs[:, j, :, :], q[:, j, :, :], iwb[:, :, :], ALU.mult)

                def weigh(c, j):
                    dve.wait_ge(dw_ready, c + 1)
                    nc.vector.tensor_tensor(sc[:, j, :, :], bS[:, :, :], dw[:, :, :], ALU.mult).then_inc(sc_ready, 1)

                def denominators(c, j):
                    dve.wait_ge(num_ready, c + 1)
                    nc.vector.scalar_tensor_tensor(den[:, :], bD[:, 0:AH], -1.0, cq[:, j, QEM, :], ALU.mult, ALU.max)
                    nc.vector.tensor_tensor(n[:, :], n[:, :], dk[:, j, 1, :], ALU.mult)
                    dve.drain()
                    nc.vector.tensor_tensor(den[:, :], bD[:, 0:AH], den[:, :], ALU.max)
                    dve.drain()
                    nc.vector.reciprocal(rden[:, j, :], den[:, :]).then_inc(rden_ready, 1)
                    nc.vector.tensor_tensor(n[:, :], n[:, :], bD[:, AH:2 * AH], ALU.add)

                def statistics(c, j):
                    dve.wait_ge(ht_ready, c + 1)
                    for h in range(AH):
                        nc.vector.bn_stats(stats[:, h, :], ht[:, j, h, :])
                    dve.drain()
                    for h in range(AH):
                        nc.vector.bn_aggr(mv[:, j, h, :], stats[:, h, :])
                    dve.drain()
                    nc.vector.tensor_scalar(std[:, j, 0, :], mv[:, j, :, 1], A_NORM_EPS, None, ALU.add).then_inc(v_ready, 1)

                def normalise(c, j):
                    dve.wait_ge(std_ready, c + 1)
                    nc.vector.reciprocal(std[:, j, 2, :], std[:, j, 1, :])
                    dve.drain()
                    for h in range(AH):
                        ins = nc.vector.tensor_scalar(ht[:, j, h, :], ht[:, j, h, :], mv[:, j, h, 0:1], std[:, j, 2, h:h + 1], ALU.subtract, ALU.mult)
                    ins.then_inc(hn_ready, 1)

                def gate(c, j):
                    dve.wait_ge(og_in[j], 8 * (c - j) + 16)
                    dve.wait_ge(ng_done, c + 1)
                    nc.vector.tensor_tensor(y[:, j, :], y[:, j, :], og[:, j, :], ALU.mult).then_inc(y_ready, 1)

                skewed(dve, [(statistics, -1), (own_logs, 1), (gate, -2), (weigh, 1), (denominators, 0), (state, 0), (columns, 2), (normalise, -1)])

            @block.gpsimd
            def _(pool):
                pool.wait_ge(c_in, 16 * 7)

                def norm_gain(c, j):
                    pool.wait_ge(hn_ready, c + 1)
                    wait_from(pool, stored[j], 8 * (c - j))
                    nc.gpsimd.tensor_tensor(y[:, j, :], ht[:, j, :, :].rearrange("p h e -> p (h e)"), ng[:, :], ALU.mult).then_inc(ng_done, 1)

                skewed(pool, [(norm_gain, -1)])


def load_norm(eng, nc, d, norm, gain, l, which, sem):
    eng.dma_start(norm[:, 0, :], d["ln_g"][l, which:which + 1, :].to_broadcast([P, D])).then_inc(sem, 16)
    eng.dma_start(norm[:, 1, :], d["ln_b"][l, which:which + 1, :].to_broadcast([P, D])).then_inc(sem, 16)
    kind = 3 * which + 2
    eng.dma_start(gain[:, :], d["mod"][l:l + 1, kind * D:(kind + 1) * D].to_broadcast([P, D])).then_inc(sem, 16)


def after_mixer(nc, d, l):
    K = KD if l == 0 else BW // P
    W = K * P
    name = f"am{l}"
    with Phase(nc, name) as ph:
        w = ph.sb("w", [P, K, D])
        ws = ph.sb("ws", [P, 2, K, D], F32R)
        wr = ph.sb("wr", [P, KD, NR])
        br = ph.sb("br", [P, NR])
        ident = ph.sb("ident", [P, P])
        cols = ph.sb("cols", [P, 2, KD])
        norm = ph.sb("norm", [P, 2, D])
        gain = ph.sb("gain", [P, D])
        y = ph.sb("y", [P, 2, W])
        x = ph.sb("x", [P, 2, D])
        yT = ph.sb("yT", [P, 2, 2, K, P], F32R)
        z = ph.sb("z", [P, 2, D])
        x1 = ph.sb("x1", [P, 2, D])
        hT = ph.sb("hT", [P, KD, P])
        stats = ph.sb("stats", [P, 2, 6])
        mv = ph.sb("mv", [P, 2, 2])
        std = ph.sb("std", [P, 2, 3])
        nb = ph.sb("nb", [P, 2, 1])
        lg = ph.sb("lg", [P, 2, NR])
        if l:
            o = ph.sb("o", [P, 2, G, HP * OW])
            coef = ph.sb("coef", [P, 2, G, BH])
            cd = ph.sb("cd", [P, G, BH])
            mx = ph.sb("mx", [P, BH])
            dn = ph.sb("dn", [P, BH])
            og = ph.sb("og", [P, G, BW])
        ytp = [ph.ps(f"ytp{i}", [P, 4, P]) for i in range(K // 4)]
        xtp = [ph.ps(f"xtp{i}", [P, 4, P]) for i in range(2)]
        acc = [[ph.ps(f"acc{j}{i}", [P, CH]) for i in range(2)] for j in range(2)]
        bl = ph.ps("bl", [P, NR]) if l else xtp[0][:, 0, 0:NR]
        names = ("c_in", "cols_ready", "whi_ready", "wlo_ready", "ytp_ready", "yhi_ready", "ylo_ready", "acc_ready", "z_ready", "v_ready", "std_ready", "nb_ready",
                 "xn_ready", "xg_ready", "x1_ready", "xtp_ready", "hT_ready", "lg_acc", "lg_ready", "waited", "y_ready", "e_in", "e_ready", "og_ready")
        (c_in, cols_ready, whi_ready, wlo_ready, ytp_ready, yhi_ready, ylo_ready, acc_ready, z_ready, v_ready, std_ready, nb_ready,
         xn_ready, xg_ready, x1_ready, xtp_ready, hT_ready, lg_acc, lg_ready, waited, y_ready, e_in, e_ready, og_ready) = (ph.sem(s) for s in names)
        pieces = [(slice(k, k + 2), slice(half * CH, (half + 1) * CH)) for half in range(2) for k in range(0, K, 2)]
        HALF = len(pieces) // 2
        w_in = [ph.sem(f"w_in{n}") for n in range(len(pieces))]
        y_in = [ph.sem(f"y_in{j}") for j in range(2)]
        x_in = [ph.sem(f"x_in{j}") for j in range(2)]
        x_st = [ph.sem(f"x_st{j}") for j in range(2)]
        l_st = [ph.sem(f"l_st{j}") for j in range(2)]
        x_dram = d["x"][0] if l == 0 else d["x2"]
        w_dram = (d["a_w_out"] if l == 0 else d["b_w_o"])[0].rearrange("(p k) n -> p k n", k=K)

        with nc.Block() as block:
            @block.sync
            def _(sp):
                def load_y(c, j):
                    wait_from(sp, og_ready if l else ytp_ready, c - 1)
                    settle(sp, waited)
                    if l == 0:
                        sp.dma_start(y[:, j, :], d["y"][ds(c * P, P), :]).then_inc(y_in[j], 16)
                    else:
                        sp.dma_start(o[:, j, :, :], d["o"][:, ds(c * P, P), :].rearrange("g p n -> p g n")).then_inc(y_in[j], 16)

                def load_x(c, j):
                    wait_from(sp, z_ready, c - 1)
                    settle(sp, waited)
                    sp.dma_start(x[:, j, :], x_dram[ds(c * P, P), :]).then_inc(x_in[j], 16)

                def store_x1(c, j):
                    sp.wait_ge(x1_ready, c + 1)
                    settle(sp, waited)
                    sp.dma_start(d["x1"][ds(c * P, P), :], x1[:, j, :]).then_inc(x_st[j], 16)

                def store_logits(c, j):
                    sp.wait_ge(lg_ready, c + 1)
                    settle(sp, waited)
                    sp.dma_start(d["lg"][ds(c * P, P), :], lg[:, j, :]).then_inc(l_st[j], 16)

                sp.dma_start(ident[:, :], d["consts"][:, C_ID:C_ID + P]).then_inc(c_in, 16)
                load_mod_columns(sp, nc, d, cols, l, (3, 4), c_in)
                load_norm(sp, nc, d, norm, gain, l, 0, c_in)
                sp.dma_start(wr[:, :, 0:MG], d["moe_w_r1"][l].rearrange("(p k) n -> p k n", k=KD)).then_inc(c_in, 16)
                sp.dma_start(wr[:, :, MG:NR], d["moe_w_r2"][l].rearrange("(p k) n -> p k n", k=KD)).then_inc(c_in, 16)
                sp.dma_start(br[:, 0:MG], d["moe_b_r1"][l:l + 1, :].to_broadcast([P, MG])).then_inc(c_in, 16)
                sp.dma_start(br[:, MG:NR], d["moe_b_r2"][l:l + 1, :].to_broadcast([P, NE])).then_inc(c_in, 16)
                for c in range(2):
                    load_y(c, c)
                for n, (rows, cut) in enumerate(pieces):
                    sp.dma_start(w[:, rows, cut], w_dram[:, rows, cut]).then_inc(w_in[n], 16)

                def load_y_later(c, j):
                    if not (isinstance(c, int) and c < 2):
                        load_y(c, j)

                skewed(sp, [(load_y_later, 5 if l else 4), (load_x, 2), (store_logits, -2), (store_x1, -1)])
                for j in range(2):
                    sp.wait_ge(x_st[j], 16 * NT // 2)
                    sp.wait_ge(l_st[j], 16 * NT // 2)

            @block.tensor
            def _(pe):
                pe.wait_ge(c_in, 16 * 10)

                def y_transposes(c, j):
                    if l:
                        pe.wait_ge(y_ready, c + 1)
                    else:
                        pe.wait_ge(y_in[j], 8 * (c - j) + 16)
                    wait_from(pe, ylo_ready, c)
                    for k in range(K):
                        ins = nc.tensor.transpose(ytp[k // 4][:, k % 4, :], y[:, j, k:W:K], ident[:, :])
                    ins.then_inc(ytp_ready, 1)

                def out_half(c, j, half):
                    if half == 0:
                        pe.wait_ge(yhi_ready, c + 1)
                        pe.wait_ge(ylo_ready, c + 1)
                        wait_from(pe, z_ready, c - 1)
                    for k in range(K):
                        if k % 2 == 0 and isinstance(c, int) and c == 0:
                            pe.wait_ge(wlo_ready, half * HALF + k // 2 + 1)
                        for n, (a, b) in enumerate(((0, 0), (0, 1), (1, 0))):
                            ins = nc.tensor.matmul(acc[j][half][:, :], yT[:, j, a, k, :], ws[:, b, k, half * CH:(half + 1) * CH],
                                                   start=(k == 0 and n == 0), stop=(k == K - 1 and n == 2))
                    if half:
                        ins.then_inc(acc_ready, 1)

                def logits(c, j):
                    pe.wait_ge(hT_ready, c + 1)
                    wait_from(pe, lg_ready, c)
                    for k in range(KD):
                        ins = nc.tensor.matmul(bl[:, :], hT[:, k, :], wr[:, k, :], start=(k == 0), stop=(k == KD - 1))
                    ins.then_inc(lg_acc, 1)

                def x1_transposes(c, j):
                    pe.wait_ge(x1_ready, c + 1)
                    wait_from(pe, hT_ready, c)
                    if l == 0:
                        wait_from(pe, lg_ready, c)
                    for k in range(KD):
                        ins = nc.tensor.transpose(xtp[k // 4][:, k % 4, :], x1[:, j, k:D:KD], ident[:, :])
                    ins.then_inc(xtp_ready, 1)

                skewed(pe, [(lambda c, j: out_half(c, j, 0), 1), (y_transposes, 2), (logits, -2),
                            (lambda c, j: out_half(c, j, 1), 1), (x1_transposes, -1)])

            @block.scalar
            def _(act):
                def weights_hi(some):
                    for n in some:
                        rows, cut = pieces[n]
                        act.wait_ge(w_in[n], 16)
                        nc.scalar.activation(ws[:, 0, rows, cut], w[:, rows, cut], ACT.Copy).then_inc(whi_ready, 1)

                def rest_of_weights(c, j):
                    if isinstance(c, int) and c == 0:
                        weights_hi(range(HALF, 2 * HALF))

                weights_hi(range(HALF))
                act.wait_ge(cols_ready, 1)

                def branch_weights(c, j):
                    act.wait_ge(e_in, c + 1)
                    nc.scalar.activation(coef[:, j, :, :], coef[:, j, :, :], ACT.Exp).then_inc(e_ready, 1)

                def y_hi(c, j):
                    act.wait_ge(ytp_ready, c + 1)
                    wait_from(act, acc_ready, c - 1)
                    for i in range(K // 4):
                        ins = nc.scalar.activation(yT[:, j, 0, i * 4:(i + 1) * 4, :], ytp[i][:, :, :], ACT.Copy)
                    ins.then_inc(yhi_ready, 1)

                def root(c, j):
                    act.wait_ge(v_ready, c + 1)
                    nc.scalar.activation(std[:, j, 1:2], std[:, j, 0:1], ACT.Sqrt).then_inc(std_ready, 1)

                def normalise(c, j):
                    act.wait_ge(nb_ready, c + 1)
                    nc.scalar.activation(z[:, j, :], z[:, j, :], ACT.Identity, bias=nb[:, j, 0:1], scale=std[:, j, 2:3]).then_inc(xn_ready, 1)

                def modulate(c, j):
                    act.wait_ge(xtp_ready, c + 1)
                    wait_from(act, lg_acc, c)
                    for k in range(KD):
                        ins = nc.scalar.activation(hT[:, k, :], xtp[k // 4][:, k % 4, :], ACT.Identity,
                                                   bias=cols[:, 0, k:k + 1], scale=cols[:, 1, k:k + 1])
                    ins.then_inc(hT_ready, 1)

                skewed(act, [(modulate, -2), (y_hi, 2), (rest_of_weights, 2), (root, 0), (normalise, 0)] + ([(branch_weights, 4)] if l else []))

            @block.vector
            def _(dve):
                dve.wait_ge(c_in, 16 * 10)
                nc.vector.tensor_scalar(cols[:, 1, :], cols[:, 1, :], 1.0, None, ALU.add).then_inc(cols_ready, 1)
                nc.vector.tensor_scalar(gain[:, :], gain[:, :], 1.0, None, ALU.add)
                def weights_lo(some):
                    for n in some:
                        rows, cut = pieces[n]
                        dve.wait_ge(whi_ready, n + 1)
                        nc.vector.tensor_tensor(ws[:, 1, rows, cut], w[:, rows, cut], ws[:, 0, rows, cut], ALU.subtract).then_inc(wlo_ready, 1)

                def rest_of_weights(c, j):
                    if isinstance(c, int) and c == 0:
                        weights_lo(range(HALF, 2 * HALF))

                weights_lo(range(HALF))

                def branch_maxima(c, j):
                    dve.wait_ge(y_in[j], 8 * (c - j) + 16)
                    m = o[:, j, :, :].rearrange("p g (h e) -> p g h e", e=DH + 2)[:, :, :, DH]
                    nc.vector.tensor_tensor(mx[:, :], m[:, 0, :], m[:, 1, :], ALU.min)
                    dve.drain()
                    nc.vector.tensor_tensor(mx[:, :], mx[:, :], m[:, 2, :], ALU.min)
                    dve.drain()
                    for g in range(G):
                        ins = nc.vector.tensor_tensor(coef[:, j, g, :], mx[:, :], m[:, g, :], ALU.subtract)
                    ins.then_inc(e_in, 1)

                def branches(c, j):
                    v = o[:, j, :, :].rearrange("p g (h e) -> p g h e", e=DH + 2)
                    dve.wait_ge(e_ready, c + 1)
                    nc.vector.tensor_tensor(cd[:, :, :], coef[:, j, :, :], v[:, :, :, DH + 1], ALU.mult)
                    dve.drain()
                    nc.vector.tensor_tensor(dn[:, :], cd[:, 0, :], cd[:, 1, :], ALU.add)
                    dve.drain()
                    nc.vector.tensor_tensor(dn[:, :], dn[:, :], cd[:, 2, :], ALU.add)
                    dve.drain()
                    nc.vector.reciprocal(dn[:, :], dn[:, :])
                    dve.drain()
                    nc.vector.tensor_tensor(coef[:, j, :, :], coef[:, j, :, :], dn[:, :].rearrange("p (o h) -> p o h", o=1).to_broadcast([P, G, BH]), ALU.mult)
                    dve.drain()
                    wait_from(dve, y_ready, c)
                    for g in range(G):
                        ins = nc.vector.tensor_tensor(og[:, g, :].rearrange("p (h e) -> p h e", e=DH), v[:, g, :, 0:DH],
                                                      coef[:, j, g, :].rearrange("p (h o) -> p h o", o=1).to_broadcast([P, BH, DH]), ALU.mult)
                    ins.then_inc(og_ready, 1)

                def y_lo(c, j):
                    dve.wait_ge(yhi_ready, c + 1)
                    for i in range(K // 4):
                        ins = nc.vector.tensor_tensor(yT[:, j, 1, i * 4:(i + 1) * 4, :], ytp[i][:, :, :], yT[:, j, 0, i * 4:(i + 1) * 4, :], ALU.subtract)
                    ins.then_inc(ylo_ready, 1)

                def total(c, j):
                    dve.wait_ge(acc_ready, c + 1)
                    wait_from(dve, xg_ready, c - 1)
                    for half in range(2):
                        cut = slice(half * CH, (half + 1) * CH)
                        nc.vector.tensor_tensor(z[:, j, cut], acc[j][half][:, :], gain[:, cut], ALU.mult)
                    dve.drain()
                    dve.wait_ge(x_in[j], 8 * (c - j) + 16)
                    nc.vector.scalar_tensor_tensor(z[:, j, :], x[:, j, :], ALPHA, z[:, j, :], ALU.mult, ALU.add).then_inc(z_ready, 1)
                    dve.wait_ge(z_ready, c + 1)
                    for half in range(2):
                        nc.vector.bn_stats(stats[:, half, :], z[:, j, half * CH:(half + 1) * CH])
                    dve.drain()
                    nc.vector.bn_aggr(mv[:, j, :], stats[:, :, :].rearrange("p a b -> p (a b)"))
                    dve.drain()
                    nc.vector.tensor_scalar(std[:, j, 0:1], mv[:, j, 1:2], LN_EPS, None, ALU.add).then_inc(v_ready, 1)

                def scale(c, j):
                    dve.wait_ge(std_ready, c + 1)
                    nc.vector.reciprocal(std[:, j, 2:3], std[:, j, 1:2])
                    dve.drain()
                    nc.vector.tensor_scalar(nb[:, j, :], mv[:, j, 0:1], std[:, j, 2:3], -1.0, ALU.mult, ALU.mult).then_inc(nb_ready, 1)

                def finish(c, j):
                    dve.wait_ge(xg_ready, c + 1)
                    nc.vector.tensor_tensor(x1[:, j, :], x1[:, j, :], norm[:, 1, :], ALU.add).then_inc(x1_ready, 1)

                def bias_logits(c, j):
                    dve.wait_ge(lg_acc, c + 1)
                    wait_from(dve, l_st[j], 8 * (c - j))
                    nc.vector.tensor_tensor(lg[:, j, :], bl[:, :], br[:, :], ALU.add).then_inc(lg_ready, 1)

                skewed(dve, [(total, 0), (bias_logits, -2), (finish, -1), (y_lo, 2), (rest_of_weights, 2), (scale, 0)]
                       + ([(branches, 3), (branch_maxima, 4)] if l else []))

            @block.gpsimd
            def _(pool):
                pool.wait_ge(c_in, 16 * 10)

                def sum_branches(c, j):
                    pool.wait_ge(og_ready, c + 1)
                    wait_from(pool, ytp_ready, c - 1)
                    nc.gpsimd.tensor_tensor(og[:, 0, :], og[:, 0, :], og[:, 1, :], ALU.add)
                    pool.drain()
                    nc.gpsimd.tensor_tensor(y[:, j, :], og[:, 0, :], og[:, 2, :], ALU.add).then_inc(y_ready, 1)

                def gamma(c, j):
                    pool.wait_ge(xn_ready, c + 1)
                    wait_from(pool, x_st[j], 8 * (c - j))
                    wait_from(pool, xtp_ready, c - 1)
                    nc.gpsimd.tensor_tensor(x1[:, j, :], z[:, j, :], norm[:, 0, :], ALU.mult).then_inc(xg_ready, 1)

                skewed(pool, ([(sum_branches, 3)] if l else []) + [(gamma, 0)])


def route(nc, d, l):
    with Phase(nc, f"rt{l}") as ph:
        lg = ph.sb("lg", [P, NT, NR])
        iota = ph.sb("iota", [P, NE])
        blk = ph.sb("blk", [P, NBP])
        before = ph.sb("before", [P, P])
        ones = ph.sb("ones", [P, P])
        tokf = ph.sb("tokf", [P, NT])
        rows = ph.sb("rows", [P, P])
        d128 = ph.sb("d128", [P, NT, 2], I32)
        blkf = ph.sb("blkf", [P, NT, 2])
        rowf = ph.sb("rowf", [P, NT, 2])
        ohb = ph.sb("ohb", [P, 2 * NT, NBP])
        ohr = ph.sb("ohr", [P, 2 * NT, P])
        sloti = ph.sb("sloti", [P, NBP], I32)
        gpad = ph.sb("gpad", [P, NT, 8])
        gval, gidx = ph.sb("gval", [P, NT, 8]), ph.sb("gidx", [P, NT, 8], U32)
        gf = ph.sb("gf", [P, NT])
        eg = ph.sb("eg", [P, NT, MG])
        pg = ph.sb("pg", [P, NT])
        oh4 = ph.sb("oh4", [P, NT, MG])
        pen = ph.sb("pen", [P, NT, MG])
        masked = ph.sb("masked", [P, NT, NE])
        val, idx = ph.sb("val", [P, NT, 8]), ph.sb("idx", [P, NT, 8], U32)
        ef = ph.sb("ef", [P, NT, 2])
        dif = ph.sb("dif", [P, NT])
        ex = ph.sb("ex", [P, NT])
        wt = ph.sb("wt", [P, NT, 2])
        oh = [ph.sb(f"oh{j}", [P, NT, NE]) for j in range(2)]
        both = ph.sb("both", [P, NT, NE])
        pre = ph.sb("pre", [P, NT + 1, NE])
        cnti = ph.sb("cnti", [P, NE], I32)
        pc = ph.sb("pc", [P, NE])
        pend = ph.sb("pend", [P, NE])
        pstart = ph.sb("pstart", [P, NE])
        dest = ph.sb("dest", [P, NT, NE])
        hit = ph.sb("hit", [P, NT, NE])
        destf = ph.sb("destf", [P, NT, 2])
        desti = ph.sb("desti", [P, NT, 2], I32)
        le = ph.sb("le", [P, NBP, NE])
        bef = ph.sb("bef", [P, NBP])
        bei = ph.sb("bei", [P, NBP], I32)
        slot = ph.ps("slot", [P, NBP])
        rank, total = ph.ps("rank", [P, NT, NE]), ph.ps("total", [P, NT, NE])
        in_sem, e_in, e_out, d_in, d_out = (ph.sem(s) for s in ("in", "e_in", "e_out", "d_in", "d_out"))
        both_ready, rank_ready, hot_ready, slot_acc, slot_ready = (ph.sem(s) for s in ("both_ready", "rank_ready", "hot_ready", "slot_acc", "slot_ready"))
        dest_ready, blk_ready, out_done = (ph.sem(s) for s in ("dest_ready", "blk_ready", "out_done"))

        def over(a, shape):
            return a.rearrange("p (n o) -> p n o", o=1).to_broadcast(shape)

        def per_tile(a, n, k):
            return a.rearrange("p (o k) -> p o k", o=1).to_broadcast([P, n, k])

        with nc.Block() as block:
            @block.sync
            def _(sp):
                sp.dma_start(lg[:, :, :], d["lg"].rearrange("(c p) n -> p c n", p=P)).then_inc(in_sem, 16)
                for t, c, n in ((iota, C_EXP, NE), (blk, C_BLK, NBP), (before, C_BEFORE, P), (ones, C_ONES, P), (tokf, C_TOK, NT), (rows, C_ROW, P)):
                    sp.dma_start(t[:, :], d["consts"][:, c:c + n]).then_inc(in_sem, 16)
                sp.wait_ge(dest_ready, 1)
                sp.dma_start(d["dest"], desti[:, :, :].rearrange("p c j -> p (c j)")).then_inc(out_done, 16)
                sp.dma_start(d["wt"], wt[:, :, :].rearrange("p c j -> p (c j)")).then_inc(out_done, 16)
                sp.wait_ge(slot_ready, 1)
                sp.dma_start(d["slots"], sloti[:, :]).then_inc(out_done, 16)
                sp.wait_ge(blk_ready, 1)
                sp.dma_start(d["block_e"], bei[0:1, :]).then_inc(out_done, 16)
                sp.wait_ge(out_done, 64)

            @block.scalar
            def _(act):
                act.wait_ge(e_in, 1)
                nc.scalar.activation(eg[:, :, :], eg[:, :, :], ACT.Exp).then_inc(e_out, 1)
                act.wait_ge(d_in, 1)
                nc.scalar.activation(ex[:, :], dif[:, :], ACT.Exp).then_inc(d_out, 1)

            @block.tensor
            def _(pe):
                pe.wait_ge(both_ready, 1)
                nc.tensor.matmul(rank[:, :, :], before[:, :], both[:, :, :], start=True, stop=True)
                nc.tensor.matmul(total[:, :, :], ones[:, :], both[:, :, :], start=True, stop=True).then_inc(rank_ready, 1)
                for n in range(2 * NT):
                    pe.wait_ge(hot_ready, n + 1)
                    ins = nc.tensor.matmul(slot[:, :], ohr[:, n, :], ohb[:, n, :], start=(n == 0), stop=(n == 2 * NT - 1))
                ins.then_inc(slot_acc, 1)

            @block.vector
            def _(dve):
                v = nc.vector
                v.memset(gpad[:, :, :], -3e38)
                dve.drain()
                dve.wait_ge(in_sem, 16 * 7)
                v.tensor_copy(gpad[:, :, 0:MG], lg[:, :, 0:MG])
                dve.drain()
                for c in range(NT):
                    v.max(gval[:, c, :], gpad[:, c, :])
                dve.drain()
                for c in range(NT):
                    v.max_index(gidx[:, c, :], gval[:, c, :], gpad[:, c, :])
                v.tensor_tensor(eg[:, :, :], lg[:, :, 0:MG], over(gval[:, :, 0], [P, NT, MG]), ALU.subtract).then_inc(e_in, 1)
                dve.drain()
                v.tensor_copy(gf[:, :], gidx[:, :, 0])
                dve.drain()
                v.tensor_tensor(oh4[:, :, :], per_tile(iota[:, 0:MG], NT, MG), over(gf[:, :], [P, NT, MG]), ALU.is_equal)
                dve.drain()
                v.tensor_scalar(pen[:, :, :], oh4[:, :, :], -NEG, NEG, ALU.mult, ALU.add)
                m4 = masked[:, :, :].rearrange("p c (g e) -> p c g e", g=MG)
                wide = [P, NT, MG, ME]
                v.tensor_tensor(m4, lg[:, :, MG:NR].rearrange("p c (g e) -> p c g e", g=MG),
                                oh4[:, :, :].rearrange("p c (g o) -> p c g o", o=1).to_broadcast(wide), ALU.mult)
                dve.drain()
                v.tensor_tensor(m4, m4, pen[:, :, :].rearrange("p c (g o) -> p c g o", o=1).to_broadcast(wide), ALU.add)
                dve.drain()
                for c in range(NT):
                    v.max(val[:, c, :], masked[:, c, :])
                dve.drain()
                for c in range(NT):
                    v.max_index(idx[:, c, :], val[:, c, :], masked[:, c, :])
                v.tensor_tensor(dif[:, :], val[:, :, 1], val[:, :, 0], ALU.subtract).then_inc(d_in, 1)
                dve.drain()
                v.tensor_copy(ef[:, :, :], idx[:, :, 0:2])
                dve.drain()
                for j in range(2):
                    v.tensor_tensor(oh[j][:, :, :], per_tile(iota[:, :], NT, NE), over(ef[:, :, j], [P, NT, NE]), ALU.is_equal)
                dve.drain()
                v.tensor_tensor(both[:, :, :], oh[0][:, :, :], oh[1][:, :, :], ALU.add).then_inc(both_ready, 1)
                dve.wait_ge(e_out, 1)
                v.tensor_reduce(pg[:, :], eg[:, :, :], AX_X, ALU.add)
                dve.wait_ge(d_out, 1)
                v.tensor_scalar(dif[:, :], ex[:, :], 1.0, None, ALU.add)
                dve.drain()
                v.tensor_tensor(pg[:, :], pg[:, :], dif[:, :], ALU.mult)
                dve.drain()
                v.reciprocal(wt[:, :, 0], pg[:, :])
                dve.drain()
                v.tensor_tensor(wt[:, :, 1], wt[:, :, 0], ex[:, :], ALU.mult)
                v.memset(pre[:, 0, :], 0.0)
                dve.wait_ge(rank_ready, 1)
                for c in range(NT):
                    dve.drain()
                    v.tensor_tensor(pre[:, c + 1, :], pre[:, c, :], total[:, c, :], ALU.add)
                dve.drain()
                v.tensor_copy(cnti[:, :], pre[:, NT, :])
                dve.drain()
                v.tensor_scalar(cnti[:, :], cnti[:, :], float(P - 1), None, ALU.add)
                dve.drain()
                v.tensor_scalar(cnti[:, :], cnti[:, :], 7, 7, ALU.logical_shift_right, ALU.logical_shift_left)
                dve.drain()
                v.tensor_copy(pc[:, :], cnti[:, :])
                dve.drain()
                v.tensor_tensor_scan(pend[:, :], ones[:, 0:NE], pc[:, :], 0.0, ALU.mult, ALU.add)
                dve.drain()
                v.tensor_tensor(pstart[:, :], pend[:, :], pc[:, :], ALU.subtract)
                v.tensor_tensor(dest[:, :, :], rank[:, :, :], pre[:, 0:NT, :], ALU.add)
                dve.drain()
                v.tensor_tensor(dest[:, :, :], dest[:, :, :], per_tile(pstart[:, :], NT, NE), ALU.add)
                for j in range(2):
                    dve.drain()
                    v.tensor_tensor(hit[:, :, :], dest[:, :, :], oh[j][:, :, :], ALU.mult)
                    dve.drain()
                    v.tensor_reduce(destf[:, :, j], hit[:, :, :], AX_X, ALU.add)
                dve.drain()
                v.tensor_copy(desti[:, :, :], destf[:, :, :])
                dve.drain().then_inc(dest_ready, 1)
                v.tensor_scalar(d128[:, :, :], desti[:, :, :], 7, 7, ALU.logical_shift_right, ALU.logical_shift_left)
                dve.drain()
                v.tensor_copy(blkf[:, :, :], d128[:, :, :])
                dve.drain()
                v.tensor_tensor(rowf[:, :, :], destf[:, :, :], blkf[:, :, :], ALU.subtract)
                dve.drain()
                for n in range(2 * NT):
                    c, j = n // 2, n % 2
                    v.tensor_scalar(ohb[:, n, :], blk[:, :], blkf[:, c, j:j + 1], tokf[:, c:c + 1], ALU.is_equal, ALU.mult)
                    v.tensor_scalar(ohr[:, n, :], rows[:, :], rowf[:, c, j:j + 1], None, ALU.is_equal).then_inc(hot_ready, 1)
                v.tensor_tensor(le[:, :, :], per_tile(pend[:, :], NBP, NE), over(blk[:, :], [P, NBP, NE]), ALU.is_le)
                dve.drain()
                v.tensor_reduce(bef[:, :], le[:, :, :], AX_X, ALU.add)
                dve.drain()
                v.tensor_scalar(bef[:, :], bef[:, :], float(NE - 1), None, ALU.min)
                dve.drain()
                v.tensor_copy(bei[:, :], bef[:, :]).then_inc(blk_ready, 1)
                dve.wait_ge(slot_acc, 1)
                v.tensor_copy(sloti[:, :], slot[:, :]).then_inc(slot_ready, 1)


def experts(nc, d, l):
    JH = HID // P
    with Phase(nc, f"ex{l}") as ph:
        ident = ph.sb("ident", [P, P])
        cols = ph.sb("cols", [P, 2, KD])
        tok = ph.sb("tok", [P, NBP], I32)
        tokb = ph.sb("tokb", [P, 2], I32)
        be = ph.sb("be", [1, NBP], I32)
        xg = ph.sb("xg", [P, 2, D])
        hT = ph.sb("hT", [P, 2, KD, P])
        WB = 4
        wgu = ph.sb("wgu", [P, WB, KD, 2, HID])
        wd = ph.sb("wd", [P, 2, JH, D])
        wds = ph.sb("wds", [P, 2, 2, JH, D], F32R)
        sg = ph.sb("sg", [P, HID])
        a = ph.sb("a", [P, HID])
        aT = ph.sb("aT", [P, 2, JH, P], F32R)
        y = ph.sb("y", [P, 2, D])
        tp = [ph.ps(f"tp{i}", [P, 4, P]) for i in range(2)]
        gu = [ph.ps(f"gu{j}", [P, 2, HID]) for j in range(2)]
        at = ph.ps("at", [P, JH, P])
        acc = [ph.ps(f"acc{i}", [P, CH]) for i in range(2)]
        (c_in, s_in, cols_ready, htp_ready, hT_act, hT_dve, gu_ready, sg_ready, a_ready, atp_ready, aT_ready,
         acc_ready, y_act, y_dve, waited) = (ph.sem(s) for s in (
             "c_in", "s_in", "cols_ready", "htp_ready", "hT_act", "hT_dve", "gu_ready", "sg_ready", "a_ready",
             "atp_ready", "aT_ready", "acc_ready", "y_act", "y_dve", "waited"))
        gu_in = [ph.sem(f"gu_in{j}") for j in range(WB)]
        wd_in, stored = ([ph.sem(f"{n}{j}") for j in range(2)] for n in ("wd_in", "stored"))
        whi_ready, wlo_ready = ph.sem("whi_ready"), ph.sem("wlo_ready")
        x_in = d["pool_dma"](f"ex{l}")
        views = [d[n][l].rearrange("e (p k) n -> e p k n", p=P) for n in ("moe_w_gate", "moe_w_up", "moe_w_down")]

        with nc.Block() as block:
            @block.sync
            def _(sp):
                for credited, by in ((a_ready, 1), (aT_ready, 1), (y_act, 1), (y_dve, 1), (acc_ready, 1), (stored[0], 16), (stored[1], 16)):
                    sp.sem_inc(credited, by)
                sp.dma_start(be[:, :], d["block_e"]).then_inc(s_in, 16)
                sp.dma_start(tok[:, :], d["slots"]).then_inc(s_in, 16)
                sp.dma_start(ident[:, :], d["consts"][:, C_ID:C_ID + P]).then_inc(c_in, 16)
                load_mod_columns(sp, nc, d, cols, l, (3, 4), c_in)
                sp.wait_ge(s_in, 32)

                def step(b, j):
                    wait_from(sp, gu_ready, b - WB + 1)
                    e = sp.value_load(be[0:1, ds(b, 1)], min_val=0, max_val=NE - 1)
                    for n in range(2):
                        sp.dma_start(wgu[:, j, :, n, :], views[n][ds(e, 1), :, :, :].rearrange("e p k n -> p (e k) n")).then_inc(gu_in[j], 16)
                    if not (isinstance(b, int) and b < 2):
                        sp.wait_ge(wlo_ready, b - 1)
                        settle(sp, waited)
                    sp.dma_start(wd[:, j % 2, :, :], views[2][ds(e, 1), :, :, :].rearrange("e p k n -> p (e k) n")).then_inc(wd_in[j % 2], 16)

                for b in range(WB):
                    step(b, b)
                with sp.Fori(1, NB // WB) as i:
                    for j in range(WB):
                        step(i * WB + j, j)
                for b in range(NB - NB % WB, NB):
                    step(b, b % WB)

            @block.gpsimd
            def _(pool):
                pool.wait_ge(s_in, 32)

                def step(b, j):
                    if not (isinstance(b, int) and b < 2):
                        pool.wait_ge(htp_ready, b - 1)
                    nc.gpsimd.tensor_copy(tokb[:, j:j + 1], tok[:, ds(b, 1)])
                    pool.drain()
                    nc.gpsimd.indirect_dma_start(out=xg[:, j, :], out_offset=None, in_=d["x1"],
                                                 in_offset=bass.IndirectOffsetOnAxis(ap=tokb[:, j:j + 1], axis=0)).then_inc(x_in[j], 16)

                step(0, 0)
                step(1, 1)
                with pool.Fori(1, (NB - 1) // 2) as i:
                    for j in range(2):
                        step(i * 2 + j, j)
                step(NB - 1, 0)

            @block.tensor
            def _(pe):
                pe.wait_ge(c_in, 48)

                def transposes(b, j):
                    pe.wait_ge(x_in[j], 8 * (b - j) + 16)
                    pe.wait_ge(hT_act, b)
                    pe.wait_ge(hT_dve, b)
                    for k in range(KD):
                        ins = nc.tensor.transpose(tp[k // 4][:, k % 4, :], xg[:, j, k:D:KD], ident[:, :])
                    ins.then_inc(htp_ready, 1)

                def gate_up(b, j, jw, half):
                    if half == 0:
                        pe.wait_ge(hT_act, b + 1)
                        pe.wait_ge(hT_dve, b + 1)
                        pe.wait_ge(gu_in[jw], (32 // WB) * (b - jw) + 32)
                        if not (isinstance(b, int) and b < 2):
                            pe.wait_ge(a_ready, b)
                    for k in range(half * 4, half * 4 + 4):
                        ins = nc.tensor.matmul(gu[j][:, :, :], hT[:, j, k, :], wgu[:, jw, k, :, :], start=(k == 0), stop=(k == KD - 1))
                    if half:
                        ins.then_inc(gu_ready, 1)

                def act_transposes(b):
                    pe.wait_ge(a_ready, b + 2)
                    pe.wait_ge(aT_ready, b + 1)
                    for k in range(JH):
                        ins = nc.tensor.transpose(at[:, k, :], a[:, k:HID:JH], ident[:, :])
                    ins.then_inc(atp_ready, 1)

                def down(b, j):
                    pe.wait_ge(aT_ready, b + 2)
                    pe.wait_ge(wlo_ready, b + 1)
                    pe.wait_ge(y_act, b + 1)
                    pe.wait_ge(y_dve, b + 1)
                    for half in range(2):
                        for k in range(JH):
                            for n, (hi_a, hi_w) in enumerate(((0, 0), (0, 1), (1, 0))):
                                ins = nc.tensor.matmul(acc[half][:, :], aT[:, hi_a, k, :], wds[:, j, hi_w, k, half * CH:(half + 1) * CH],
                                                       start=(k == 0 and n == 0), stop=(k == JH - 1 and n == 2))
                    ins.then_inc(acc_ready, 1)

                def step(b, jw, first, last):
                    j = jw % 2
                    gate_up(b, j, jw, 0)
                    if not first:
                        act_transposes(b - 1)
                    gate_up(b, j, jw, 1)
                    if not last:
                        transposes(b + 1, 1 - j)
                    if not first:
                        down(b - 1, 1 - j)

                transposes(0, 0)
                step(0, 0, True, False)
                with pe.Fori(0, (NB - 2) // WB) as i:
                    for j in range(WB):
                        step(i * WB + j + 1, (j + 1) % WB, False, False)
                for b in range((NB - 2) // WB * WB + 1, NB):
                    step(b, b % WB, False, b == NB - 1)
                act_transposes(NB - 1)
                down(NB - 1, (NB - 1) % 2)

            @block.scalar
            def _(act):
                act.wait_ge(cols_ready, 1)

                def rows(b, j):
                    act.wait_ge(htp_ready, b + 1)
                    if not (isinstance(b, int) and b < 2):
                        act.wait_ge(gu_ready, b - 1)
                    for k in range(4):
                        ins = nc.scalar.activation(hT[:, j, k, :], tp[0][:, k, :], ACT.Identity, bias=cols[:, 0, k:k + 1], scale=cols[:, 1, k:k + 1])
                    ins.then_inc(hT_act, 1)

                def weights_hi(b, j):
                    act.wait_ge(wd_in[j], 8 * (b - j) + 16)
                    if not (isinstance(b, int) and b < 2):
                        act.wait_ge(acc_ready, b)
                    nc.scalar.activation(wds[:, j, 0, :, :], wd[:, j, :, :], ACT.Copy).then_inc(whi_ready, 1)

                def store(b, j):
                    act.wait_ge(acc_ready, b + 2)
                    act.wait_ge(stored[j], 8 * (b - j) + 16)
                    nc.scalar.activation(y[:, j, CH:D], acc[1][:, :], ACT.Copy).then_inc(y_act, 1)
                    act.wait_ge(y_act, b + 2)
                    act.wait_ge(y_dve, b + 2)
                    settle(act, waited)
                    act.dma_start(d["ybuf"][ds(b * P, P), :], y[:, j, :]).then_inc(stored[j], 16)

                def step(b, j, first, last):
                    act.wait_ge(gu_ready, b + 1)
                    act.wait_ge(a_ready, b + 1)
                    nc.scalar.activation(sg[:, :], gu[j][:, 0, :], ACT.Silu).then_inc(sg_ready, 1)
                    if not last:
                        rows(b + 1, 1 - j)
                    weights_hi(b, j)
                    if not first:
                        store(b - 1, 1 - j)

                rows(0, 0)
                step(0, 0, True, False)
                with act.Fori(0, (NB - 3) // 2) as i:
                    for j in range(2):
                        step(i * 2 + j + 1, (j + 1) % 2, False, False)
                step(NB - 2, 1, False, False)
                step(NB - 1, 0, False, True)
                store(NB - 1, 0)
                act.wait_ge(stored[0], 8 * (NB + 1) + 16)
                act.wait_ge(stored[1], 8 * (NB - 1) + 16)

            @block.vector
            def _(dve):
                dve.wait_ge(c_in, 48)
                nc.vector.tensor_scalar(cols[:, 1, :], cols[:, 1, :], 1.0, None, ALU.add).then_inc(cols_ready, 1)
                dve.wait_ge(cols_ready, 1)

                def rows(b, j):
                    dve.wait_ge(htp_ready, b + 1)
                    if not (isinstance(b, int) and b < 2):
                        dve.wait_ge(gu_ready, b - 1)
                    for k in range(4, KD):
                        ins = nc.vector.tensor_scalar(hT[:, j, k, :], tp[1][:, k - 4, :], cols[:, 1, k:k + 1], cols[:, 0, k:k + 1], ALU.mult, ALU.add)
                    ins.then_inc(hT_dve, 1)

                def output(b, j):
                    dve.wait_ge(acc_ready, b + 2)
                    dve.wait_ge(stored[j], 8 * (b - j) + 16)
                    nc.vector.tensor_copy(y[:, j, 0:CH], acc[0][:, :]).then_inc(y_dve, 1)

                def turned(b):
                    dve.wait_ge(atp_ready, b + 1)
                    dve.wait_ge(acc_ready, b + 1)
                    nc.vector.tensor_copy(aT[:, 0, :, :], at[:, :, :])
                    dve.drain()
                    nc.vector.tensor_tensor(aT[:, 1, :, :], at[:, :, :], aT[:, 0, :, :], ALU.subtract).then_inc(aT_ready, 1)

                def weights_lo(b, j):
                    dve.wait_ge(whi_ready, b + 1)
                    nc.vector.tensor_tensor(wds[:, j, 1, :, :], wd[:, j, :, :], wds[:, j, 0, :, :], ALU.subtract).then_inc(wlo_ready, 1)

                def step(b, j, first, last):
                    if not first:
                        turned(b - 1)
                    dve.wait_ge(sg_ready, b + 1)
                    dve.wait_ge(atp_ready, b)
                    nc.vector.tensor_tensor(a[:, :], sg[:, :], gu[j][:, 1, :], ALU.mult).then_inc(a_ready, 1)
                    if not last:
                        rows(b + 1, 1 - j)
                    weights_lo(b, j)
                    if not first:
                        output(b - 1, 1 - j)

                rows(0, 0)
                step(0, 0, True, False)
                with dve.Fori(0, (NB - 3) // 2) as i:
                    for j in range(2):
                        step(i * 2 + j + 1, (j + 1) % 2, False, False)
                step(NB - 2, 1, False, False)
                step(NB - 1, 0, False, True)
                turned(NB - 1)
                output(NB - 1, 0)


class LaterModulation:

    CW = 6 * D // NT

    def __init__(self, nc, d, ph):
        self.nc, self.d, CW = nc, d, self.CW
        self.c, self.cond, self.ones = ph.sb("m_c", [P, KD]), ph.sb("m_cond", [P, KD]), ph.sb("m_ones", [P, 1])
        self.w, self.b = ph.sb("m_w", [P, 2, KD, CW]), ph.sb("m_b", [1, 6 * D])
        self.part, self.row = ph.sb("m_part", [P, 2, CW]), ph.sb("m_row", [1, 2, CW])
        self.acc = ph.ps("m_acc", [P, CW])
        self.m_in, self.m_cond_ready, self.part_ready, self.row_ready, self.acc_ready, self.m_waited = (
            ph.sem(s) for s in ("m_in", "m_cond_ready", "m_part_ready", "m_row_ready", "m_acc_ready", "m_waited"))
        self.w_in, self.row_st = ([ph.sem(f"m_{n}{j}") for j in range(2)] for n in ("w_in", "row_st"))

    def sync_start(self, sp):
        sp.dma_start(self.c[:, :], self.d["c"].rearrange("b (p k) -> (b p) k", k=KD)).then_inc(self.m_in, 16)
        sp.dma_start(self.b[:, :], self.d["ada_b"][1:2, :]).then_inc(self.m_in, 16)

    def sync_stages(self, sp):
        CW, w_dram = self.CW, self.d["ada_w"][1].rearrange("(p k) n -> p k n", k=KD)

        def load(c, j):
            wait_from(sp, self.part_ready, c - 1)
            settle(sp, self.m_waited)
            sp.dma_start(self.w[:, j, :, :], w_dram[:, :, ds(c * CW, CW)]).then_inc(self.w_in[j], 16)

        def store(c, j):
            sp.wait_ge(self.row_ready, c + 1)
            settle(sp, self.m_waited)
            sp.dma_start(self.d["mod"][1:2, ds(c * CW, CW)], self.row[:, j, :]).then_inc(self.row_st[j], 16)

        return [(load, 2), (store, -1)]

    def sync_end(self, sp):
        for j in range(2):
            sp.wait_ge(self.row_st[j], 16 * NT // 2)

    def scalar_start(self, act):
        act.wait_ge(self.m_in, 32)
        self.nc.scalar.activation(self.cond[:, :], self.c[:, :], ACT.Silu).then_inc(self.m_cond_ready, 1)

    def tensor_stages(self, pe):
        def total(c, j):
            pe.wait_ge(self.part_ready, c + 1)
            wait_from(pe, self.row_ready, c)
            self.nc.tensor.matmul(self.acc[0:1, :], self.ones[:, :], self.part[:, j, :], start=True, stop=True).then_inc(self.acc_ready, 1)

        return [(total, 0)]

    def vector_start(self, dve):
        self.nc.vector.memset(self.ones[:, :], 1.0)
        dve.drain()
        dve.wait_ge(self.m_cond_ready, 1)

    def vector_stages(self, dve):
        v = self.nc.vector

        def partial(c, j):
            dve.wait_ge(self.w_in[j], 8 * (c - j) + 16)
            wait_from(dve, self.acc_ready, c - 1)
            out = self.part[:, j, :]
            v.tensor_scalar(out, self.w[:, j, 0, :], self.cond[:, 0:1], None, ALU.mult)
            for k in range(1, KD):
                dve.drain()
                ins = v.scalar_tensor_tensor(out, self.w[:, j, k, :], self.cond[:, k:k + 1], out, ALU.mult, ALU.add)
            ins.then_inc(self.part_ready, 1)

        def add_bias(c, j):
            dve.wait_ge(self.acc_ready, c + 1)
            wait_from(dve, self.row_st[j], 8 * (c - j))
            v.tensor_tensor(self.row[:, j, :], self.acc[0:1, :], self.b[:, ds(c * self.CW, self.CW)], ALU.add).then_inc(self.row_ready, 1)

        return [(add_bias, -1), (partial, 0)]


class Combine:

    def __init__(self, nc, d, l, ph, lead=0, x2_used=None):
        alone = x2_used is None
        self.nc, self.alone, self.d, self.l, self.lead, self.x2_used = nc, alone, d, l, lead, x2_used
        self.out = d["x2"] if l == 0 else d["out"][0]
        self.norm, self.gain = ph.sb("norm", [P, 2, D]), ph.sb("gain", [P, D])
        self.dest, self.wt = ph.sb("dest", [P, NT, 2], I32), ph.sb("wt", [P, NT, 2])
        self.destb, self.wb = ph.sb("destb", [P, 2, 2], I32), ph.sb("wb", [P, 2, 2])
        self.x1 = ph.sb("x1", [P, 2, D])
        self.y = ph.sb("y", [P, 2, 2, D])
        self.z = ph.sb("z", [P, 2, D]) if alone else self.y[:, :, 0, :]
        self.x2 = ph.sb("x2", [P, 2, D])
        self.stats, self.mv = ph.sb("stats", [P, 2, 6]), ph.sb("mv", [P, 2, 2])
        self.std = ph.sb("std", [P, 2, 3])
        self.nb = ph.sb("nb", [P, 2, 1])
        self.cb_in, self.y0_ready, self.z_ready, self.v_ready, self.std_ready, self.nb_ready, self.xn_ready, self.xg_ready, self.x2_ready = (
            ph.sem(s) for s in ("cb_in", "y0_ready", "z_ready", "v_ready", "std_ready", "nb_ready", "xn_ready", "xg_ready", "x2_ready"))
        self.gained, self.y_used, self.waited = ph.sem("gained"), ph.sem("y_used"), ph.sem("cb_waited")
        self.x1_in, self.stored = ([ph.sem(f"{n}{j}") for j in range(2)] for n in ("x1_in", "stored"))
        self.y_in = d["pool_dma"](f"cb{l}")

    def sync_start(self, sp):
        d = self.d
        sp.dma_start(self.dest[:, :, :].rearrange("p c j -> p (c j)"), d["dest"]).then_inc(self.cb_in, 16)
        sp.dma_start(self.wt[:, :, :].rearrange("p c j -> p (c j)"), d["wt"]).then_inc(self.cb_in, 16)
        load_norm(sp, self.nc, d, self.norm, self.gain, self.l, 1, self.cb_in)

    def sync_stages(self, sp):
        def load(c, j):
            wait_from(sp, self.z_ready, c - 1)
            settle(sp, self.waited)
            sp.dma_start(self.x1[:, j, :], self.d["x1"][ds(c * P, P), :]).then_inc(self.x1_in[j], 16)

        def store(c, j):
            sp.wait_ge(self.x2_ready, c + 1)
            settle(sp, self.waited)
            sp.dma_start(self.out[ds(c * P, P), :], self.x2[:, j, :]).then_inc(self.stored[j], 16)

        return [(load, self.lead + 2), (store, self.lead - 1)]

    def sync_end(self, sp):
        for j in range(2):
            sp.wait_ge(self.stored[j], 16 * NT // 2)

    def pool_stages(self, pool):
        nc = self.nc

        def gather(c, j):
            wait_from(pool, self.y_used if self.alone else self.xg_ready, c - 1)
            nc.gpsimd.tensor_copy(self.destb[:, j, :], self.dest[:, ds(c, 1), :])
            pool.drain()
            for n in range(2):
                nc.gpsimd.indirect_dma_start(out=self.y[:, j, n, :], out_offset=None, in_=self.d["ybuf"],
                                             in_offset=bass.IndirectOffsetOnAxis(ap=self.destb[:, j, n:n + 1], axis=0)).then_inc(self.y_in[j], 16)

        def gamma(c, j):
            pool.wait_ge(self.xn_ready, c + 1)
            wait_from(pool, self.stored[j], 8 * (c - j))
            if self.x2_used:
                wait_from(pool, self.x2_used, c - 1)
            nc.gpsimd.tensor_tensor(self.x2[:, j, :], self.z[:, j, :], self.norm[:, 0, :], ALU.mult).then_inc(self.xg_ready, 1)

        if self.alone:
            return [(gather, self.lead + 2), (gamma, self.lead - 1)]
        return [(gamma, self.lead - 1), (gather, self.lead + 1)]

    def scalar_stages(self, act):
        nc, y, std = self.nc, self.y, self.std

        def first_expert(c, j):
            act.wait_ge(self.y_in[j], 16 * (c - j) + 32)
            nc.scalar.activation(self.wb[:, j, :], self.wt[:, ds(c, 1), :], ACT.Copy)
            act.drain()
            nc.scalar.activation(y[:, j, 0, :], y[:, j, 0, :], ACT.Copy, scale=self.wb[:, j, 0:1]).then_inc(self.y0_ready, 1)

        def root(c, j):
            act.wait_ge(self.v_ready, c + 1)
            nc.scalar.activation(std[:, j, 1:2], std[:, j, 0:1], ACT.Sqrt).then_inc(self.std_ready, 1)

        def normalise(c, j):
            act.wait_ge(self.nb_ready, c + 1)
            nc.scalar.activation(self.z[:, j, :], self.z[:, j, :], ACT.Identity, bias=self.nb[:, j, 0:1], scale=std[:, j, 2:3]).then_inc(self.xn_ready, 1)

        if self.alone:
            return [(root, self.lead), (first_expert, self.lead + 1), (normalise, self.lead)]
        return [(root, self.lead), (normalise, self.lead), (first_expert, self.lead + 1)]

    def vector_start(self, dve):
        dve.wait_ge(self.cb_in, 80)
        self.nc.vector.tensor_scalar(self.gain[:, :], self.gain[:, :], 1.0, None, ALU.add).then_inc(self.gained, 1)
        dve.wait_ge(self.gained, 1)

    def vector_stages(self, dve):
        v, std = self.nc.vector, self.std

        def total(c, j):
            z = self.z[:, j, :]
            dve.wait_ge(self.y0_ready, c + 1)
            if self.alone:
                wait_from(dve, self.xg_ready, c - 1)
            v.scalar_tensor_tensor(z, self.y[:, j, 1, :], self.wb[:, j, 1:2], self.y[:, j, 0, :], ALU.mult, ALU.add).then_inc(self.y_used, 1)
            dve.drain()
            v.tensor_tensor(z, z, self.gain[:, :], ALU.mult)
            dve.drain()
            dve.wait_ge(self.x1_in[j], 8 * (c - j) + 16)
            v.scalar_tensor_tensor(z, self.x1[:, j, :], ALPHA, z, ALU.mult, ALU.add).then_inc(self.z_ready, 1)
            dve.wait_ge(self.z_ready, c + 1)
            for half in range(2):
                v.bn_stats(self.stats[:, half, :], self.z[:, j, half * CH:(half + 1) * CH])
            dve.drain()
            v.bn_aggr(self.mv[:, j, :], self.stats[:, :, :].rearrange("p a b -> p (a b)"))
            dve.drain()
            v.tensor_scalar(std[:, j, 0:1], self.mv[:, j, 1:2], LN_EPS, None, ALU.add).then_inc(self.v_ready, 1)

        def scale(c, j):
            dve.wait_ge(self.std_ready, c + 1)
            v.reciprocal(std[:, j, 2:3], std[:, j, 1:2])
            dve.drain()
            v.tensor_scalar(self.nb[:, j, :], self.mv[:, j, 0:1], std[:, j, 2:3], -1.0, ALU.mult, ALU.mult).then_inc(self.nb_ready, 1)

        def finish(c, j):
            dve.wait_ge(self.xg_ready, c + 1)
            v.tensor_tensor(self.x2[:, j, :], self.x2[:, j, :], self.norm[:, 1, :], ALU.add).then_inc(self.x2_ready, 1)

        sums = [(finish, self.lead - 1), (total, self.lead)]
        return (sums[::-1] if self.alone else sums) + [(scale, self.lead)]


def combine(nc, d, l):
    with Phase(nc, f"cb{l}") as ph:
        cb = Combine(nc, d, l, ph)
        with nc.Block() as block:
            @block.sync
            def _(sp):
                cb.sync_start(sp)
                skewed(sp, cb.sync_stages(sp))
                cb.sync_end(sp)

            @block.gpsimd
            def _(pool):
                pool.wait_ge(cb.cb_in, 80)
                skewed(pool, cb.pool_stages(pool))

            @block.scalar
            def _(act):
                act.wait_ge(cb.cb_in, 80)
                skewed(act, cb.scalar_stages(act))

            @block.vector
            def _(dve):
                cb.vector_start(dve)
                skewed(dve, cb.vector_stages(dve))


def project(nc, d, which):
    first_layer = which == "vo"
    turned_in = which in ("v", "q")
    fused, roped_out, modulated = which == "k", which in ("k", "q"), which in ("vo", "q")
    HH = DH // 2
    NBK = 2 * AH * DV // CH if first_layer else G
    WC = NBK * CH
    with Phase(nc, f"p{which}") as ph:
        ws = ph.sb("ws", [P, 2, KD, WC], F32R)
        WR, WK = 3, 2
        wst = ph.sb("wst", [P, WR, WK, CH])
        ident = ph.sb("ident", [P, P])
        hT = ph.sb("hT", [P, 2, 2, KD, P], F32R)
        tp = [ph.ps(f"tp{i}", [P, 4, P]) for i in range(2)]
        mm = [ph.ps(f"mm{i}", [P, CH]) for i in range(NBK)]
        (c_in, cols_ready, whi_ready, wlo_ready, tp_ready, full_ready, hi_ready, lo_ready, mm_ready, ev, roped_ready, rt_ready, rT_ready, csb_ready, waited) = (
            ph.sem(s) for s in ("c_in", "cols_ready", "whi_ready", "wlo_ready", "tp_ready", "full_ready", "hi_ready", "lo_ready", "mm_ready", "ev",
                                "roped_ready", "rt_ready", "rT_ready", "csb_ready", "waited"))
        x_in, st = ([ph.sem(f"{n}{j}") for j in range(2)] for n in ("x_in", "st"))
        w_in = [ph.sem(f"w_in{j}") for j in range(WR)]
        if modulated:
            cols = ph.sb("cols", [P, 2, KD])
        if modulated or fused:
            full = ph.sb("full", [P, KD, P])
        if roped_out:
            cs = ph.sb("cs", [P, 2, NT, HH])
            csb = ph.sb("csb", [P, 2, HH])
            part = ph.sb("part", [P, 4, G, BH, HH])
            roped = ph.sb("roped", [P, G, BH, 2, HH])
            rT = ph.sb("rT", [P, G, 4, P])
            rt = [ph.ps(f"rt{i}", [P, 4, P]) for i in range(G)]
        else:
            vo = ph.sb("vo", [P, 2, NBK, CH])
        cb = Combine(nc, d, 0, ph, lead=3, x2_used=tp_ready) if fused else None
        lm = LaterModulation(nc, d, ph) if which == "v" else None
        x = cb.x2 if fused else ph.sb("x", [P, 2, D])
        x_dram = d["x"][0] if first_layer else d.get("x2")
        w_dram, col0 = {"vo": (d.get("a_w_in"), 2 * QK), "k": (d.get("b_w_kv"), 0), "v": (d.get("b_w_kv"), QW), "q": (d.get("b_w_q"), 0)}[which]
        w_dram = w_dram if which in ("k", "v") else w_dram[0]
        out_dram = {"vo": "vo", "k": "kT", "v": "v", "q": "qT"}[which]
        full_st = ph.sem("full_st")
        w_rows = w_dram.rearrange("(p k) n -> p k n", k=KD)
        NC_IN = 1 + roped_out + 2 * modulated
        FIRST = KD // WK
        pieces = [(slice(k, k + WK), slice(g * CH, (g + 1) * CH)) for g in range(NBK) for k in range(0, KD, WK)]

        def xT(j):
            return x[:, j, :].rearrange("p (k t) -> p k t", k=KD)

        with nc.Block() as block:
            @block.sync
            def _(sp):
                if fused:
                    cb.sync_start(sp)
                if lm:
                    lm.sync_start(sp)
                sp.dma_start(ident[:, :], d["consts"][:, C_ID:C_ID + P]).then_inc(c_in, 16)
                if roped_out:
                    sp.dma_start(cs[:, :, :, :].rearrange("p a c e -> p (a c e)"), d["cs"]).then_inc(c_in, 16)
                if modulated:
                    load_mod_columns(sp, nc, d, cols, 0 if first_layer else 1, (0, 1), c_in)

                def load(c, j):
                    wait_from(sp, (full_ready if modulated else lo_ready) if turned_in else tp_ready, c - 1)
                    settle(sp, waited)
                    if turned_in:
                        sp.dma_start(xT(j), d["x2T"][:, :, ds(c * P, P)].rearrange("k p t -> p k t")).then_inc(x_in[j], 16)
                    else:
                        sp.dma_start(x[:, j, :], x_dram[ds(c * P, P), :]).then_inc(x_in[j], 16)

                def store(c, j):
                    sp.wait_ge(ev, NBK * c + NBK)
                    settle(sp, waited)
                    sp.dma_start(d[out_dram][ds(c * P, P), :], vo[:, j, :, :].rearrange("p g n -> p (g n)")).then_inc(st[j], 16)

                def store_rows(c, j):
                    sp.wait_ge(full_ready, c + 1)
                    settle(sp, waited)
                    sp.dma_start(d["x2T" if fused else "hT"][:, :, ds(c * P, P)].rearrange("k p t -> p k t"), full[:, :, :]).then_inc(full_st, 16)

                def store_roped(c, j):
                    sp.wait_ge(rT_ready, G * c + G)
                    settle(sp, waited)
                    sp.dma_start(d[out_dram][:, :, ds(c * P, P)].rearrange("g p t -> p g t"),
                                 rT[:, :, :, :].rearrange("p g h t -> p (g h) t")).then_inc(st[0], 16)

                def weights():
                    for n, (rows, cut) in enumerate(pieces):
                        if n >= WR:
                            sp.wait_ge(wlo_ready, n - WR + 1)
                        sp.dma_start(wst[:, n % WR, :, :], w_rows[:, rows, col0 + cut.start:col0 + cut.stop]).then_inc(w_in[n % WR], 16)

                if fused:
                    for c in range(2):
                        cb_load, cb_lead = cb.sync_stages(sp)[0]
                        cb_load(c, c)
                    weights()
                    stages = [(lambda c, j: None if isinstance(c, int) and c < 2 else cb_load(c, j), cb_lead), cb.sync_stages(sp)[1]]
                else:
                    for c in range(2):
                        load(c, c)
                    weights()
                    stages = [(lambda c, j: None if isinstance(c, int) and c < 2 else load(c, j), 3)]
                if lm:
                    stages += lm.sync_stages(sp)
                skewed(sp, stages + ([(store_rows, 1)] if first_layer or fused else []) + [(store_roped, -1) if roped_out else (store, 0)])
                if fused:
                    cb.sync_end(sp)
                if lm:
                    lm.sync_end(sp)
                if first_layer or fused:
                    sp.wait_ge(full_st, 16 * NT)
                for j in range(1 if roped_out else 2):
                    sp.wait_ge(st[j], 16 * NT if roped_out else 16 * NT // 2)

            @block.tensor
            def _(pe):
                pe.wait_ge(c_in, 16 * NC_IN)

                def transposes(c, j):
                    if fused:
                        pe.wait_ge(cb.x2_ready, c + 1)
                    else:
                        pe.wait_ge(x_in[j], 8 * (c - j) + 16)
                    wait_from(pe, full_ready, c)
                    for k in range(KD):
                        ins = nc.tensor.transpose(tp[k // 4][:, k % 4, :], x[:, j, k:D:KD], ident[:, :])
                    ins.then_inc(tp_ready, 1)

                def bank(c, j, g):
                    if g == 0:
                        pe.wait_ge(lo_ready, c + 1)
                        pe.wait_ge(hi_ready, c + 1)
                    wait_from(pe, ev, NBK * (c - 1) + g + 1)
                    for k in range(KD):
                        if isinstance(c, int) and c == 0 and k % WK == 0:
                            pe.wait_ge(wlo_ready, (g * KD + k) // WK + 1)
                        for n, (a, b) in enumerate(((0, 0), (0, 1), (1, 0))):
                            ins = nc.tensor.matmul(mm[g][:, :], hT[:, j, a, k, :], ws[:, b, k, g * CH:(g + 1) * CH],
                                                   start=(k == 0 and n == 0), stop=(k == KD - 1 and n == 2))
                    ins.then_inc(mm_ready, 1)

                def roped_transposes(c, j):
                    pe.wait_ge(roped_ready, c + 1)
                    wait_from(pe, rT_ready, G * c)
                    for g in range(G):
                        for h in range(4):
                            ins = nc.tensor.transpose(rt[g][:, h, :], roped[:, g, 2 * h:2 * h + 2, :, :].rearrange("p a b e -> p (a b e)"), ident[:, :])
                        ins.then_inc(rt_ready, 1)

                skewed(pe, [(lambda c, j: bank(c, j, 0), 0)] + ([] if turned_in else [(transposes, 1)]) + [(lambda c, j: bank(c, j, 1), 0)]
                       + ([(roped_transposes, -1)] if roped_out else []) + [(lambda c, j: bank(c, j, 2), 0)]
                       + ([(lambda c, j: bank(c, j, 3), 0)] if NBK == 4 else []) + (lm.tensor_stages(pe) if lm else []))

            @block.scalar
            def _(act):
                def weights_hi(some):
                    for n in some:
                        rows, cut = pieces[n]
                        act.wait_ge(w_in[n % WR], 16 * (n // WR + 1))
                        nc.scalar.activation(ws[:, 0, rows, cut], wst[:, n % WR, :, :], ACT.Copy).then_inc(whi_ready, 1)

                def transposed(c, j):
                    if turned_in:
                        act.wait_ge(x_in[j], 8 * (c - j) + 16)
                    else:
                        act.wait_ge(tp_ready, c + 1)
                    if modulated:
                        wait_from(act, lo_ready, c)
                        if first_layer:
                            wait_from(act, full_st, 16 * c)
                        for k in range(KD):
                            ins = nc.scalar.activation(full[:, k, :], xT(j)[:, k, :] if turned_in else tp[k // 4][:, k % 4, :], ACT.Identity, bias=cols[:, 0, k:k + 1], scale=cols[:, 1, k:k + 1])
                        ins.then_inc(full_ready, 1)
                    else:
                        wait_from(act, mm_ready, NBK * (c - 1))
                        for i in range(2):
                            four = slice(i * 4, (i + 1) * 4)
                            ins = nc.scalar.activation(hT[:, j, 0, four, :], xT(j)[:, four, :] if turned_in else tp[i][:, :, :], ACT.Copy)
                        ins.then_inc(hi_ready, 1)

                def whole_rows(c, j):
                    act.wait_ge(lo_ready, c + 1)
                    wait_from(act, full_st, 16 * c)
                    for i in range(2):
                        ins = nc.scalar.activation(full[:, i * 4:(i + 1) * 4, :], tp[i][:, :, :], ACT.Copy)
                    ins.then_inc(full_ready, 1)

                def turned(c, j):
                    wait_from(act, st[0], 16 * c)
                    for g in range(G):
                        act.wait_ge(rt_ready, G * c + g + 1)
                        nc.scalar.activation(rT[:, g, :, :], rt[g][:, :, :], ACT.Copy).then_inc(rT_ready, 1)

                def values(c, j):
                    wait_from(act, st[j], 8 * (c - j))
                    for g in range(NBK):
                        act.wait_ge(mm_ready, NBK * c + g + 1)
                        gate = first_layer and g >= NBK // 2
                        nc.scalar.activation(vo[:, j, g, :], mm[g][:, :], ACT.Sigmoid if gate else ACT.Copy).then_inc(ev, 1)

                if modulated:
                    act.wait_ge(cols_ready, 1)
                if fused:
                    act.wait_ge(cb.cb_in, 80)
                if lm:
                    lm.scalar_start(act)
                weights_hi(range(FIRST))

                def rest_of_weights(c, j):
                    if isinstance(c, int) and c == 0:
                        weights_hi(range(FIRST, len(pieces)))

                skewed(act, [(transposed, 1)] + ([(whole_rows, 1)] if fused else []) + [(rest_of_weights, 1)] + (cb.scalar_stages(act) if fused else []) + [(turned, -1) if roped_out else (values, 0)])

            @block.vector
            def _(dve):
                v = nc.vector
                if modulated:
                    dve.wait_ge(c_in, 16 * NC_IN)
                    v.tensor_scalar(cols[:, 1, :], cols[:, 1, :], 1.0, None, ALU.add)
                    dve.drain().then_inc(cols_ready, 1)
                if fused:
                    cb.vector_start(dve)
                if roped_out:
                    dve.wait_ge(c_in, 16 * NC_IN)
                def weights_lo(some):
                    for n in some:
                        rows, cut = pieces[n]
                        dve.wait_ge(whi_ready, n + 1)
                        v.tensor_tensor(ws[:, 1, rows, cut], wst[:, n % WR, :, :], ws[:, 0, rows, cut], ALU.subtract).then_inc(wlo_ready, 1)

                if lm:
                    lm.vector_start(dve)
                weights_lo(range(FIRST))

                def rest_of_weights(c, j):
                    if isinstance(c, int) and c == 0:
                        weights_lo(range(FIRST, len(pieces)))

                def split(c, j):
                    if modulated:
                        dve.wait_ge(full_ready, c + 1)
                        wait_from(dve, mm_ready, NBK * (c - 1))
                        v.tensor_copy(hT[:, j, 0, :, :], full[:, :, :]).then_inc(hi_ready, 1)
                    else:
                        dve.wait_ge(hi_ready, c + 1)
                        for i in range(2):
                            four = slice(i * 4, (i + 1) * 4)
                            ins = v.tensor_tensor(hT[:, j, 1, four, :], xT(j)[:, four, :] if turned_in else tp[i][:, :, :], hT[:, j, 0, four, :], ALU.subtract)
                        ins.then_inc(lo_ready, 1)

                def rotate(c, j, g):
                    if g == 0:
                        wait_from(dve, roped_ready, c)
                        v.tensor_copy(csb[:, :, :], cs[:, :, ds(c, 1), :]).then_inc(csb_ready, 1)
                        dve.wait_ge(csb_ready, c + 1)
                    sin, cos = (csb[:, a, :].rearrange("p (o e) -> p o e", o=1).to_broadcast([P, BH, HH]) for a in range(2))
                    dve.wait_ge(mm_ready, G * c + g + 1)
                    m = mm[g][:, :].rearrange("p (h a e) -> p h a e", h=BH, a=2)
                    v.tensor_tensor(part[:, 0, g, :, :], m[:, :, 0, :], cos, ALU.mult)
                    v.tensor_tensor(part[:, 1, g, :, :], m[:, :, 1, :], sin, ALU.mult)
                    v.tensor_tensor(part[:, 2, g, :, :], m[:, :, 1, :], cos, ALU.mult)
                    v.tensor_tensor(part[:, 3, g, :, :], m[:, :, 0, :], sin, ALU.mult).then_inc(ev, 1)

                combining = cb.vector_stages(dve) if fused else []
                stages = combining[:1] + [(split, 1), (rest_of_weights, 1)]
                if roped_out:
                    stages += [(lambda c, j: rotate(c, j, 0), 0)] + combining[1:2] + [(lambda c, j: rotate(c, j, 1), 0)] + combining[2:] + [(lambda c, j: rotate(c, j, 2), 0)]
                skewed(dve, stages + (lm.vector_stages(dve) if lm else []))

            @block.gpsimd
            def _(pool):
                def lo(c, j):
                    pool.wait_ge(hi_ready, c + 1)
                    nc.gpsimd.tensor_tensor(hT[:, j, 1, :, :], full[:, :, :], hT[:, j, 0, :, :], ALU.subtract).then_inc(lo_ready, 1)

                def rope_sums(c, j):
                    pool.wait_ge(ev, G * c + G)
                    wait_from(pool, rt_ready, G * c)
                    r = roped[:, :, :, :, :].rearrange("p g h a e -> p (g h) a e")
                    q = part[:, :, :, :, :].rearrange("p q g h e -> p q (g h) e")
                    nc.gpsimd.tensor_tensor(r[:, :, 0, :], q[:, 0], q[:, 1], ALU.subtract)
                    nc.gpsimd.tensor_tensor(r[:, :, 1, :], q[:, 2], q[:, 3], ALU.add)
                    pool.drain().then_inc(roped_ready, 1)

                if fused:
                    pool.wait_ge(cb.cb_in, 80)
                stages = (cb.pool_stages(pool) if fused else []) + ([(lo, 1)] if modulated else []) + ([(rope_sums, 0)] if roped_out else [])
                if stages:
                    skewed(pool, stages)


def attention(nc, d):
    NBLK = S // P
    UN = 2 * NBLK
    BODY = 2 * UN
    RS, RT, RB, GRP = 4, 2, 4, 8
    with Phase(nc, "at") as ph:
        ident = ph.sb("ident", [P, P])
        band = ph.sb("band", [P, 2 * P])
        q = ph.sb("q", [P, 2, S])
        k = ph.sb("k", [P, 2, S])
        v = ph.sb("v", [P, 2, NBLK, P])
        o = ph.sb("o", [P, 2, NBLK, 2, DH + 2])
        pr = ph.sb("pr", [P, RB, 2 * P])
        pT = ph.sb("pT", [P, RB, 2 * P])
        bs = [ph.ps(f"bs{i}", [P, 2 * P]) for i in range(RS)]
        bt = [ph.ps(f"bt{i}", [P, 2 * P]) for i in range(RT)]
        bo = [ph.ps(f"bo{i}", [P, GRP // 2, 2, DH]) for i in range(2)]
        (c_in, s_ready, m_ready, p_ready, t_ready, pT_act, pT_dve, pv_ready, o_ready, waited) = (
            ph.sem(s) for s in ("c_in", "s_ready", "m_ready", "p_ready", "t_ready", "pT_act", "pT_dve", "pv_ready", "o_ready", "waited"))
        in_sem, stored, used = ([ph.sem(f"{n}{j}") for j in range(2)] for n in ("in", "stored", "used"))

        def unit(g, u):
            par, j, hh = u // UN, (u % UN) // 2, u % 2
            dil = DILATIONS[g]
            nb = NBLK // dil
            return par, j, hh, j % nb > 0, (j % nb) * P * dil + j // nb, dil

        PIECES = [1 if dil == 1 or dil * P == S else dil for dil in DILATIONS]

        def by_block(a, g):
            dil = DILATIONS[g]
            if dil == 1:
                return [a.rearrange("(j i) c -> i j c", i=P)]
            if dil * P == S:
                return [a.rearrange("(i r) c -> i r c", i=P)]
            pieces = a.rearrange("(n i r) c -> r i n c", i=P, r=dil)
            return [pieces[r] for r in range(dil)]

        def split(a, g):
            n = NBLK // PIECES[g]
            return [a[:, r * n:(r + 1) * n] for r in range(PIECES[g])]

        def loads(g, i):
            return sum((2 + PIECES[h]) * (HP // 2) for h in range(g)) + (2 + PIECES[g]) * (i + 1)

        def stores(g, i):
            return sum(PIECES[h] * (HP // 2) for h in range(g)) + PIECES[g] * i

        def on_act(u):
            return u % 2 == 0

        def evacuated(eng, b, u):
            eng.wait_ge(pT_act if on_act(u) else pT_dve, (BODY // 2) * b + u // 2 + 1)

        def copy_out(u, g, copy):
            n = 2 * P if unit(g, u)[3] else P
            return copy(pT[:, u % RB, 0:n], bt[u % RT][:, 0:n])

        def bodies(eng, body):
            for g in range(G):
                with eng.Fori(0, HP // 2) as i:
                    body(g, i, g * (HP // 2) + i)

        with nc.Block() as block:
            @block.sync
            def _(sp):
                for par in range(2):
                    sp.sem_inc(stored[par], 16)
                sp.dma_start(ident[:, :], d["consts"][:, C_ID:C_ID + P]).then_inc(c_in, 16)
                sp.dma_start(band[:, :], d["consts"][:, C_BAND:C_BAND + 2 * P]).then_inc(c_in, 16)

                def body(g, i, b):
                    for par in range(2):
                        hp = i * 2 + par
                        sp.wait_ge(used[par], b + 1)
                        settle(sp, waited)
                        sp.dma_start(q[:, par, :], d["qT"][ds(g * HP + hp, 1), :, :].rearrange("o p t -> p (o t)")).then_inc(in_sem[par], 16)
                        sp.dma_start(k[:, par, :], d["kT"][ds(g * HP + hp, 1), :, :].rearrange("o p t -> p (o t)")).then_inc(in_sem[par], 16)
                        for dst, src in zip(split(v[:, par, :, :], g), by_block(d["v"][:, ds(g * BW + hp * P, P)], g)):
                            sp.dma_start(dst, src).then_inc(in_sem[par], 16)

                bodies(sp, body)

            @block.tensor
            def _(pe):
                pe.wait_ge(c_in, 32)
                pe.sem_inc(used[0], 1)
                pe.sem_inc(used[1], 1)

                def body(g, i, b):
                    def scores(u):
                        par, j, hh, prev, t0, dil = unit(g, u)
                        if u % UN == 0:
                            pe.wait_ge(in_sem[par], 16 * loads(g, i))
                        if u >= RS:
                            pe.wait_ge(m_ready, BODY * b + u - RS + 1)
                        rows = slice(hh * DH, (hh + 1) * DH)
                        first = t0 - P * dil if prev else t0
                        n = 2 * P if prev else P
                        nc.tensor.matmul(bs[u % RS][:, 0:n], q[rows, par, t0:t0 + (P - 1) * dil + 1:dil], k[rows, par, first:first + (n - 1) * dil + 1:dil],
                                         start=True, stop=True).then_inc(s_ready, 1)

                    def turn(u):
                        prev = unit(g, u)[3]
                        pe.wait_ge(p_ready, BODY * b + u + 1)
                        if u >= RT:
                            evacuated(pe, b, u - RT)
                        for h in range(2 if prev else 1):
                            ins = nc.tensor.transpose(bt[u % RT][:, h * P:(h + 1) * P], pr[:, u % RB, h * P:(h + 1) * P], ident[:, :])
                        ins.then_inc(t_ready, 1)

                    def weigh(u):
                        par, j, hh, prev, t0, dil = unit(g, u)
                        evacuated(pe, b, u)
                        if u % GRP == 0:
                            pe.wait_ge(o_ready, (BODY // GRP) * b + u // GRP + 1)
                        out = bo[(u // GRP) % 2][:, (u % GRP) // 2, hh, :]
                        cols = slice(hh * DH, (hh + 1) * DH)
                        if prev:
                            nc.tensor.matmul(out, pT[:, u % RB, 0:P], v[:, par, j - 1, cols], start=True, stop=False)
                        ins = nc.tensor.matmul(out, pT[:, u % RB, P:2 * P] if prev else pT[:, u % RB, 0:P], v[:, par, j, cols], start=not prev, stop=True)
                        ins.then_inc(pv_ready, 1)
                        if u % UN == UN - 1:
                            pe.wait_ge(pv_ready, BODY * b + u + 1)
                            pe.sem_inc(used[par], 1)

                    scores(0)
                    scores(1)
                    for u in range(BODY):
                        if u + 2 < BODY:
                            scores(u + 2)
                        turn(u)
                        if u:
                            weigh(u - 1)
                    weigh(BODY - 1)

                bodies(pe, body)

            @block.scalar
            def _(act):
                act.sem_inc(o_ready, 2)

                def body(g, i, b):
                    def exp(u):
                        par, j, hh, prev, t0, dil = unit(g, u)
                        n = 2 * P if prev else P
                        act.wait_ge(m_ready, BODY * b + u + 1)
                        nc.scalar.activation(pr[:, u % RB, 0:n], pr[:, u % RB, 0:n], ACT.Exp, scale=-1.0, bias=o[:, par, j, hh, DH:DH + 1],
                                             accum_out=o[:, par, j, hh, DH + 1:DH + 2]).then_inc(p_ready, 1)

                    def output(u):
                        par, j = u // UN, (u % UN) // 2
                        act.wait_ge(pv_ready, BODY * b + u + 1)
                        nc.scalar.activation(o[:, par, j + 1 - GRP // 2:j + 1, :, 0:DH], bo[(u // GRP) % 2][:, :, :, :], ACT.Copy).then_inc(o_ready, 1)
                        if u % UN == UN - 1:
                            act.wait_ge(o_ready, (BODY // GRP) * b + u // GRP + 3)
                            act.wait_ge(p_ready, BODY * b + u + 1)
                            settle(act, waited)
                            src = o[:, par, :, :, :].rearrange("p j h e -> p j (h e)")
                            for s_, t_ in zip(split(src, g), by_block(d["o"][g][:, ds((i * 2 + par) * OW, OW)], g)):
                                act.dma_start(t_, s_).then_inc(stored[par], 16)

                    exp(0)
                    for u in range(BODY):
                        if u + 1 < BODY:
                            exp(u + 1)
                        if on_act(u):
                            act.wait_ge(t_ready, BODY * b + u + 1)
                            if u >= RB:
                                act.wait_ge(pv_ready, BODY * b + u - RB + 1)
                            copy_out(u, g, lambda dst, src: nc.scalar.activation(dst, src, ACT.Copy)).then_inc(pT_act, 1)
                        if u % GRP == 1 and u > 1:
                            output(u - 2)
                    output(BODY - 1)

                bodies(act, body)
                for par in range(2):
                    act.wait_ge(stored[par], 16 * sum(PIECES[g] * (HP // 2) for g in range(G)) + 16)

            @block.vector
            def _(dve):
                dve.wait_ge(c_in, 32)

                def body(g, i, b):
                    def mask(u):
                        par, j, hh, prev, t0, dil = unit(g, u)
                        n = 2 * P if prev else P
                        if u % UN == 0:
                            dve.wait_ge(stored[par], 16 * stores(g, i) + 16)
                        dve.wait_ge(s_ready, BODY * b + u + 1)
                        if u >= RB:
                            dve.wait_ge(t_ready, BODY * b + u - RB + 1)
                        settle(dve, waited)
                        nc.vector.tensor_tensor_reduce(out=pr[:, u % RB, 0:n], in0=bs[u % RS][:, 0:n], in1=band[:, 2 * P - n:2 * P], scale=-DH ** -0.5,
                                                       scalar=3e38, op0=ALU.add, op1=ALU.min, accum_out=o[:, par, j, hh, DH:DH + 1]).then_inc(m_ready, 1)

                    mask(0)
                    mask(1)
                    for u in range(BODY):
                        if u + 2 < BODY:
                            mask(u + 2)
                        if not on_act(u):
                            dve.wait_ge(t_ready, BODY * b + u + 1)
                            if u >= RB:
                                dve.wait_ge(pv_ready, BODY * b + u - RB + 1)
                            copy_out(u, g, nc.vector.tensor_copy).then_inc(pT_dve, 1)

                bodies(dve, body)


def trunk(nc, d):
    pool_dma = {n: [nc.semaphore(f"{n}_pool_dma{j}").__enter__() for j in range(2)] for n in ("ex0", "ex1", "cb0", "cb1")}
    d["pool_dma"] = pool_dma.__getitem__
    modulation(nc, d)
    project(nc, d, "vo")
    project_qk(nc, d)
    gate_rows(nc, d)
    mlstm(nc, d)
    for l in range(DEPTH):
        if l == 1:
            project(nc, d, "k")
            project(nc, d, "v")
            project(nc, d, "q")
            attention(nc, d)
        after_mixer(nc, d, l)
        route(nc, d, l)
        experts(nc, d, l)
    combine(nc, d, DEPTH - 1)


SCRATCH = {
    "mod": ((DEPTH, 6 * D), F32),
    "hT": ((KD, P, S), F32),
    "x2T": ((KD, P, S), F32),
    "qkT": ((2 * AH, DQK, S), F32), "vo": ((S, 2 * AH * DV), F32), "gates": ((2, AH, S), F32),
    "rowbm": ((AH, S), F32), "colq": ((P, NT * NQT * AH), F32), "decay": ((P, 2 * AH * NT), F32),
    "y": ((S, D), F32), "x1": ((S, D), F32), "x2": ((S, D), F32), "lg": ((S, NR), F32),
    "slots": ((P, NBP), I32), "dest": ((P, 2 * NT), I32), "wt": ((P, 2 * NT), F32), "block_e": ((1, NBP), I32),
    "ybuf": ((NB * P, D), F32),
    "kT": ((G * HP, P, S), F32), "qT": ((G * HP, P, S), F32), "cs": ((P, NT * DH), F32), "v": ((S, QW), F32), "o": ((G, S, HP * OW), F32),
}


_INS = ["x", "c", "positions", "ada_w", "ada_b", "ln_g", "ln_b", "a_w_in", "a_b_gate", "a_norm_g", "a_w_out", "b_w_kv", "b_w_q", "b_w_o",
        "moe_w_r1", "moe_b_r1", "moe_w_r2", "moe_b_r2", "moe_w_gate", "moe_w_up", "moe_w_down"]


def kernel(**inputs):
    import numpy as _np
    import concourse.bacc as _bacc
    from concourse import mybir as _mybir
    from concourse.bass_utils import run_bass_kernel_spmd as _run

    nc = _bacc.Bacc("TRN2", target_bir_lowering=False, num_devices=1)
    arrays, d = {}, {}
    for name in _INS + ["consts"]:
        a = constant_table() if name == "consts" else _np.ascontiguousarray(inputs[name])
        arrays[f"in_{name}_dram"] = a
        d[name] = nc.dram_tensor(f"in_{name}_dram", a.shape, _mybir.dt.from_np(a.dtype), kind="ExternalInput").ap()
    d["out"] = nc.dram_tensor("out_0_dram", (1, S, D), F32, kind="ExternalOutput").ap()
    for name, (shape, dtype) in SCRATCH.items():
        d[name] = nc.dram_tensor(f"{name}_scratch", shape, dtype, kind="Internal").ap()
    trunk(nc, d)
    r = _run(nc, [arrays], core_ids=[0])
    return r.results[0]["out_0_dram"]
```
